# Optimizing a Trainium2 kernel written in Bass

```python
import jax, jax.numpy as jnp
from jax import lax
import numpy as np

D_MODEL = 1024
BATCH = 1
SEQ = 512
DEPTH = 1
DEC_BATCH = 1
DEC_SEQ = 64
PAST_LEN = 256

CHUNK = 64
HG_HEADS = 4
HG_DK = 128
HG_DV = 128
HG_WIDTH = HG_HEADS * HG_DK
ATT_HEADS = 8
ATT_DIM = 64
ATT_WIDTH = ATT_HEADS * ATT_DIM
IDX_HEADS = 4
IDX_DIM = 64
TOPK_MAX = 256
QBLOCK = CHUNK
ATT_SCALE = ATT_DIM ** -0.5
IDX_SCALE = IDX_DIM ** -0.5
IDX_W_SCALE = IDX_HEADS ** -0.5
N_GROUPS = 4
EXPERTS_PER_GROUP = 4
D_EXPERT = 256
TOP_K_WITHIN = 2
DN_ALPHA = (2 * DEPTH) ** 0.25
DN_BETA = (8 * DEPTH) ** -0.25
LN_EPS = 1e-5
RMS_EPS = 1e-6
IN_SIZES = (HG_WIDTH, HG_WIDTH, HG_HEADS * HG_DV, HG_HEADS * HG_DV,
            ATT_WIDTH, ATT_WIDTH, ATT_WIDTH, IDX_HEADS * IDX_DIM, IDX_DIM, IDX_HEADS,
            D_MODEL, D_MODEL)
IN_COLS = sum(IN_SIZES)

kernel_name = "hgrn2_dsa_hiermoe_streaming_step"

F32 = jnp.float32

def split_in(h):
    parts, off = [], 0
    for s in IN_SIZES:
        parts.append(h[..., off:off + s])
        off += s
    return parts

def layer_norm(x, g, b):
    xf = x.astype(F32)
    mu = jnp.mean(xf, -1, keepdims=True)
    var = jnp.mean(jnp.square(xf - mu), -1, keepdims=True)
    y = (xf - mu) * lax.rsqrt(var + LN_EPS) * g.astype(F32) + b.astype(F32)
    return y.astype(x.dtype)

def hgrn_lower_bounds(lb_logits):
    p = jax.nn.softmax(lb_logits.astype(F32), axis=0)
    return jnp.concatenate([jnp.zeros_like(p[:1]), jnp.cumsum(p[1:], axis=0)], axis=0)

def hgrn2_chunk(S0, q, logf, k, v):
    T = q.shape[1]
    Bc = jnp.cumsum(logf, axis=1)
    tpos = jnp.arange(T)
    causal = (tpos[:, None] >= tpos[None, :])[None, :, :, None, None]
    diff = Bc[:, :, None] - Bc[:, None, :]
    decay = jnp.exp(jnp.where(causal, diff, -jnp.inf))
    A = jnp.einsum('btshk,bshk->bhts', q[:, :, None] * decay, k)
    o = jnp.einsum('bhts,bshv->bthv', A, v) + jnp.einsum('bthk,bhkv->bthv', q * jnp.exp(Bc), S0)
    BT = Bc[:, -1]
    S = jnp.exp(BT)[..., None] * S0 + jnp.einsum('bshk,bshv->bhkv', k * jnp.exp(BT[:, None] - Bc), v)
    return o, S

def hgrn2_scan(S0, q, logf, k, v):
    B, T = q.shape[:2]
    n = T // CHUNK
    to_chunks = lambda a: jnp.moveaxis(a.reshape(B, n, CHUNK, *a.shape[2:]), 1, 0)

    def step(S, xs):
        o, S = hgrn2_chunk(S, *xs)
        return S, o

    S, o = lax.scan(step, S0, (to_chunks(q), to_chunks(logf), to_chunks(k), to_chunks(v)))
    o = jnp.moveaxis(o, 0, 1).reshape(B, T, HG_HEADS, HG_DV)
    return o, S

def dsa_attend(q, qi, wi, q_pos, k, v, ki, k_pos, topk):
    s_idx = jnp.einsum('bthd,bsd->bths', qi.astype(F32), ki.astype(F32)) * IDX_SCALE
    score = jnp.einsum('bth,bths->bts', wi.astype(F32) * IDX_W_SCALE, jax.nn.relu(s_idx))
    admissible = (k_pos[None, :] // CHUNK) <= (q_pos[:, None] // CHUNK)
    score = jnp.where(admissible[None], score, -jnp.inf)
    top_val, top_idx = lax.top_k(score, topk)
    valid = top_val > -jnp.inf
    gather = jax.vmap(lambda rows, idx: rows[idx])
    k_sel = gather(k, top_idx).astype(F32)
    v_sel = gather(v, top_idx).astype(F32)
    logits = jnp.einsum('bthd,btjhd->bthj', q.astype(F32), k_sel) * ATT_SCALE
    logits = jnp.where(valid[:, :, None, :], logits, -jnp.inf)
    p = jax.nn.softmax(logits, axis=-1)
    return jnp.einsum('bthj,btjhd->bthd', p, v_sel).astype(q.dtype)

def dsa_prompt(q, qi, wi, k, v, ki):
    B, T = q.shape[:2]
    topk = min(TOPK_MAX, T // 4)
    pos = jnp.arange(T)
    nb = T // QBLOCK
    blk = lambda a: jnp.moveaxis(a.reshape(B, nb, QBLOCK, *a.shape[2:]), 1, 0)

    def one(args):
        qb, qib, wib, pb = args
        return dsa_attend(qb, qib, wib, pb, k, v, ki, pos, topk)

    out = lax.map(one, (blk(q), blk(qi), blk(wi), pos.reshape(nb, QBLOCK)))
    return jnp.moveaxis(out, 0, 1).reshape(B, T, ATT_HEADS, ATT_DIM)

def token_mixer(x, w_in, lb, hg_norm_w, w_br_hg, w_br_att, w_out, hg_state, past_k, past_v, past_ki):
    B, T, _ = x.shape
    (hq, hf, hi, hg, aq, ak, av, iq, ik, iw, g_hg, g_att) = split_in(jnp.einsum('btd,dc->btc', x, w_in))
    z = hf.astype(F32)
    logf = jnp.logaddexp(jnp.log(lb), jnp.log1p(-lb) + jax.nn.log_sigmoid(z))
    kk = (1.0 - lb) * jax.nn.sigmoid(-z)
    q_h = jax.nn.silu(hq.astype(F32)).reshape(B, T, HG_HEADS, HG_DK)
    f_h = logf.reshape(B, T, HG_HEADS, HG_DK)
    k_h = kk.reshape(B, T, HG_HEADS, HG_DK)
    v_h = hi.astype(F32).reshape(B, T, HG_HEADS, HG_DV)
    if hg_state is None:
        S0 = jnp.zeros((B, HG_HEADS, HG_DK, HG_DV), F32)
        o_hg, S = hgrn2_scan(S0, q_h, f_h, k_h, v_h)
    else:
        o_hg, S = hgrn2_chunk(hg_state.astype(F32), q_h, f_h, k_h, v_h)
    o_hg = o_hg * lax.rsqrt(jnp.mean(o_hg * o_hg, -1, keepdims=True) + RMS_EPS) * hg_norm_w.astype(F32)
    y_hg = (o_hg.reshape(B, T, HG_HEADS * HG_DV) * jax.nn.silu(hg.astype(F32))).astype(x.dtype)
    q_a = aq.reshape(B, T, ATT_HEADS, ATT_DIM)
    k_a = ak.reshape(B, T, ATT_HEADS, ATT_DIM)
    v_a = av.reshape(B, T, ATT_HEADS, ATT_DIM)
    qi = iq.reshape(B, T, IDX_HEADS, IDX_DIM)
    if past_k is None:
        o_att = dsa_prompt(q_a, qi, iw, k_a, v_a, ik)
    else:
        P = past_k.shape[1]
        k_all = jnp.concatenate([past_k.astype(k_a.dtype), k_a], axis=1)
        v_all = jnp.concatenate([past_v.astype(v_a.dtype), v_a], axis=1)
        ki_all = jnp.concatenate([past_ki.astype(ik.dtype), ik], axis=1)
        L = P + T
        o_att = dsa_attend(q_a, qi, iw, P + jnp.arange(T), k_all, v_all, ki_all, jnp.arange(L),
                           min(TOPK_MAX, L // 4))
    br_hg = jnp.einsum('btc,cd->btd', y_hg, w_br_hg)
    br_att = jnp.einsum('btc,cd->btd', o_att.reshape(B, T, ATT_WIDTH), w_br_att)
    merged = jax.nn.sigmoid(g_hg) * br_hg + jax.nn.sigmoid(g_att) * br_att
    out = jnp.einsum('btd,de->bte', merged, w_out)
    return out, k_a, v_a, ik, S.astype(x.dtype)

def hier_moe(x, w_rg, b_rg, w_re, b_re, w_gate, w_up, w_down):
    B, T, D = x.shape
    xt = x.reshape(B * T, D)
    g_logits = (xt @ w_rg + b_rg).astype(F32)
    g_prob = jax.nn.softmax(g_logits, -1)
    g_sel = jnp.argmax(g_logits, -1)
    g_w = jnp.take_along_axis(g_prob, g_sel[:, None], axis=1)
    e_logits = (xt @ w_re + b_re).astype(F32).reshape(-1, N_GROUPS, EXPERTS_PER_GROUP)
    e_logits = jnp.take_along_axis(e_logits, g_sel[:, None, None], axis=1)[:, 0]
    e_prob = jax.nn.softmax(e_logits, -1)
    top_p, top_i = lax.top_k(e_prob, TOP_K_WITHIN)
    top_p = top_p / jnp.sum(top_p, -1, keepdims=True)
    e_w = jnp.einsum('nj,nje->ne', top_p, jax.nn.one_hot(top_i, EXPERTS_PER_GROUP, dtype=F32))
    combine = jax.nn.one_hot(g_sel, N_GROUPS, dtype=F32)[:, :, None] * (g_w * e_w)[:, None, :]
    y = jnp.zeros((B * T, D), F32)
    for g in range(N_GROUPS):
        h = jax.nn.silu(jnp.einsum('nd,edf->nef', xt, w_gate[g])) * jnp.einsum('nd,edf->nef', xt, w_up[g])
        y = y + jnp.einsum('nef,efd->nd', h * combine[:, g, :, None].astype(h.dtype), w_down[g]).astype(F32)
    return y.astype(x.dtype).reshape(B, T, D)

def setup_inputs(seed: int = 0) -> dict:
    key = jax.random.key(seed)
    ks = jax.random.split(key, 28)
    nrm = lambda k, shape, s: jax.random.normal(k, shape, jnp.float32) * s
    G, E, F = N_GROUPS, EXPERTS_PER_GROUP, D_EXPERT
    return {
        "x_prompt": nrm(ks[0], (BATCH, SEQ, D_MODEL), 1.0),
        "x_sample": nrm(ks[1], (DEC_BATCH, DEC_SEQ, D_MODEL), 1.0),
        "cache_k": nrm(ks[2], (DEPTH, DEC_BATCH, PAST_LEN, ATT_HEADS, ATT_DIM), 1.0),
        "cache_v": nrm(ks[3], (DEPTH, DEC_BATCH, PAST_LEN, ATT_HEADS, ATT_DIM), 1.0),
        "cache_idx_k": nrm(ks[4], (DEPTH, DEC_BATCH, PAST_LEN, IDX_DIM), 1.0),
        "state_hgrn": nrm(ks[5], (DEPTH, DEC_BATCH, HG_HEADS, HG_DK, HG_DV), 0.5),
        "w_in": nrm(ks[6], (DEPTH, D_MODEL, IN_COLS), D_MODEL ** -0.5),
        "hg_lb_logits": nrm(ks[7], (DEPTH, HG_WIDTH), 0.5),
        "hg_norm_w": 1.0 + nrm(ks[8], (DEPTH, HG_DV), 0.02),
        "w_br_hg": nrm(ks[9], (DEPTH, HG_HEADS * HG_DV, D_MODEL), (HG_HEADS * HG_DV) ** -0.5 * DN_BETA),
        "w_br_att": nrm(ks[10], (DEPTH, ATT_WIDTH, D_MODEL), ATT_WIDTH ** -0.5 * DN_BETA),
        "w_out": nrm(ks[11], (DEPTH, D_MODEL, D_MODEL), D_MODEL ** -0.5 * DN_BETA),
        "ln1_g": 1.0 + nrm(ks[12], (DEPTH, D_MODEL), 0.02),
        "ln1_b": nrm(ks[13], (DEPTH, D_MODEL), 0.02),
        "ln2_g": 1.0 + nrm(ks[14], (DEPTH, D_MODEL), 0.02),
        "ln2_b": nrm(ks[15], (DEPTH, D_MODEL), 0.02),
        "w_rg": nrm(ks[16], (DEPTH, D_MODEL, G), D_MODEL ** -0.5),
        "b_rg": nrm(ks[17], (DEPTH, G), 0.01),
        "w_re": nrm(ks[18], (DEPTH, D_MODEL, G * E), D_MODEL ** -0.5),
        "b_re": nrm(ks[19], (DEPTH, G * E), 0.01),
        "w_gate": nrm(ks[20], (DEPTH, G, E, D_MODEL, F), D_MODEL ** -0.5),
        "w_up": nrm(ks[21], (DEPTH, G, E, D_MODEL, F), D_MODEL ** -0.5),
        "w_down": nrm(ks[22], (DEPTH, G, E, F, D_MODEL), F ** -0.5 * DN_BETA),
    }

def reference(x_prompt, x_sample, cache_k, cache_v, cache_idx_k, state_hgrn,
              w_in, hg_lb_logits, hg_norm_w, w_br_hg, w_br_att, w_out,
              ln1_g, ln1_b, ln2_g, ln2_b, w_rg, b_rg, w_re, b_re, w_gate, w_up, w_down):
    lbs = hgrn_lower_bounds(hg_lb_logits)
    xp, xs = x_prompt, x_sample
    kp_l, vp_l, ikp_l, sp_l = [], [], [], []
    ks_l, vs_l, iks_l, ss_l = [], [], [], []
    for l in range(DEPTH):
        mp, kp, vp, ikp, sp = token_mixer(xp, w_in[l], lbs[l], hg_norm_w[l], w_br_hg[l], w_br_att[l],
                                          w_out[l], None, None, None, None)
        ms, ks, vs, iks, ss = token_mixer(xs, w_in[l], lbs[l], hg_norm_w[l], w_br_hg[l], w_br_att[l],
                                          w_out[l], state_hgrn[l], cache_k[l], cache_v[l], cache_idx_k[l])
        kp_l.append(kp); vp_l.append(vp); ikp_l.append(ikp); sp_l.append(sp)
        ks_l.append(ks); vs_l.append(vs); iks_l.append(iks); ss_l.append(ss.astype(state_hgrn.dtype))
        xp = layer_norm(DN_ALPHA * xp + mp, ln1_g[l], ln1_b[l])
        xs = layer_norm(DN_ALPHA * xs + ms, ln1_g[l], ln1_b[l])
        xp = layer_norm(DN_ALPHA * xp + hier_moe(xp, w_rg[l], b_rg[l], w_re[l], b_re[l], w_gate[l], w_up[l], w_down[l]),
                        ln2_g[l], ln2_b[l])
        xs = layer_norm(DN_ALPHA * xs + hier_moe(xs, w_rg[l], b_rg[l], w_re[l], b_re[l], w_gate[l], w_up[l], w_down[l]),
                        ln2_g[l], ln2_b[l])
    new_k_prompt = jnp.stack(kp_l)
    new_v_prompt = jnp.stack(vp_l)
    new_idx_k_prompt = jnp.stack(ikp_l)
    new_state_hgrn_prompt = jnp.stack(sp_l)
    new_k_sample = jnp.stack(ks_l)
    new_v_sample = jnp.stack(vs_l)
    new_idx_k_sample = jnp.stack(iks_l)
    new_state_hgrn_sample = jnp.stack(ss_l)
    return (xp, xs, new_k_prompt, new_v_prompt, new_idx_k_prompt, new_state_hgrn_prompt,
            new_k_sample, new_v_sample, new_idx_k_sample, new_state_hgrn_sample)


_drawn_inputs = setup_inputs


def setup_inputs(seed=0):
    import zlib

    import numpy as np

    out = dict(_drawn_inputs(seed))
    spreads = {}
    factors = {'state_hgrn': 8.0,
     'hg_norm_w': 28.278,
     'ln2_g': 8.202,
     'ln2_b': 8.214,
     'b_rg': 8.0,
     'b_re': 26.522,
     'cache_k': 3.564}
    for name, (base, spread) in spreads.items():
        noise = np.random.default_rng([zlib.crc32(name.encode()), seed]).standard_normal(out[name].shape)
        drawn = base * np.exp(spread * noise) if base else spread * noise
        out[name] = __import__('jax').numpy.asarray(drawn.astype(out[name].dtype))
    for name, factor in factors.items():
        out[name] = (out[name] * factor).astype(out[name].dtype)
    return out
```

```python
from contextlib import ExitStack

import concourse.bass as bass
from concourse import mybir

F32 = mybir.dt.float32
F32R = mybir.dt.float32r
I32 = mybir.dt.int32
U32 = mybir.dt.uint32
ALU = mybir.AluOpType
ACT = mybir.ActivationFunctionType
AX = mybir.AxisListType

P = 128
D = 1024
KD = D // P
TP, TS = 512, 64
T = TP + TS
HT = T // 2
NT = 5
ROWS = [128, 128, 128, 128, 64]
HH = 4
AH, AD = 8, 64
IH, ID = 4, 64
PAST = 256
NX, F = 16, 256
CAP = 128
BLOCKS = 5
SLOT = BLOCKS * CAP
TOPK = [0, 128, 128, 128, 80]
KEYS = [128, 256, 384, 512, PAST + TS]
MOFF = [0, 0, 256, 640, 1152]
NEG = -3.0e38
BIG = 1.0e30
ALPHA = 2.0 ** 0.25
GW = 256
RAW = 3

C_HQ, C_HF, C_HI, C_HG, C_AQ, C_AK, C_AV, C_IQ, C_IK, C_GH, C_GA = (
    0, 512, 1024, 1536, 2048, 2560, 3072, 3584, 3840, 3908, 4932)

LEVELS = 7


class Count:

    def __init__(self, sem):
        self.sem, self.n = sem, 0

    def by(self, ins):
        self.n += 1
        ins.then_inc(self.sem, 1)
        return self.n


def plan():
    groups, fills = [], []

    def group(kind, col, width, units):
        g = len(groups)
        groups.append((kind, col, width))
        for what in units:
            fills.append((g, what))

    group("in", C_IQ, 256, [("iq", 0), ("iq", 1)])
    group("in", C_IK, 68, [("ik", 0)])
    for j in range(2):
        group("in", C_HF + GW * j, GW, [("hf", 2 * j), ("hf", 2 * j + 1)])
    for j in range(2):
        group("in", C_HQ + GW * j, GW, [("hq", 2 * j), ("hq", 2 * j + 1)])
    for j in range(2):
        group("in", C_HI + GW * j, GW, [("hi", 3 * j + p) for p in range(3)])
    for j in range(2):
        group("in", C_HG + GW * j, GW, [("hg", 2 * j), ("hg", 2 * j + 1)])
    for j in range(8):
        group("in", C_GH + GW * j, GW, [("gate", 2 * j), ("gate", 2 * j + 1)])
    for j in range(2):
        group("in", C_AK + GW * j, GW, [("ak", 2 * j), ("ak", 2 * j + 1)])
    fills += [(None, ("kt", i)) for i in range(NT)]
    for j in range(2):
        group("in", C_AQ + GW * j, GW, [("aq", 2 * j), ("aq", 2 * j + 1)])
    for j in range(2):
        group("in", C_AV + GW * j, GW, [("av", 3 * j + p) for p in range(3)])
    fills += [(None, ("ao", i)) for i in range(NT)]
    for j in range(4):
        group("branch", GW * j, GW, [("br", 4 * j + n) for n in range(4)])
    for j in range(4):
        group("out", GW * j, GW, [("out", 3 * j + p) for p in range(3)])
    return groups, fills


def encoder_layer(nc, x_prompt, x_sample, cache_k, cache_v, cache_idx_k, state_hgrn, w_in, hg_norm_w,
                  w_br_hg, w_br_att, w_out, ln1_g, ln1_b, ln2_g, ln2_b, w_rg, b_rg, w_re, b_re,
                  w_gate, w_up, w_down, c_ident, c_pairs, c_reset, c_lower, c_small, c_eoff, c_tid,
                  y_prompt, y_sample, nk_p, nv_p, nik_p, ns_p, nk_s, nv_s, nik_s, ns_s):
    groups, fills = plan()
    NG = len(groups)
    fill_of = {what: KD + n for n, (_, what) in enumerate(fills)}
    last_of = {}
    for g, what in fills:
        last_of[g] = what

    gates_d = nc.dram_tensor("gates_d", [16, P, T], F32).ap()
    x1_d = nc.dram_tensor("x1_d", [T, D], F32).ap()
    slot_d = nc.dram_tensor("slot_d", [NX * SLOT, 1], U32).ap()
    ys_d = nc.dram_tensor("ys_d", [NX * SLOT, D], F32).ap()

    with ExitStack() as ctx:
        base = nc.sbuf_base + (-nc.sbuf_base) % 64

        class Area:

            def __init__(self, start):
                self.at = start

            def __call__(self, name, shape, dt=F32):
                n = 4
                for s in shape[1:]:
                    n *= s
                t = nc.alloc_sbuf_tensor_at(name, shape, dt, offset=base + self.at)
                self.at += n + (-n) % 64
                return t

        def sem(name):
            return ctx.enter_context(nc.semaphore(name))

        xa = Area(0)
        xh = xa("x_hi", [P, KD, T], F32R)
        xl = xa("x_lo", [P, KD, T], F32R)
        raw = xa("w_raw", [P, RAW, KD, GW])
        wh = xa("w_hi", [P, 2, KD, GW], F32R)
        wl = xa("w_lo", [P, 2, KD, GW], F32R)
        ident = xa("ident", [P, P])
        ones = xa("ones", [P, P])
        pairs = xa("pairs", [P, LEVELS + 1, P])
        reset = xa("reset", [P, T])
        small = xa("small", [P, 8])
        normw = xa("normw", [P, 1])
        maskb = xa("maskb", [P, 1472])
        tok4 = xa("tok4", [P, NT, 68])
        gring = xa("gring", [P, 3, T])
        o_all = xa("o_all", [P, HH, T])
        S = xa("S", [P, 2, HH, P])
        mixer_end = xa.at

        ya = Area(0)
        yh = ya("y_hi", [P, 8, T], F32R)
        yl = ya("y_lo", [P, 8, T], F32R)

        ha = Area(mixer_end)
        q = ha("q", [P, HH, T])
        kk = ha("kk", [P, HH, T])
        B = ha("B", [P, HH, T])
        L = ha("L", [P, HH, T])
        v = ha("v", [P, NT, 512])
        sg = ha("sg", [P, HH, T])
        qe = ha("qe", [P, T])
        kd = ha("kd", [P, T])
        Gm = ha("Gm", [P, LEVELS + 1, P])
        AT = ha("AT", [P, P])
        kdT = ha("kdT", [P, P])
        eBT = ha("eBT", [P, NT])
        xoff = ha.at
        X = ha("X", [P, LEVELS, T])
        rms = X[:, 0, :]
        osq = X[:, 1, :]
        ia = Area(xoff)
        qi = ia("qi", [P, 2, T])
        kiw = ia("kiw", [68, T])
        ki2 = ia("ki2", [P, T])
        kic = ia("kic", [P, 2, 2, ID])
        kicT = ia("kicT", [P, PAST])
        relu = ia("relu", [P, 2, 512])
        gflat = gring[:, :, :].rearrange("p a b -> p (a b)")
        wk, gt, eq = gflat[:, 0:512], gflat[:, 512:1024], gflat[:, 1024:1536]
        top = ha("top", [P, 8])
        cnt = ha("cnt", [P, 2])
        xtok_area = Area(mixer_end)
        xtok = xtok_area("xtok", [P, NT, D])

        aa = Area(mixer_end)
        qa = aa("qa", [P, 4, T])
        ka = aa("ka", [P, 4, T])
        va = aa("va", [P, NT, 512])
        kc = aa("kc", [P, 2, 512])
        kcT = aa("kcT", [P, 4, PAST])
        vc = aa("vc", [P, 2, 512])
        Lm = aa("Lm", [P, 2, 512])
        Pr = aa("Pr", [P, 2, 512])
        PT = aa("PT", [P, 2, 4, P])
        ktok = aa("ktok", [P, NT, 512])
        ao = aa("ao", [P, 2, 512])
        mask0 = aa("mask0", [P, P])
        rden = aa("rden", [P, AH])
        mx = aa("mx", [P, 2, 2])
        den = aa("den", [P, 2, AH])

        ma = Area(mixer_end)
        mh = ma("m_hi", [P, KD, T], F32R)
        ml = ma("m_lo", [P, KD, T], F32R)
        gld = ma("gld", [P, 2, 2, T])
        xr = ma("xr", [P, NT, D])
        lnr = ma("lnr", [P, 4, D])

        ra = Area(mixer_end)
        x1T = ra("x1T", [P, 2, KD, P])
        wr = ra("wr", [P, KD, 20])
        br_ = ra("br_", [P, 20])
        lower = ra("lower", [P, P])
        eoff = ra("eoff", [P, NX])
        tid = ra("tid", [P, NT], U32)
        zero = ra("zero", [P, NX * SLOT // P], U32)
        stats = ra("stats", [P, NT, 2, 6])
        mv = ra("mv", [P, NT, 2])
        rstd = ra("rstd", [P, NT])
        lg = ra("lg", [P, NT, 20])
        ge = ra("ge", [P, NT, 4])
        gx = ra("gx", [P, NT, 4])
        ohg = ra("ohg", [P, NT, 4])
        taken = ra("taken", [P, NT])
        prod = ra("prod", [P, NT, 4, 4])
        es = ra("es", [P, NT, 4])
        ee = ra("ee", [P, NT, 4])
        oh1 = ra("oh1", [P, NT, 4])
        oh2 = ra("oh2", [P, NT, 4])
        cols = ra("cols", [P, 10, NT])
        M1 = ra("M1", [P, NT, 4, 4])
        M2 = ra("M2", [P, NT, 4, 4])
        M = ra("M", [P, NT, NX])
        rank = ra("rank", [P, NT, NX])
        destf = ra("destf", [P, 2, NT])
        dest = ra("dest", [P, 2, NT], U32)
        flag = ra("flag", [P, 1], I32)
        stok = ra("stok", [P, NX], U32)
        stx = ra("stx", [P, 2], U32)
        zcol = ra("zcol", [P, 1], U32)
        zcol2 = ra("zcol2", [P, 1], U32)
        yg = ra("yg", [P, 2, 2, D])
        ea = Area(0)
        xg = ea("xg", [P, 2, D])
        xgT = ea("xgT", [P, 2, KD, P])
        hs = ea("hs", [P, 2, 2, CAP])
        hT = ea("hT", [P, 2, 2, CAP])
        ysb = ea("ysb", [P, 2, D])
        wa = Area(36864)
        wgu = wa("wgu", [P, 2, 2, KD, F])
        wd = wa("wd", [P, 2, 2, D])

        pp = ctx.enter_context(nc.psum_tensor("pp", [P, 2, 2, 512], F32))
        pw = ctx.enter_context(nc.psum_tensor("pw", [P, 4, 512], F32))
        ppf = [pp[:, b].rearrange("p a b -> p (a b)") for b in range(2)]

        s_x = [sem(f"s_xin{i}") for i in range(NT)]
        s_const = sem("s_const")
        s_raw = [sem(f"s_raw{i}") for i in range(RAW)]
        s_wh = sem("s_wh")
        s_wl = sem("s_wl")
        s_full = [sem(f"s_full{b}") for b in range(2)]
        s_free = [sem(f"s_free{b}") for b in range(2)]
        s_xh = sem("s_xh")
        s_xl = sem("s_xl")
        s_ones = sem("s_ones")
        d_chain, a_chain, p_chain = sem("d_chain"), sem("a_chain"), sem("p_chain")
        s_ev = {k: sem("s_ev_" + k) for k in ("iq", "ik", "hf", "hq", "hi", "hg", "gate", "ak", "aq", "av", "br", "out")}
        s_kic = sem("s_kic")
        s_ki2 = sem("s_ki2")
        s_it = sem("s_it")
        s_itc = sem("s_itc")
        s_sc = sem("s_sc")
        s_rl = sem("s_rl")
        s_acc = sem("s_acc")
        s_mask = sem("s_mask")
        s_L = sem("s_L")
        s_g = sem("s_g")
        s_k = sem("s_k")
        s_D = sem("s_D")
        s_X = sem("s_X")
        s_XM = sem("s_XM")
        s_qe = sem("s_qe")
        s_qem = sem("s_qem")
        s_G = sem("s_G")
        s_Gf = sem("s_Gf")
        s_AT = sem("s_AT")
        s_kdt = sem("s_kdt")
        s_ktc = sem("s_ktc")
        s_o = sem("s_o")
        s_of = sem("s_of")
        s_osq = sem("s_osq")
        s_ms = sem("s_ms")
        s_rms = sem("s_rms")
        s_y = sem("s_y")
        s_st = sem("s_st")
        s_gst = [sem(f"s_gst{i}") for i in range(3)]
        s_store = sem("s_store")
        s_kt = sem("s_kt_done")
        s_kc = sem("s_kc")
        s_vc = sem("s_vc")
        s_sk = sem("s_sk")
        s_ct = sem("s_ct")
        s_ctc = sem("s_ctc")
        s_lg = sem("s_lg")
        s_Lm = sem("s_Lm")
        s_nb = sem("s_nb")
        s_P = sem("s_P")
        s_PT = sem("s_PT")
        s_PTc = sem("s_PTc")
        s_O = sem("s_O")
        s_rd = sem("s_rd")
        s_ao = sem("s_ao")
        s_yh = sem("s_yh")
        s_yl = sem("s_yl")
        s_gl = [sem("s_gl0"), sem("s_gl1")]
        s_sig = sem("s_sig")
        s_br = sem("s_br")
        s_m = sem("s_m")
        s_mh = sem("s_mh")
        s_ml = sem("s_ml")
        s_xr = sem("s_xr")
        s_ln = sem("s_ln")
        s_pad = sem("s_pad")
        s_res = sem("s_res")
        s_var = sem("s_var")
        s_sd = sem("s_sd")
        s_x1 = sem("s_x1")
        s_x1d = sem("s_x1d")
        s_rc = sem("s_rc")
        s_zero = sem("s_zero")
        s_zd = sem("s_zd")
        s_tx = sem("s_tx")
        s_txc = sem("s_txc")
        s_rl_ = sem("s_rl_")
        s_ge = sem("s_ge")
        s_gx = sem("s_gx")
        s_M = sem("s_M")
        s_rk = sem("s_rk")
        s_dest = sem("s_dest")
        s_sct = sem("s_sct")
        s_stok = sem("s_stok")
        m_w = [sem(f"m_w{i}") for i in range(2)]
        m_wd = [sem(f"m_wd{i}") for i in range(2)]
        m_g = [sem(f"m_g{i}") for i in range(2)]
        m_t, m_tc, m_gu, m_si, m_h, m_y, m_yc = (sem(n) for n in ("m_t", "m_tc", "m_gu", "m_si", "m_h", "m_y", "m_yc"))
        m_ys = [sem(f"m_ys{i}") for i in range(2)]
        e_g2 = sem("e_g2")
        e_next = sem("e_next")
        e_i, e_w, e_ix, e_g = sem("e_i"), sem("e_w"), sem("e_ix"), sem("e_g")
        e_t, e_tc, e_gu, e_si, e_h, e_y, e_yc, e_ys = (sem(n) for n in ("e_t", "e_tc", "e_gu", "e_si", "e_h", "e_y", "e_yc", "e_ys"))
        s_yg = [sem(f"s_yg{i}") for i in range(2)]
        s_ygf = sem("s_ygf")
        s_xa = sem("s_xa")
        s_v2 = sem("s_v2")
        s_sd2 = sem("s_sd2")
        s_out = sem("s_out")

        ys_v = ys_d.rearrange("(b s e) d -> e b s d", e=NX, b=BLOCKS)
        slot_v = slot_d.rearrange("(b s e) a -> e b s a", e=NX, b=BLOCKS)
        w_gate_e = w_gate[0].rearrange("g e (k p) f -> (g e) p k f", p=P)
        w_up_e = w_up[0].rearrange("g e (k p) f -> (g e) p k f", p=P)
        w_down_e = w_down[0].rearrange("g e (k p) d -> (g e) p k d", p=P)

        def dram_w(kind, col, width, slot):
            if kind == "in":
                return [(raw[:, slot, :, 0:width], w_in[0].rearrange("(k p) c -> p k c", p=P)[:, :, col:col + width])]
            if kind == "branch":
                return [(raw[:, slot, 0:4, 0:width], w_br_hg[0].rearrange("(k p) c -> p k c", p=P)[:, :, col:col + width]),
                        (raw[:, slot, 4:8, 0:width], w_br_att[0].rearrange("(k p) c -> p k c", p=P)[:, :, col:col + width])]
            return [(raw[:, slot, :, 0:width], w_out[0].rearrange("(k p) c -> p k c", p=P)[:, :, col:col + width])]

        raw_need = []
        sums = [0] * RAW
        for g, (kind, _, _) in enumerate(groups):
            sums[g % RAW] += 32 if kind == "branch" else 16
            raw_need.append(sums[g % RAW])

        def group_used(engine, g):
            n = fill_of[last_of[g]]
            engine.wait_ge(s_full[n % 2], n // 2 + 1)

        block = ctx.enter_context(nc.Block())

        @block.sync
        def _(sp):
            xp = x_prompt[0].rearrange("(i p) d -> i p d", p=P)
            sp.dma_start(ident[:], c_ident).then_inc(s_const, 16)
            for i in range(4):
                sp.dma_start(xtok[:, i, :], xp[i]).then_inc(s_x[i], 16)
            sp.dma_start(xtok[0:64, 4, :], x_sample[0]).then_inc(s_x[4], 16)

            def load_group(g):
                if g >= RAW:
                    sp.wait_ge(s_wh, g - RAW + 1)
                    sp.wait_ge(s_wl, g - RAW + 1)
                for dst, src in dram_w(*groups[g], g % RAW):
                    sp.dma_start(dst, src).then_inc(s_raw[g % RAW], 16)

            def load_gates(m):
                if m >= 2:
                    sp.wait_ge(s_br, 2 * (m - 1))
                sp.dma_start(gld[:, m % 2], gates_d[m:m + 9:8].rearrange("a p t -> p a t")).then_inc(s_gl[m % 2], 16)

            for g in range(2):
                load_group(g)
            for dup in range(2):
                sp.dma_start(kic[:, :, dup, :], cache_idx_k[0, 0].rearrange("(j p) d -> p j d", p=P)).then_inc(s_kic, 16)
            sp.dma_start(pairs[:], c_pairs).then_inc(s_const, 16)
            sp.dma_start(reset[:], c_reset).then_inc(s_const, 16)
            sp.dma_start(small[:], c_small).then_inc(s_const, 16)
            sp.dma_start(normw[:], hg_norm_w.rearrange("a d -> d a")).then_inc(s_const, 16)
            load_group(2)
            for g in range(3, NG):
                load_group(g)
                if g == 4:
                    sp.wait_ge(s_ev["ik"], 1)
                    sp.dma_start(ki2[64:128, :], kiw[0:64, :]).then_inc(s_ki2, 16)
                if g == 5:
                    sp.wait_ge(s_xl, KD)
                    for h in range(HH):
                        sp.dma_start(S[:, 1, h, :], state_hgrn[0, 0, h]).then_inc(s_st, 16)
                if g == 21:
                    sp.wait_ge(s_y, HH)
                    sp.dma_start(kc[:], cache_k[0, 0].rearrange("(j p) h d -> p j (h d)", p=P)).then_inc(s_kc, 16)
                    sp.dma_start(vc[:], cache_v[0, 0].rearrange("(j p) h d -> p j (h d)", p=P)).then_inc(s_vc, 16)
                if g == 24:
                    sp.wait_ge(s_kt, NT)
                    sp.dma_start(nk_p[0, 0].rearrange("(i p) h d -> p i (h d)", p=P), ktok[:, 0:4, :]).then_inc(s_sk, 16)
                    sp.dma_start(nk_s[0, 0].rearrange("s h d -> s (h d)"), ktok[0:64, 4, :]).then_inc(s_sk, 16)
                if g == 27:
                    sp.wait_ge(s_ev["av"], 6)
                    sp.dma_start(nv_p[0, 0].rearrange("(i p) h d -> p i (h d)", p=P), va[:, 0:4, :]).then_inc(s_sk, 16)
                    sp.dma_start(nv_s[0, 0].rearrange("s h d -> s (h d)"), va[0:64, 4, :]).then_inc(s_sk, 16)
                    sp.wait_ge(s_yl, 1 + NT)
                    sp.wait_ge(s_sk, 64)
                    for c in range(3):
                        sp.wait_ge(s_gst[c], 16 * (6 if c == 0 else 5))
                    load_gates(0)
                    load_gates(1)
                    sp.dma_start(xr[:, 0:4, :], x_prompt[0].rearrange("(i p) d -> p i d", p=P)).then_inc(s_xr, 16)
                    sp.dma_start(xr[0:64, 4, :], x_sample[0]).then_inc(s_xr, 16)
                    for n, row in enumerate((ln1_g, ln1_b, ln2_g, ln2_b)):
                        sp.dma_start(lnr[:, n, :], row.broadcast_to([P, D])).then_inc(s_ln, 16)
                if 28 <= g < 31:
                    load_gates(2 * (g - 27))
                    load_gates(2 * (g - 27) + 1)

            sp.wait_ge(s_st, 64)
            for h in range(HH):
                sp.dma_start(ns_p[0, 0, h], S[:, 0, h, :]).then_inc(s_store, 16)
                sp.dma_start(ns_s[0, 0, h], S[:, 1, h, :]).then_inc(s_store, 16)
            sp.dma_start(nik_p[0, 0].rearrange("(i p) c -> p i c", p=P), tok4[:, 0:4, 0:64]).then_inc(s_store, 16)
            sp.dma_start(nik_s[0, 0], tok4[0:64, 4, 0:64]).then_inc(s_store, 16)
            def expert_weights(e, j):
                sp.dma_start(wgu[:, j, 0], w_gate_e[e]).then_inc(m_w[j], 16)
                sp.dma_start(wgu[:, j, 1], w_up_e[e]).then_inc(m_w[j], 16)

            def expert_down(e, j):
                sp.dma_start(wd[:, j], w_down_e[e]).then_inc(m_wd[j], 16)

            group_used(sp, NG - 1)
            sp.wait_ge(s_wl, NG)
            for dst, src in ((wr[:, :, 0:4], w_rg[0].rearrange("(k p) c -> p k c", p=P)),
                             (wr[:, :, 4:20], w_re[0].rearrange("(k p) c -> p k c", p=P)),
                             (br_[:, 0:4], b_rg.broadcast_to([P, 4])), (br_[:, 4:20], b_re.broadcast_to([P, 16])),
                             (lower[:], c_lower), (eoff[:], c_eoff), (tid[:], c_tid)):
                sp.dma_start(dst, src).then_inc(s_rc, 16)
            sp.wait_ge(s_zero, 1)
            sp.dma_start(slot_d.rearrange("(p n) a -> p (n a)", p=P), zero[:]).then_inc(s_zd, 16)
            for j in range(2):
                expert_weights(j, j)
                expert_down(j, j)
            for i in range(NT):
                sp.wait_ge(s_x1, i + 1)
                sp.dma_start(x1_d[i * P:i * P + ROWS[i]], xr[0:ROWS[i], i, :]).then_inc(s_x1d, 16)
            sp.wait_ge(s_sct, 16 * 2 * NT)
            sp.dma_start(stok[:], slot_d[0:CAP * NX].rearrange("(s e) a -> s (e a)", e=NX)).then_inc(s_stok, 16)

            def store_y(e, j):
                sp.dma_start(ys_v[e, 0], ysb[:, j, :]).then_inc(m_ys[j], 16)

            with sp.Fori(1, NX // 2) as i:
                for j in range(2):
                    sp.wait_ge(m_gu, 2 * i + (j - 1))
                    expert_weights(2 * i + j, j)
                    sp.wait_ge(m_y, 2 * i + (j - 1))
                    expert_down(2 * i + j, j)
                    sp.wait_ge(m_yc, 2 * i + (j - 1))
                    store_y(2 * i + (j - 2), j)
            for j in range(2):
                sp.wait_ge(m_yc, NX - 1 + j)
                store_y(NX - 2 + j, j)
            sp.wait_ge(s_dest, 1)
            over = sp.value_load(flag[0:1, 0:1], min_val=0, max_val=1)
            with sp.If(over > 0):
                sp.wait_ge(m_y, NX)
                sp.wait_ge(m_ys[0], 16 * NX // 2)
                sp.wait_ge(m_ys[1], 16 * NX // 2)
                with sp.Fori(0, NX) as e:
                    for k in range(1, BLOCKS):
                        n = (BLOCKS - 1) * e + k
                        sp.wait_ge(e_i, n)
                        sp.dma_start(wgu[:, 0, 0], w_gate_e[e]).then_inc(e_w, 16)
                        sp.dma_start(wgu[:, 0, 1], w_up_e[e]).then_inc(e_w, 16)
                        sp.dma_start(wd[:, 0], w_down_e[e]).then_inc(e_w, 16)
                        sp.dma_start(stx[:, 0:1], slot_v[e, k], allow_slow_non_contiguous=True).then_inc(e_w, 16)
                        sp.wait_ge(e_yc, n)
                        sp.dma_start(ys_v[e, k], ysb[:, 0, :]).then_inc(e_ys, 16)
                        sp.wait_ge(e_ys, 16 * n)
                        sp.sem_inc(e_next, 1)
            for i in range(NT):
                sp.wait_ge(s_out, i + 1)
                dst = y_prompt[0, i * P:(i + 1) * P] if i < 4 else y_sample[0]
                sp.dma_start(dst, xr[0:ROWS[i], i, :]).then_inc(s_store, 16)
            sp.wait_ge(s_store, 16 * (2 * HH + 2 + NT))
            sp.wait_ge(s_sk, 16 * 4)

        @block.tensor
        def _(pe):
            pe.wait_ge(s_const, 16)

            def open_fill(n):
                b = n % 2
                if n >= 2:
                    pe.wait_ge(s_free[b], n // 2)
                return b

            def transpose_x(k):
                b = open_fill(k)
                for i in range(NT):
                    if k == 0:
                        pe.wait_ge(s_x[i], 16)
                    r = ROWS[i]
                    mm = pe.transpose(ppf[b][:, i * P:i * P + r], xtok[0:r, i, k * P:(k + 1) * P], ident[0:r, 0:r])
                mm.then_inc(s_full[b], 1)

            def columns(lhs_h, lhs_l, rhs_h, rhs_l, ks, b):
                for x, k in enumerate(ks):
                    for y, (lw, rx) in enumerate(((lhs_h, rhs_h), (lhs_h, rhs_l), (lhs_l, rhs_h))):
                        for half in range(2):
                            mm = pe.matmul(pp[0:lw(k).shape[1], b, half, 0:HT], lw(k), rx(k, half),
                                           start=(x == 0 and y == 0), stop=(x == len(ks) - 1 and y == 2))
                return mm

            def fill(n, g, what):
                kind, c = what
                slot = g % 2
                b = open_fill(n)
                if kind in ("iq", "ik", "hf", "hq", "hg", "gate", "ak", "aq"):
                    lo = 0 if kind == "ik" else P * (c % 2)
                    hi = lo + (68 if kind == "ik" else P)
                    mm = columns(lambda k: wh[:, slot, k, lo:hi], lambda k: wl[:, slot, k, lo:hi],
                                 lambda k, h: xh[:, k, h * HT:(h + 1) * HT],
                                 lambda k, h: xl[:, k, h * HT:(h + 1) * HT], range(KD), b)
                elif kind == "br":
                    lo = P * (c // 2 % 2)
                    k0 = 4 * (c % 2)
                    if c == 0:
                        pe.wait_ge(s_yh, 1 + NT)
                        pe.wait_ge(s_yl, 1 + NT)
                    mm = columns(lambda k: wh[:, slot, k, lo:lo + P], lambda k: wl[:, slot, k, lo:lo + P],
                                 lambda k, h: yh[:, k, h * HT:(h + 1) * HT],
                                 lambda k, h: yl[:, k, h * HT:(h + 1) * HT], range(k0, k0 + 4), b)
                elif kind in ("hi", "av", "out"):
                    ah, al = (mh, ml) if kind == "out" else (xh, xl)
                    if kind == "out" and c == 0:
                        pe.wait_ge(s_mh, KD)
                        pe.wait_ge(s_ml, KD)
                    for i in range(2 * (c % 3), min(2 * (c % 3) + 2, NT)):
                        r = ROWS[i]
                        for k in range(KD):
                            for y, (lx, rw) in enumerate(((ah, wh), (al, wh), (ah, wl))):
                                mm = pe.matmul(pp[0:r, b, i % 2, 0:GW], lx[:, k, i * P:i * P + r], rw[:, slot, k, :],
                                               start=(k == 0 and y == 0), stop=(k == KD - 1 and y == 2))
                mm.then_inc(s_full[b], 1)
                return mm

            def index_transposes():
                pe.wait_ge(s_kic, 32)
                for j in range(2):
                    mm = pe.transpose(pw[:, 2, j * P:(j + 1) * P], kic[:, j].rearrange("p a b -> p (a b)"), ident[:])
                mm.then_inc(s_it, 1)
                pe.wait_ge(s_ev["ik"], 1)
                for i in range(NT):
                    r = ROWS[i]
                    mm = pe.transpose(pw[0:r, 3, i * 68:(i + 1) * 68], kiw[:, i * P:i * P + r], ident[0:68, 0:68])
                mm.then_inc(s_it, 1)

            def index_scores(n, i):
                for ih in range(IH):
                    s = 4 * n + ih
                    if s >= 2:
                        pe.wait_ge(s_rl, s - 1)
                    lo = 64 * (ih % 2)
                    r = ROWS[i]
                    ql = qi[lo:lo + 64, ih // 2, i * P:i * P + r]
                    kt = ki2 if ih % 2 else kiw
                    if ih % 2:
                        pe.wait_ge(s_ki2, 16)
                    out = pw[0:r, s % 2, :]
                    if i < 4:
                        mm = pe.matmul(out[:, 0:KEYS[i]], ql, kt[lo:lo + 64, 0:KEYS[i]], start=True, stop=True)
                    else:
                        pe.matmul(out[:, 0:PAST], ql, kicT[lo:lo + 64, :], start=True, stop=True)
                        mm = pe.matmul(out[:, PAST:PAST + TS], ql, kt[lo:lo + 64, TP:T], start=True, stop=True)
                    mm.then_inc(s_sc, 1)

            def hgrn_pairs(u):
                h, c = u // NT, u % NT
                cs, cw = c * P, ROWS[c]
                nl = LEVELS if c < 4 else LEVELS - 1
                if u == 0:
                    pe.wait_ge(s_rl, 16)
                    pe.wait_ge(s_itc, 2)
                else:
                    pe.wait_ge(s_Gf, u)
                pe.wait_ge(s_XM, 14 * h + 14)
                G = pw[:, 0:2, :].rearrange("p a (b c) -> p (a b) c", c=P)
                pe.matmul(G[0:cw, 0, 0:cw], kk[:, h, cs:cs + cw], q[:, h, cs:cs + cw], start=True, stop=True)
                for l in range(nl):
                    xx = X[:, l, cs:cs + cw]
                    mm = pe.matmul(G[0:cw, l + 1, 0:cw], xx, xx, start=True, stop=True)
                mm.then_inc(s_G, 1)
                if u >= 1:
                    pe.wait_ge(s_ktc, u)
                pe.wait_ge(s_qem, 2 * h + 2)
                pe.transpose(pw[0:cw, 2, 0:P], kd[:, cs:cs + cw], ident[:]).then_inc(s_kdt, 1)

            def hgrn_out(u):
                h, c = u // NT, u % NT
                cs, cw = c * P, ROWS[c]
                pe.wait_ge(s_AT, u + 1)
                if u >= 1:
                    pe.wait_ge(s_of, u)
                if u >= 1 and u % NT == 0:
                    pe.wait_ge(s_rms, u // NT)
                if c == 4:
                    pe.wait_ge(s_st, 64)
                vv = v[0:cw, c, h * P:(h + 1) * P]
                group = 0 if c < 4 else 1
                pe.matmul(pw[:, 3, 0:cw], vv, AT[0:cw, 0:cw], start=True, stop=(c == 0))
                if c > 0:
                    pe.matmul(pw[:, 3, 0:cw], S[:, group, h, :], qe[:, cs:cs + cw], start=False, stop=True)
                pe.wait_ge(s_ktc, u + 1)
                pe.matmul(pw[:, 3, 256:384], kdT[0:cw, :], vv, start=True, stop=True).then_inc(s_o, 1)

            def hgrn_square(h):
                pe.wait_ge(s_osq, h + 1)
                pe.wait_ge(s_Gf, NT * (h + 1))
                for half in range(2):
                    mm = pe.matmul(pw[:, half, 0:HT], ones[:], osq[:, half * HT:(half + 1) * HT], start=True, stop=True)
                mm.then_inc(s_ms, 1)

            for k in range(KD):
                transpose_x(k)
            hg_step = [0]

            def hgrn_some(n):
                for _ in range(n):
                    u = hg_step[0]
                    if u >= HH * NT:
                        return
                    hgrn_pairs(u)
                    hgrn_out(u)
                    if u % NT == NT - 1:
                        hgrn_square(u // NT)
                    hg_step[0] += 1

            def key_rows(i):
                n = fill_of[("kt", i)]
                b = open_fill(n)
                pe.wait_ge(s_ev["ak"], 4)
                r = ROWS[i]
                for c in range(4):
                    mm = pe.transpose(ppf[b][0:r, c * P:(c + 1) * P], ka[:, c, i * P:i * P + r], ident[:])
                mm.then_inc(s_full[b], 1)

            def cache_keys():
                for j in range(2):
                    pe.wait_ge(s_kc, 16)
                    pe.wait_ge(s_rms, HH)
                    for c in range(4):
                        mm = pe.transpose(pw[:, j, c * P:(c + 1) * P], kc[:, j, c * P:(c + 1) * P], ident[:])
                    mm.then_inc(s_ct, 1)

            def logits(a):
                i, h = a // AH, a % AH
                r, lo, w = ROWS[i], 64 * (h % 2), KEYS[i]
                if a == 0:
                    pe.wait_ge(s_ctc, 2)
                    pe.wait_ge(s_ev["aq"], 4)
                if a >= 2:
                    pe.wait_ge(s_Lm, a - 1)
                ql = qa[lo:lo + 64, h // 2, i * P:i * P + r]
                out = pw[0:r, a % 2, :]
                if i < 4:
                    mm = pe.matmul(out[:, 0:w], ql, ka[lo:lo + 64, h // 2, 0:w], start=True, stop=True)
                else:
                    pe.matmul(out[:, 0:PAST], ql, kcT[lo:lo + 64, h // 2, :], start=True, stop=True)
                    mm = pe.matmul(out[:, PAST:w], ql, ka[lo:lo + 64, h // 2, TP:T], start=True, stop=True)
                mm.then_inc(s_lg, 1)

            def key_parts(i):
                return [(j * P, min(P, KEYS[i] - j * P)) for j in range((KEYS[i] + P - 1) // P)]

            def turn(a):
                i = a // AH
                r = ROWS[i]
                pe.wait_ge(s_P, a + 1)
                if a >= 1:
                    pe.wait_ge(s_PTc, a)
                for j, (at, w) in enumerate(key_parts(i)):
                    mm = pe.transpose(pw[0:w, 2, j * P:j * P + r], Pr[0:r, a % 2, at:at + w], ident[0:r, 0:r])
                mm.then_inc(s_PT, 1)

            def values(a):
                i, h = a // AH, a % AH
                r = ROWS[i]
                pe.wait_ge(s_PTc, a + 1)
                if a == 0:
                    pe.wait_ge(s_vc, 16)
                    pe.wait_ge(s_ev["av"], 6)
                if h == 0 and i >= 1:
                    pe.wait_ge(s_ao, i)
                parts = key_parts(i)
                for j, (at, w) in enumerate(parts):
                    vv = va[0:w, j if i < 4 else 4, h * AD:(h + 1) * AD] if i < 4 or j == 2 else vc[:, j, h * AD:(h + 1) * AD]
                    mm = pe.matmul(pw[0:r, 3, h * AD:(h + 1) * AD], PT[0:w, a % 2, j, 0:r], vv,
                                   start=(j == 0), stop=(j == len(parts) - 1))
                mm.then_inc(s_O, 1)

            def tile_columns(i):
                n = fill_of[("ao", i)]
                b = open_fill(n)
                pe.wait_ge(s_ao, i + 1)
                r = ROWS[i]
                for c in range(4):
                    mm = pe.transpose(ppf[b][:, c * P:c * P + r], ao[0:r, i % 2, c * P:(c + 1) * P], ident[0:r, 0:r])
                mm.then_inc(s_full[b], 1)

            def attention():
                NA = NT * AH
                for a in range(NA + 2):
                    if a < NA:
                        logits(a)
                    if 1 <= a <= NA:
                        turn(a - 1)
                    if a >= 2:
                        values(a - 2)
                    if a >= 4 and (a - 4) % AH == AH - 1:
                        tile_columns((a - 4) // AH)
                tile_columns(NT - 1)

            for n, (g, what) in enumerate(fills):
                if what[0] == "kt":
                    key_rows(what[1])
                    if what[1] == NT - 1:
                        cache_keys()
                    continue
                if what[0] == "ao":
                    if what[1] == 0:
                        attention()
                    continue
                if n == 0 or fills[n - 1][0] != g:
                    pe.wait_ge(s_wh, g + 1)
                    pe.wait_ge(s_wl, g + 1)
                    if g == 0:
                        pe.wait_ge(s_xh, KD)
                        pe.wait_ge(s_xl, KD)
                fill(KD + n, g, what)
                if what == ("hf", 0):
                    index_transposes()
                if what == ("hf", 1):
                    pe.wait_ge(s_itc, 2)
                    pe.wait_ge(s_ev["iq"], 2)
                    index_scores(0, 3)
                    index_scores(1, 4)
                if what == ("hf", 3):
                    index_scores(2, 2)
                    index_scores(3, 1)
                if what[0] == "gate":
                    hgrn_some(2 if what[1] % 4 else 1)

            for i in range(NT):
                b = i % 2
                pe.wait_ge(s_x1, i + 1)
                if i == 0:
                    pe.wait_ge(s_res, 12)
                    pe.wait_ge(s_rc, 112)
                if i >= 2:
                    pe.wait_ge(s_txc, i - 1)
                for k in range(KD):
                    mm = pe.transpose(ppf[b][:, k * P:(k + 1) * P], xr[:, i, k * P:(k + 1) * P], ident[:])
                mm.then_inc(s_tx, 1)
                pe.wait_ge(s_txc, i + 1)
                for k in range(KD):
                    mm = pe.matmul(pw[:, 0, 20 * i:20 * i + 20], x1T[:, b, k, :], wr[:, k, :], start=(k == 0), stop=(k == KD - 1))
                mm.then_inc(s_rl_, 1)
            pe.wait_ge(s_M, 1)
            for i in range(NT):
                for j in range(i + 1):
                    pe.matmul(pw[:, 1, NX * i:NX * (i + 1)], lower[:] if j == i else ones[:], M[:, j, :],
                              start=(j == 0), stop=(j == i))
            for j in range(NT):
                mm = pe.matmul(pw[:, 1, NX * NT:NX * (NT + 1)], ones[:], M[:, j, :], start=(j == 0), stop=(j == NT - 1))
            mm.then_inc(s_rk, 1)

            def expert(n, j, first, sems):
                g, t, tc, w, wdn, gu, h_, y_, yc, si, ga, wa_, wb = sems
                pe.wait_ge(g, ga)
                if not first:
                    pe.wait_ge(tc, n)
                for k in range(KD):
                    mm = pe.transpose(ppf[0][:, k * P:(k + 1) * P], xg[:, j, k * P:(k + 1) * P], ident[:])
                mm.then_inc(t, 1)
                pe.wait_ge(w, wa_)
                pe.wait_ge(tc, n + 1)
                if not first:
                    pe.wait_ge(h_, n)
                for half in range(2):
                    for f in range(2):
                        for k in range(KD):
                            mm = pe.matmul(pw[:, 0, (2 * half + f) * P:(2 * half + f + 1) * P], wgu[:, j, half, k, f * P:(f + 1) * P],
                                           xgT[:, j, k, :], start=(k == 0), stop=(k == KD - 1))
                mm.then_inc(gu, 1)
                pe.wait_ge(h_, n + 1)
                pe.wait_ge(wdn, wb)
                if not first:
                    pe.wait_ge(yc, n)
                for half in range(2):
                    for f in range(2):
                        mm = pe.matmul(ppf[1][:, half * 512:(half + 1) * 512], hT[:, j, f, :], wd[:, j, f, half * 512:(half + 1) * 512],
                                       start=(f == 0), stop=(f == 1))
                mm.then_inc(y_, 1)

            def main_expert(i, j, first):
                expert(2 * i + j, j, first, (m_g[j], m_t, m_tc, m_w[j], m_wd[j], m_gu, m_h, m_y, m_yc, m_si,
                                             16 * i + 16, 32 * i + 32, 16 * i + 16))

            main_expert(0, 0, True)
            main_expert(0, 1, False)
            with pe.Fori(1, NX // 2) as i:
                for j in range(2):
                    main_expert(i, j, False)
            over = pe.value_load(flag[0:1, 0:1], min_val=0, max_val=1)
            with pe.If(over > 0):
                pe.wait_ge(m_tc, NX)
                pe.wait_ge(m_h, NX)
                pe.wait_ge(m_yc, NX)
                with pe.Fori(0, NX * (BLOCKS - 1)) as n:
                    expert(n, 0, True, (e_g, e_t, e_tc, e_w, e_w, e_gu, e_h, e_y, e_yc, e_si,
                                        16 * n + 16, 64 * n + 64, 64 * n + 64))

        @block.scalar
        def _(act):
            chain = Count(a_chain)

            def link(ins):
                act.wait_ge(a_chain, chain.by(ins))

            def cut(g):
                act.wait_ge(s_raw[g % RAW], raw_need[g])
                if g >= 2:
                    group_used(act, g - 2)
                width = groups[g][2]
                act.activation(wh[:, g % 2, :, 0:width], raw[:, g % RAW, :, 0:width], ACT.Copy).then_inc(s_wh, 1)

            def evacuate(what):
                kind, c = what
                n = fill_of[what]
                b = n % 2
                act.wait_ge(s_full[b], n // 2 + 1)
                src = pp[:, b, :, 0:HT]
                two = lambda t: t.rearrange("p (a b) -> p a b", a=2)
                func = ACT.Copy
                if kind in ("ak", "aq"):
                    if c == 0 and kind == "ak":
                        act.wait_ge(s_y, HH)
                    dst = two((ka if kind == "ak" else qa)[:, c, :])
                elif kind == "iq":
                    dst = two(qi[:, c, :])
                elif kind == "ik":
                    src, dst = pp[0:68, b, :, 0:HT], two(kiw[:, :])
                elif kind == "hf":
                    dst = two(B[:, c, :])
                elif kind == "hq":
                    dst, func = two(q[:, c, :]), ACT.Silu
                elif kind == "hg":
                    dst, func = two(sg[:, c, :]), ACT.Silu
                elif kind == "gate":
                    if c == 0:
                        act.wait_ge(s_mask, 4)
                    if c >= 3:
                        act.wait_ge(s_gst[c % 3], 16 * (c // 3))
                    dst = two(gring[:, c % 3, :])
                elif kind in ("hi", "av"):
                    t = v if kind == "hi" else va
                    i, cc = 2 * (c % 3), GW * (c // 3)
                    if i < 4:
                        src, dst = pp[:, b, :, 0:GW], t[:, i:i + 2, cc:cc + GW]
                    else:
                        src, dst = pp[0:64, b, 0, 0:GW], t[0:64, 4, cc:cc + GW]
                ev = act.activation(dst, src, func)
                ev.then_inc(s_ev[kind], 1)
                act.wait_ge(s_ev[kind], c + 1)
                act.nop().then_inc(s_free[b], 1)
                if kind == "gate":
                    act.dma_start(gates_d[c], gring[:, c % 3, :]).then_inc(s_gst[c % 3], 16)

            def x_high(k):
                b = k % 2
                act.wait_ge(s_full[b], k // 2 + 1)
                act.activation(xh[:, k, :], ppf[b][:, 0:T], ACT.Copy).then_inc(s_xh, 1)

            def index_copies():
                act.wait_ge(s_it, 1)
                act.activation(kicT[:], pw[:, 2, 0:PAST], ACT.Copy).then_inc(s_itc, 1)
                act.wait_ge(s_it, 2)
                act.activation(tok4[:, 0:4, :], pw[:, 3, 0:272].rearrange("p (i c) -> p i c", c=68), ACT.Copy).then_inc(a_chain, 1)
                chain.n += 1
                act.activation(tok4[0:64, 4, :], pw[0:64, 3, 272:340], ACT.Copy).then_inc(s_itc, 1)

            def index_relu(n, i):
                r = ROWS[i]
                for ih in range(IH):
                    s = 4 * n + ih
                    act.wait_ge(s_sc, s + 1)
                    if s >= 2:
                        act.wait_ge(s_acc, s - 1)
                    act.activation(relu[0:r, s % 2, 0:KEYS[i]], pw[0:r, s % 2, 0:KEYS[i]], ACT.Relu, scale=ID ** -0.5).then_inc(s_rl, 1)

            def softplus(h):
                act.wait_ge(s_ev["hf"], h + 1)
                link(act.activation(L[:, h, :], B[:, h, :], ACT.Abs))
                link(act.activation(L[:, h, :], L[:, h, :], ACT.Exp, scale=-1.0))
                act.activation(L[:, h, :], L[:, h, :], ACT.Ln, bias=1.0).then_inc(s_L, 1)

            def key(h):
                act.wait_ge(s_g, 2 * h + 1)
                act.activation(kk[:, h, :], kk[:, h, :], ACT.Exp, scale=-1.0).then_inc(s_k, 1)

            def levels(h):
                for l in range(LEVELS):
                    act.wait_ge(s_D, 14 * h + 2 * l + 2)
                    w = TP if l == LEVELS - 1 else T
                    act.activation(X[:, l, 0:w], X[:, l, 0:w], ACT.Exp).then_inc(s_X, 1)
                if h >= 1:
                    act.wait_ge(s_o, NT * h)
                    act.wait_ge(s_kdt, NT * h)
                act.activation(qe[:, :], B[:, h, :], ACT.Exp).then_inc(s_qe, 1)
                for c in range(NT):
                    cs, cw = c * P, ROWS[c]
                    e = act.activation(kd[:, cs:cs + cw], B[:, h, cs:cs + cw], ACT.Exp, scale=-1.0,
                                       bias=B[:, h, cs + cw - 1:cs + cw])
                e.then_inc(s_qe, 1)
                if h >= 1:
                    act.wait_ge(s_of, NT * h)
                act.activation(eBT[:, 0:4], B[:, h, P - 1:TP:P], ACT.Exp).then_inc(a_chain, 1)
                act.activation(eBT[:, 4:5], B[:, h, T - 1:T], ACT.Exp).then_inc(s_qe, 1)
                chain.n += 1

            def kd_copy(u):
                cw = ROWS[u % NT]
                act.wait_ge(s_kdt, u + 1)
                if u >= 1:
                    act.wait_ge(s_o, u)
                act.activation(kdT[0:cw, :], pw[0:cw, 2, 0:P], ACT.Copy).then_inc(s_ktc, 1)

            def head_norm(h):
                act.wait_ge(s_ms, h + 1)
                rr = rms.rearrange("p (a b) -> p a b", a=2)
                link(act.activation(rr, pw[:, 0:2, 0:HT], ACT.Ln, scale=1.0 / P, bias=small[:, 0:1]))
                act.activation(rms, rms, ACT.Exp, scale=-0.5).then_inc(s_rms, 1)

            for k in range(KD):
                x_high(k)
                if k == 3:
                    cut(0)
            cut(1)
            act.wait_ge(s_const, 80)
            hstep = [0]

            def hgrn_some(n):
                for _ in range(n):
                    u = hstep[0]
                    if u >= HH * NT:
                        return
                    if u % NT == 0:
                        levels(u // NT)
                    kd_copy(u)
                    if u % NT == NT - 1:
                        head_norm(u // NT)
                    hstep[0] += 1

            def cached_keys():
                for j in range(2):
                    act.wait_ge(s_ct, j + 1)
                    act.activation(kcT[:, :, j * P:(j + 1) * P], pw[:, j, :].rearrange("p (c t) -> p c t", c=4), ACT.Copy).then_inc(s_ctc, 1)

            def probs(a):
                i, h = a // AH, a % AH
                r, w = ROWS[i], KEYS[i]
                act.wait_ge(s_nb, a + 1)
                if a >= 2:
                    act.wait_ge(s_PT, a - 1)
                if h == 0 and i >= 2:
                    act.wait_ge(s_rd, i - 1)
                act.activation(Pr[0:r, a % 2, 0:w], Lm[0:r, a % 2, 0:w], ACT.Exp, scale=AD ** -0.5,
                               bias=mx[0:r, a % 2, 1:2], accum_out=den[0:r, i % 2, h:h + 1]).then_inc(s_P, 1)

            def probs_copy(a):
                i = a // AH
                r, nj = ROWS[i], (KEYS[i] + P - 1) // P
                act.wait_ge(s_PT, a + 1)
                if a >= 2:
                    act.wait_ge(s_O, a - 1)
                src = pw[:, 2, :].rearrange("p (j t) -> p j t", j=4)
                if i < 4:
                    ins = act.activation(PT[:, a % 2, 0:nj, :], src[:, 0:nj, :], ACT.Copy)
                else:
                    link(act.activation(PT[:, a % 2, 0:2, 0:64], src[:, 0:2, 0:64], ACT.Copy))
                    ins = act.activation(PT[0:64, a % 2, 2, 0:64], src[0:64, 2, 0:64], ACT.Copy)
                ins.then_inc(s_PTc, 1)

            def tile_high(i):
                n = fill_of[("ao", i)]
                b, r = n % 2, ROWS[i]
                act.wait_ge(s_full[b], n // 2 + 1)
                act.activation(yh[:, 4:8, i * P:i * P + r], ppf[b][:, 0:512].rearrange("p (c t) -> p c t", c=4)[:, :, 0:r],
                               ACT.Copy).then_inc(s_yh, 1)

            def attention():
                NA = NT * AH
                group_used(act, 23)
                act.activation(yh[:, 0:4, :], o_all[:], ACT.Copy).then_inc(s_yh, 1)
                for a in range(NA + 2):
                    if a < NA:
                        probs(a)
                    if 1 <= a <= NA:
                        probs_copy(a - 1)
                    if a >= 4 and (a - 4) % AH == AH - 1:
                        tile_high((a - 4) // AH)
                tile_high(NT - 1)

            def gates(m):
                act.wait_ge(s_gl[m % 2], 16 * (m // 2 + 1))
                g_ = gld[:, m % 2].rearrange("p a t -> p (a t)")
                act.activation(g_, g_, ACT.Sigmoid).then_inc(s_sig, 1)

            def merged_high(m):
                act.wait_ge(s_m, m + 1)
                act.activation(mh[:, m, :], gring[:, 2, :], ACT.Copy).then_inc(s_mh, 1)

            for n, (gg, what) in enumerate(fills):
                if what[0] == "kt":
                    if what[1] == NT - 1:
                        cached_keys()
                    continue
                if what[0] == "ao":
                    if what[1] == 0:
                        attention()
                        cut(24)
                        cut(25)
                    continue
                if what == ("hf", 0):
                    act.wait_ge(s_xl, KD)
                if what[0] == "br":
                    if what[1] % 2 == 0:
                        gates(what[1] // 2)
                    else:
                        merged_high(what[1] // 2)
                elif what[0] != "out":
                    evacuate(what)
                if what == ("hf", 0):
                    index_copies()
                if what == ("hf", 1):
                    index_relu(0, 3)
                    index_relu(1, 4)
                if what == ("hf", 3):
                    index_relu(2, 2)
                    index_relu(3, 1)
                if last_of[gg] == what and gg + 2 < NG and gg + 2 not in (24, 25):
                    cut(gg + 2)
                if what == ("hf", 3):
                    for h in range(HH):
                        softplus(h)
                if what == ("hg", 3):
                    for h in range(HH):
                        key(h)
                if what[0] == "gate":
                    hgrn_some(2 if what[1] % 4 else 1)

            for i in range(NT):
                act.wait_ge(s_var, i + 1)
                act.activation(rstd[:, i:i + 1], mv[:, i, 1:2], ACT.Sqrt, bias=small[:, 1:2]).then_inc(s_sd, 1)
            for i in range(NT):
                b = i % 2
                act.wait_ge(s_tx, i + 1)
                if i >= 2:
                    act.wait_ge(s_rl_, i - 1)
                act.activation(x1T[:, b].rearrange("p k t -> p (k t)"), ppf[b], ACT.Copy).then_inc(s_txc, 1)
            act.wait_ge(s_gx, 1)
            act.activation(ge[:], gx[:], ACT.Exp).then_inc(s_ge, 1)
            act.wait_ge(s_gx, 2)
            act.activation(ee[:], es[:], ACT.Exp).then_inc(s_ge, 1)

            def expert(n, j, first, t, tc, gu_prev, gu, si, h_):
                act.wait_ge(t, n + 1)
                if gu_prev is not None:
                    act.wait_ge(gu, gu_prev)
                act.activation(xgT[:, j].rearrange("p k t -> p (k t)"), ppf[0], ACT.Copy).then_inc(tc, 1)
                act.wait_ge(gu, n + 1)
                if not first:
                    act.wait_ge(h_, n)
                act.activation(hs[:, j].rearrange("p f t -> p (f t)"), pw[:, 0, 0:256], ACT.Silu).then_inc(si, 1)

            expert(0, 0, True, m_t, m_tc, None, m_gu, m_si, m_h)
            expert(1, 1, False, m_t, m_tc, None, m_gu, m_si, m_h)
            with act.Fori(1, NX // 2) as i:
                for j in range(2):
                    expert(2 * i + j, j, False, m_t, m_tc, 2 * i + (j - 1), m_gu, m_si, m_h)
            over = act.value_load(flag[0:1, 0:1], min_val=0, max_val=1)
            with act.If(over > 0):
                act.wait_ge(m_h, NX)
                with act.Fori(0, NX * (BLOCKS - 1)) as n:
                    expert(n, 0, True, e_t, e_tc, None, e_gu, e_si, e_h)
            for i in range(NT):
                act.wait_ge(s_v2, i + 1)
                act.activation(rstd[:, i:i + 1], mv[:, i, 1:2], ACT.Sqrt, bias=small[:, 1:2]).then_inc(s_sd2, 1)

        @block.gpsimd
        def _(pool):
            def cut(g):
                width = groups[g][2]
                pool.wait_ge(s_wh, g + 1)
                pool.tensor_tensor(wl[:, g % 2, :, 0:width], raw[:, g % RAW, :, 0:width],
                                   wh[:, g % 2, :, 0:width].bitcast(F32), ALU.subtract).then_inc(s_wl, 1)

            pool.memset(ones[:], 1.0).then_inc(s_ones, 1)

            def times(h):
                if h == 0:
                    pool.wait_ge(s_k, HH)
                    pool.wait_ge(s_ev["hq"], HH)
                for l in range(LEVELS):
                    hs = 1 << l
                    w = TP if l == LEVELS - 1 else T
                    pool.wait_ge(s_X, LEVELS * h + l + 1)
                    xv = X[:, l, 0:w].rearrange("p (n a s) -> p n a s", a=2, s=hs)
                    qv = q[:, h, 0:w].rearrange("p (n a s) -> p n a s", a=2, s=hs)
                    kv = kk[:, h, 0:w].rearrange("p (n a s) -> p n a s", a=2, s=hs)
                    pool.tensor_tensor(xv[:, :, 1, :], xv[:, :, 1, :], qv[:, :, 1, :], ALU.mult).then_inc(s_XM, 1)
                    pool.tensor_tensor(xv[:, :, 0, :], xv[:, :, 0, :], kv[:, :, 0, :], ALU.mult).then_inc(s_XM, 1)
                pool.wait_ge(s_qe, 3 * h + 2)
                pool.tensor_tensor(qe[:], qe[:], q[:, h, :], ALU.mult).then_inc(s_qem, 1)
                pool.tensor_tensor(kd[:], kd[:], kk[:, h, :], ALU.mult).then_inc(s_qem, 1)

            for g in range(12):
                cut(g)
            u = 0
            for gg, what in fills:
                if what[0] != "gate":
                    continue
                if last_of[gg] == what:
                    cut(gg + 2)
                for _ in range(2 if what[1] % 4 else 1):
                    if u < HH * NT and u % NT == 0:
                        times(u // NT)
                    u += 1
            for g in range(20, NG):
                cut(g)
            pool.wait_ge(s_ml, KD)
            group_used(pool, NG - 1)
            pool.memset(zero[:], 0).then_inc(s_zero, 1)
            pool.memset(zcol[:], 0).then_inc(s_zero, 1)
            pool.wait_ge(s_rc, 112)
            pool.wait_ge(s_zd, 16)
            pool.wait_ge(s_dest, 1)
            for i in range(NT):
                for c in range(2):
                    r = ROWS[i]
                    pool.indirect_dma_start(slot_d, bass.IndirectOffsetOnAxis(ap=dest[0:r, c, i:i + 1], axis=0),
                                            tid[0:r, i:i + 1], None).then_inc(s_sct, 16)
            pool.wait_ge(s_x1d, 16 * NT)
            pool.wait_ge(s_stok, 16)
            for e in range(NX):
                j = e % 2
                if e >= 2:
                    pool.wait_ge(m_t, e - 1)
                pool.indirect_dma_start(xg[:, j, :], None, x1_d, bass.IndirectOffsetOnAxis(ap=stok[:, e:e + 1], axis=0)).then_inc(m_g[j], 16)
            over = pool.value_load(flag[0:1, 0:1], min_val=0, max_val=1)
            with pool.If(over > 0):
                pool.wait_ge(m_t, NX)
                pool.wait_ge(s_zero, 2)
                pool.memset(stx[:, 1:2], 0).then_inc(e_i, 1)
                with pool.Fori(0, NX * (BLOCKS - 1)) as n:
                    pool.wait_ge(e_w, 64 * n + 64)
                    pool.tensor_tensor(stx[:, 1:2], stx[:, 0:1], zcol[:], ALU.add).then_inc(e_ix, 1)
                    pool.wait_ge(e_ix, n + 1)
                    pool.sem_inc(e_g2, 1)
                    pool.indirect_dma_start(xg[:, 0, :], None, x1_d, bass.IndirectOffsetOnAxis(ap=stx[:, 1:2], axis=0)).then_inc(e_g, 16)
                    pool.wait_ge(e_yc, n + 1)
                    pool.tensor_tensor(zcol2[:], zcol[:], zcol[:], ALU.add).then_inc(e_i, 1)
            for j in range(2):
                pool.wait_ge(m_ys[j], 16 * NX // 2)

            def gather_results(rows):
                for i in range(NT):
                    r = ROWS[i]
                    if i >= 2:
                        pool.wait_ge(s_ygf, i - 1)
                    for c in range(2):
                        pool.indirect_dma_start(yg[0:r, i % 2, c, :], None, rows,
                                                bass.IndirectOffsetOnAxis(ap=dest[0:r, c, i:i + 1], axis=0)).then_inc(s_yg[i % 2], 16)

            with pool.If(over > 0):
                pool.wait_ge(e_ys, 16 * NX * (BLOCKS - 1))
                gather_results(ys_d)
            with pool.If(over < 1):
                gather_results(ys_d[0:CAP * NX])

        @block.vector
        def _(dve):
            chain = Count(d_chain)

            def link(ins):
                dve.wait_ge(d_chain, chain.by(ins))

            for k in range(KD):
                b = k % 2
                dve.wait_ge(s_xh, k + 1)
                dve.tensor_tensor(xl[:, k, :], ppf[b][:, 0:T], xh[:, k, :].bitcast(F32), ALU.subtract).then_inc(s_xl, 1)
                dve.wait_ge(s_xl, k + 1)
                dve.engine_nop().then_inc(s_free[b], 1)

            def index_sum(n, i):
                r = ROWS[i]
                acc = maskb[0:r, MOFF[i]:MOFF[i] + KEYS[i]]
                for ih in range(IH):
                    s = 4 * n + ih
                    dve.wait_ge(s_rl, s + 1)
                    rl = relu[0:r, s % 2, 0:KEYS[i]]
                    if s >= 1:
                        dve.wait_ge(s_acc, s)
                    if ih == 0:
                        dve.tensor_scalar(acc, rl, tok4[0:r, i, 64:65], None, ALU.mult).then_inc(s_acc, 1)
                    else:
                        dve.scalar_tensor_tensor(acc, rl, tok4[0:r, i, 64 + ih:65 + ih], acc, ALU.mult, ALU.add).then_inc(s_acc, 1)

            def select(n, i):
                r = ROWS[i]
                w = KEYS[i]
                acc = maskb[0:r, MOFF[i]:MOFF[i] + w]
                dve.wait_ge(s_acc, 4 * n + 4)
                if i < 4:
                    link(dve.memset(acc[0:64, w - 64:w], NEG))
                src = acc
                for it in range(TOPK[i] // 8):
                    link(dve.max(top[0:r, :], src))
                    if it < TOPK[i] // 8 - 1:
                        link(dve.match_replace(wk[0:r, 0:w], top[0:r, :], src, NEG))
                        src = wk[0:r, 0:w]
                thr = top[0:r, 7:8]
                g_, e_, c_ = gt[0:r, 0:w], eq[0:r, 0:w], wk[0:r, 0:w]
                link(dve.tensor_scalar(g_, acc, thr, None, ALU.is_gt))
                link(dve.tensor_reduce(cnt[0:r, 0:1], g_, AX.X, ALU.add))
                link(dve.tensor_scalar(cnt[0:r, 1:2], cnt[0:r, 0:1], -1.0, float(TOPK[i]), ALU.mult, ALU.add))
                link(dve.tensor_scalar(e_, acc, thr, None, ALU.is_equal))
                link(dve.tensor_tensor_scan(c_, e_, e_, 0.0, ALU.add, ALU.max))
                link(dve.scalar_tensor_tensor(e_, c_, cnt[0:r, 1:2], e_, ALU.is_le, ALU.mult))
                link(dve.tensor_tensor(g_, g_, e_, ALU.add))
                dve.tensor_scalar(acc, g_, BIG, -BIG, ALU.mult, ALU.add).then_inc(s_mask, 1)
                dve.wait_ge(s_mask, n + 1)

            def decay(h):
                z, l = B[:, h, :], L[:, h, :]
                dve.wait_ge(s_L, h + 1)
                dve.scalar_tensor_tensor(kk[:, h, :], z, 0.0, l, ALU.max, ALU.add).then_inc(s_g, 1)
                dve.wait_ge(s_g, 2 * h + 1)
                link(dve.scalar_tensor_tensor(l, z, 0.0, l, ALU.min, ALU.subtract))
                dve.tensor_tensor_scan(z, reset[:], l, 0.0, ALU.mult, ALU.add).then_inc(s_g, 1)

            def exponents(h):
                dve.wait_ge(s_g, 2 * h + 2)
                if h == 0:
                    dve.wait_ge(s_acc, 16)
                for l in range(LEVELS):
                    hs = 1 << l
                    w = TP if l == LEVELS - 1 else T
                    nb = w // (2 * hs)
                    xv = X[:, l, 0:w].rearrange("p (n a s) -> p n a s", a=2, s=hs)
                    bv = B[:, h, 0:w].rearrange("p (n a s) -> p n a s", a=2, s=hs)
                    mid = bv[:, :, 0, hs - 1:hs].broadcast_to([P, nb, hs])
                    dve.tensor_tensor(xv[:, :, 1, :], bv[:, :, 1, :], mid, ALU.subtract).then_inc(s_D, 1)
                    dve.tensor_tensor(xv[:, :, 0, :], mid, bv[:, :, 0, :], ALU.subtract).then_inc(s_D, 1)

            def chunk_weights(u):
                cw = ROWS[u % NT]
                nl = LEVELS + (1 if u % NT < 4 else 0)
                G = pw[:, 0:2, :].rearrange("p a (b c) -> p (a b) c", c=P)
                dve.wait_ge(s_G, u + 1)
                if u >= 1:
                    dve.wait_ge(s_AT, u)
                dve.tensor_tensor(Gm[0:cw, 0:nl, 0:cw], G[0:cw, 0:nl, 0:cw], pairs[0:cw, 0:nl, 0:cw], ALU.mult).then_inc(s_Gf, 1)
                dve.wait_ge(s_Gf, u + 1)
                if u >= 1:
                    dve.wait_ge(s_o, u)
                dve.tensor_reduce(AT[0:cw, 0:cw], Gm[0:cw, 0:nl, 0:cw].rearrange("p l t -> p t l"), AX.X, ALU.add).then_inc(s_AT, 1)

            def chunk_out(u):
                h, c = u // NT, u % NT
                cs, cw = c * P, ROWS[c]
                group = 0 if c < 4 else 1
                dve.wait_ge(s_o, u + 1)
                link(dve.tensor_copy(o_all[:, h, cs:cs + cw], pw[:, 3, 0:cw]))
                if c == 0:
                    ins = dve.tensor_copy(S[:, 0, h, :], pw[:, 3, 256:384])
                else:
                    dve.wait_ge(s_qe, 3 * h + 3)
                    ins = dve.scalar_tensor_tensor(S[:, group, h, :], S[:, group, h, :], eBT[:, c:c + 1], pw[:, 3, 256:384], ALU.mult, ALU.add)
                ins.then_inc(s_of, 1)
                dve.wait_ge(s_of, u + 1)

            def head_out(h):
                o = o_all[:, h, :]
                dve.wait_ge(s_G, NT * (h + 1))
                dve.tensor_tensor(osq, o, o, ALU.mult).then_inc(s_osq, 1)
                link(dve.scalar_tensor_tensor(o, o, normw[:, 0:1], sg[:, h, :], ALU.mult, ALU.mult))
                dve.wait_ge(s_rms, h + 1)
                dve.tensor_tensor(o, o, rms, ALU.mult).then_inc(s_y, 1)
                dve.wait_ge(s_y, h + 1)

            dve.wait_ge(s_itc, 2)
            for i in range(NT):
                r = ROWS[i]
                link(dve.tensor_scalar(tok4[0:r, i, 64:68], tok4[0:r, i, 64:68], IH ** -0.5, None, ALU.mult))
            index_sum(0, 3)
            index_sum(1, 4)
            index_sum(2, 2)
            index_sum(3, 1)
            dve.wait_ge(s_const, 80)
            for h in range(HH):
                decay(h)
            select(0, 3)
            select(1, 4)
            select(2, 2)
            select(3, 1)
            dve.wait_ge(s_ev["hg"], HH)
            for h in range(HH):
                exponents(h)
                for c in range(NT):
                    chunk_weights(NT * h + c)
                    chunk_out(NT * h + c)
                head_out(h)

            for i in range(NT):
                n = fill_of[("kt", i)]
                b, r = n % 2, ROWS[i]
                dve.wait_ge(s_full[b], n // 2 + 1)
                dve.tensor_copy(ktok[0:r, i, :], ppf[b][0:r, 0:512]).then_inc(s_kt, 1)
                dve.wait_ge(s_kt, i + 1)
                dve.engine_nop().then_inc(s_free[b], 1)

            link(dve.memset(mask0[:], 0.0))
            link(dve.memset(mask0[0:64, 64:128], -BIG))

            def masked(a):
                i = a // AH
                r, w = ROWS[i], KEYS[i]
                m_ = mask0[0:r, :] if i == 0 else maskb[0:r, MOFF[i]:MOFF[i] + w]
                dve.wait_ge(s_lg, a + 1)
                if a >= 2:
                    dve.wait_ge(s_P, a - 1)
                dve.tensor_tensor_reduce(Lm[0:r, a % 2, 0:w], pw[0:r, a % 2, 0:w], m_, 1.0, NEG, ALU.add, ALU.max,
                                         mx[0:r, a % 2, 0:1]).then_inc(s_Lm, 1)
                dve.wait_ge(s_Lm, a + 1)
                dve.tensor_scalar(mx[0:r, a % 2, 1:2], mx[0:r, a % 2, 0:1], -(AD ** -0.5), None, ALU.mult).then_inc(s_nb, 1)

            def tile_out(i):
                r = ROWS[i]
                dve.wait_ge(s_P, AH * (i + 1))
                dve.reciprocal(rden[0:r, :], den[0:r, i % 2, :]).then_inc(s_rd, 1)
                dve.wait_ge(s_rd, i + 1)
                dve.wait_ge(s_O, AH * (i + 1))
                if i >= 2:
                    dve.wait_ge(s_yh, i)
                three = lambda t: t.rearrange("p (h d) -> p h d", h=AH)
                dve.tensor_tensor(three(ao[0:r, i % 2, :]), three(pw[0:r, 3, :]),
                                  rden[0:r, :].unsqueeze(2).broadcast_to([r, AH, AD]), ALU.mult).then_inc(s_ao, 1)
                dve.wait_ge(s_ao, i + 1)

            def tile_low(i):
                n = fill_of[("ao", i)]
                b, r = n % 2, ROWS[i]
                dve.wait_ge(s_yh, i + 2)
                dve.tensor_tensor(yl[:, 4:8, i * P:i * P + r], ppf[b][:, 0:512].rearrange("p (c t) -> p c t", c=4)[:, :, 0:r],
                                  yh[:, 4:8, i * P:i * P + r].bitcast(F32), ALU.subtract).then_inc(s_yl, 1)
                dve.wait_ge(s_yl, i + 2)
                dve.engine_nop().then_inc(s_free[b], 1)

            NA = NT * AH
            dve.wait_ge(s_yh, 1)
            dve.tensor_tensor(yl[:, 0:4, :], o_all[:], yh[:, 0:4, :].bitcast(F32), ALU.subtract).then_inc(s_yl, 1)
            for a in range(NA + 2):
                if a >= 3 and (a - 3) % AH == AH - 1:
                    tile_out((a - 3) // AH)
                if a < NA:
                    masked(a)
                if a >= 5 and (a - 5) % AH == AH - 1:
                    tile_low((a - 5) // AH)
            tile_out(NT - 1)
            tile_low(NT - 1)

            dve.wait_ge(s_sk, 64)
            for c in range(3):
                dve.wait_ge(s_gst[c], 16 * (6 if c == 0 else 5))
            for m in range(KD):
                dve.wait_ge(s_sig, m + 1)
                for w in range(2):
                    n = fill_of[("br", 2 * m + w)]
                    b = n % 2
                    dve.wait_ge(s_full[b], n // 2 + 1)
                    two = lambda t: t.rearrange("p (a b) -> p a b", a=2)
                    dve.tensor_tensor(two(gring[:, w, :]), pp[:, b, :, 0:HT], two(gld[:, m % 2, w, :]), ALU.mult).then_inc(s_br, 1)
                    dve.wait_ge(s_br, 2 * m + w + 1)
                    dve.engine_nop().then_inc(s_free[b], 1)
                dve.tensor_tensor(gring[:, 2, :], gring[:, 0, :], gring[:, 1, :], ALU.add).then_inc(s_m, 1)
                dve.wait_ge(s_mh, m + 1)
                dve.tensor_tensor(ml[:, m, :], gring[:, 2, :], mh[:, m, :].bitcast(F32), ALU.subtract).then_inc(s_ml, 1)
                dve.wait_ge(s_ml, m + 1)

            dve.wait_ge(s_xr, 32)
            link(dve.memset(xr[64:128, 4, :], 0.0))
            for c in range(12):
                n = fill_of[("out", c)]
                b = n % 2
                i, cc = 2 * (c % 3), GW * (c // 3)
                dve.wait_ge(s_full[b], n // 2 + 1)
                if i < 4:
                    xs, src = xr[:, i:i + 2, cc:cc + GW], pp[:, b, :, 0:GW]
                else:
                    xs, src = xr[0:64, 4, cc:cc + GW], pp[0:64, b, 0, 0:GW]
                dve.scalar_tensor_tensor(xs, xs, ALPHA, src, ALU.mult, ALU.add).then_inc(s_res, 1)
                dve.wait_ge(s_res, c + 1)
                dve.engine_nop().then_inc(s_free[b], 1)

            def moments(i, done):
                for half in range(2):
                    link(dve.bn_stats(stats[:, i, half, :], xr[:, i, half * 512:(half + 1) * 512]))
                dve.bn_aggr(mv[:, i, :], stats[:, i]).then_inc(done, 1)
                dve.wait_ge(done, i + 1)

            def normalize(i, row, done, ready):
                dve.wait_ge(ready, i + 1)
                link(dve.reciprocal(rstd[:, i:i + 1], rstd[:, i:i + 1]))
                link(dve.tensor_scalar(xr[:, i, :], xr[:, i, :], mv[:, i, 0:1], rstd[:, i:i + 1], ALU.subtract, ALU.mult))
                link(dve.tensor_tensor(xr[:, i, :], xr[:, i, :], lnr[:, row, :], ALU.mult))
                dve.tensor_tensor(xr[:, i, :], xr[:, i, :], lnr[:, row + 1, :], ALU.add).then_inc(done, 1)

            for i in range(NT):
                moments(i, s_var)
            dve.wait_ge(s_ln, 64)
            for i in range(NT):
                normalize(i, 0, s_x1, s_sd)

            col = lambda n: cols[:, n, :]
            wide = lambda t: t.unsqueeze(2).broadcast_to([P, NT, 4])

            def first_of(oh):
                link(dve.tensor_copy(taken[:], oh[:, :, 0]))
                for c in range(1, 4):
                    link(dve.tensor_tensor(oh[:, :, c], oh[:, :, c], taken[:], ALU.is_gt))
                    if c < 3:
                        link(dve.tensor_tensor(taken[:], taken[:], oh[:, :, c], ALU.max))

            dve.wait_ge(s_rl_, NT)
            link(dve.tensor_tensor(lg[:], pw[:, 0, 0:100].rearrange("p (i c) -> p i c", c=20),
                                   br_[:].unsqueeze(1).broadcast_to([P, NT, 20]), ALU.add))
            link(dve.tensor_reduce(col(0), lg[:, :, 0:4], AX.X, ALU.max))
            dve.tensor_tensor(gx[:], lg[:, :, 0:4], wide(col(0)), ALU.subtract).then_inc(s_gx, 1)
            dve.wait_ge(s_gx, 1)
            link(dve.tensor_scalar(ohg[:], gx[:], 0.0, None, ALU.is_equal))
            first_of(ohg)
            link(dve.tensor_tensor(prod[:], lg[:, :, 4:20].rearrange("p i (g e) -> p i g e", g=4),
                                   ohg[:].unsqueeze(3).broadcast_to([P, NT, 4, 4]), ALU.mult))
            link(dve.tensor_reduce(es[:], prod[:].rearrange("p i g e -> p i e g"), AX.X, ALU.add))
            link(dve.tensor_reduce(col(3), es[:], AX.X, ALU.max))
            dve.tensor_tensor(es[:], es[:], wide(col(3)), ALU.subtract).then_inc(s_gx, 1)
            dve.wait_ge(s_ge, 1)
            link(dve.tensor_reduce(col(1), ge[:], AX.X, ALU.add))
            link(dve.reciprocal(col(2), col(1)))
            dve.wait_ge(s_ge, 2)
            link(dve.tensor_reduce(col(4), ee[:], AX.X, ALU.add))
            link(dve.reciprocal(col(4), col(4)))
            link(dve.tensor_tensor(es[:], ee[:], wide(col(4)), ALU.mult))
            link(dve.tensor_reduce(col(5), es[:], AX.X, ALU.max))
            link(dve.tensor_tensor(oh1[:], es[:], wide(col(5)), ALU.is_equal))
            first_of(oh1)
            link(dve.scalar_tensor_tensor(es[:], oh1[:], -2.0, es[:], ALU.mult, ALU.add))
            link(dve.tensor_reduce(col(6), es[:], AX.X, ALU.max))
            link(dve.tensor_tensor(oh2[:], es[:], wide(col(6)), ALU.is_equal))
            first_of(oh2)
            for m_, oh in ((M1, oh1), (M2, oh2)):
                link(dve.tensor_tensor(m_[:], ohg[:].unsqueeze(3).broadcast_to([P, NT, 4, 4]),
                                       oh[:].unsqueeze(2).broadcast_to([P, NT, 4, 4]), ALU.mult))
                link(dve.memset(m_[64:128, 4], 0.0))
            dve.tensor_tensor(M[:], M1[:].rearrange("p i g e -> p i (g e)"), M2[:].rearrange("p i g e -> p i (g e)"), ALU.add).then_inc(s_M, 1)
            link(dve.tensor_tensor(col(7), col(5), col(6), ALU.add))
            link(dve.reciprocal(col(7), col(7)))
            link(dve.tensor_tensor(col(7), col(7), col(2), ALU.mult))
            link(dve.tensor_tensor(col(8), col(5), col(7), ALU.mult))
            link(dve.tensor_tensor(col(9), col(6), col(7), ALU.mult))
            dve.wait_ge(s_rk, 1)
            link(dve.scalar_tensor_tensor(rank[:], pw[:, 1, 0:NX * NT].rearrange("p (i e) -> p i e", e=NX), float(NX),
                                          eoff[:].unsqueeze(1).broadcast_to([P, NT, NX]), ALU.mult, ALU.add))
            link(dve.tensor_reduce(cols[:, 0, 0:1], pw[:, 1, NX * NT:NX * (NT + 1)], AX.X, ALU.max))
            link(dve.tensor_scalar(flag[:], cols[:, 0, 0:1], float(CAP), None, ALU.is_gt))
            for c, m_ in enumerate((M1, M2)):
                pr = prod[:].rearrange("p i g e -> p i (g e)")
                link(dve.tensor_tensor(pr, m_[:].rearrange("p i g e -> p i (g e)"), rank[:], ALU.mult))
                link(dve.tensor_reduce(destf[:, c, :], pr, AX.X, ALU.add))
            dve.tensor_copy(dest[:], destf[:]).then_inc(s_dest, 1)

            dve.wait_ge(s_x1d, 16 * NT)
            for i in range(NT):
                link(dve.tensor_scalar(xr[:, i, :], xr[:, i, :], ALPHA, None, ALU.mult))

            def expert(n, j, y_prev, ys_prev, gu, si, h_, y_, yc):
                dve.wait_ge(si, n + 1)
                if y_prev is not None:
                    dve.wait_ge(y_, y_prev)
                dve.tensor_tensor(hT[:, j].rearrange("p f t -> p (f t)"), hs[:, j].rearrange("p f t -> p (f t)"),
                                  pw[:, 0, 256:512], ALU.mult).then_inc(h_, 1)
                dve.wait_ge(y_, n + 1)
                if ys_prev is not None:
                    dve.wait_ge(m_ys[j], ys_prev)
                dve.tensor_copy(ysb[:, j, :], ppf[1]).then_inc(yc, 1)

            expert(0, 0, None, None, m_gu, m_si, m_h, m_y, m_yc)
            expert(1, 1, None, None, m_gu, m_si, m_h, m_y, m_yc)
            with dve.Fori(1, NX // 2) as i:
                for j in range(2):
                    expert(2 * i + j, j, 2 * i + (j - 1), 16 * i, m_gu, m_si, m_h, m_y, m_yc)
            over = dve.value_load(flag[0:1, 0:1], min_val=0, max_val=1)
            with dve.If(over > 0):
                dve.wait_ge(m_ys[0], 16 * NX // 2)
                with dve.Fori(0, NX * (BLOCKS - 1)) as n:
                    expert(n, 0, None, None, e_gu, e_si, e_h, e_y, e_yc)

            for i in range(NT):
                r = ROWS[i]
                dve.wait_ge(s_yg[i % 2], 32 * (i // 2 + 1))
                for c in range(2):
                    ins = dve.scalar_tensor_tensor(xr[0:r, i, :], yg[0:r, i % 2, c, :], cols[0:r, 8 + c, i:i + 1], xr[0:r, i, :],
                                                   ALU.mult, ALU.add)
                    if c == 0:
                        link(ins)
                    else:
                        ins.then_inc(s_ygf, 1)
                        dve.wait_ge(s_ygf, i + 1)
                moments(i, s_v2)
                normalize(i, 2, s_out, s_sd2)


def constants():
    import numpy as np
    t = np.arange(P)
    x = t[:, None] ^ t[None, :]
    pairs = np.zeros((P, LEVELS + 1, P), np.float32)
    pairs[:, 0, :] = x == 0
    for l in range(LEVELS):
        pairs[:, l + 1, :] = ((x >> l) == 1) & (t[:, None] < t[None, :])
    reset = np.ones((P, T), np.float32)
    reset[:, ::P] = 0
    small = np.zeros((P, 8), np.float32)
    small[:, 0] = 1e-6
    small[:, 1] = 1e-5
    small[:, 2] = -0.5
    lower = (t[:, None] < t[None, :]).astype(np.float32)
    return {"c_ident": np.eye(P, dtype=np.float32), "c_pairs": pairs, "c_reset": reset,
            "c_lower": lower, "c_small": small,
            "c_eoff": np.tile(np.arange(NX, dtype=np.float32), (P, 1)),
            "c_tid": (np.arange(P, dtype=np.uint32)[:, None] + P * np.arange(NT, dtype=np.uint32)[None, :])}


_INS = ("x_prompt", "x_sample", "cache_k", "cache_v", "cache_idx_k", "state_hgrn", "w_in", "hg_norm_w",
        "w_br_hg", "w_br_att", "w_out", "ln1_g", "ln1_b", "ln2_g", "ln2_b", "w_rg", "b_rg", "w_re", "b_re",
        "w_gate", "w_up", "w_down")
_OUTS = ((1, TP, D), (1, TS, D),
         (1, 1, TP, AH, AD), (1, 1, TP, AH, AD), (1, 1, TP, ID), (1, 1, HH, P, P),
         (1, 1, TS, AH, AD), (1, 1, TS, AH, AD), (1, 1, TS, ID), (1, 1, HH, P, P))


def kernel(**inputs):
    import numpy as _np
    import concourse.bacc as _bacc
    from concourse import mybir as _mybir
    from concourse.bass_utils import run_bass_kernel_spmd as _run

    nc = _bacc.Bacc("TRN2", target_bir_lowering=False, num_devices=1)
    source = {name: _np.ascontiguousarray(inputs[name]) for name in _INS}
    source.update(constants())
    arrays, args = {}, []
    for name, a in source.items():
        arrays[f"in_{name}_dram"] = a
        args.append(nc.dram_tensor(f"in_{name}_dram", a.shape, _mybir.dt.from_np(a.dtype), kind="ExternalInput").ap())
    for i, shape in enumerate(_OUTS):
        args.append(nc.dram_tensor(f"out_{i}_dram", shape, F32, kind="ExternalOutput").ap())
    encoder_layer(nc, *args)
    r = _run(nc, [arrays], core_ids=[0])
    return tuple(r.results[0][f"out_{i}_dram"] for i in range(len(_OUTS)))
```

```python
from contextlib import ExitStack

import concourse.bass as bass
from concourse import mybir

F32 = mybir.dt.float32
F32R = mybir.dt.float32r
I32 = mybir.dt.int32
U32 = mybir.dt.uint32
ALU = mybir.AluOpType
ACT = mybir.ActivationFunctionType
AX = mybir.AxisListType

P = 128
D = 1024
KD = D // P
TP, TS = 512, 64
T = TP + TS
HT = T // 2
NT = 5
ROWS = [128, 128, 128, 128, 64]
HH = 4
AH, AD = 8, 64
IH, ID = 4, 64
PAST = 256
NX, F = 16, 256
CAP = 128
BLOCKS = 5
SLOT = BLOCKS * CAP
TOPK = [0, 128, 128, 128, 80]
KEYS = [128, 256, 384, 512, PAST + TS]
MOFF = [0, 0, 256, 640, 1152]
NEG = -3.0e38
BIG = 1.0e30
ALPHA = 2.0 ** 0.25
GW = 256
RAW = 2
RING = 4
AHEAD = RING - 1

C_HQ, C_HF, C_HI, C_HG, C_AQ, C_AK, C_AV, C_IQ, C_IK, C_GH, C_GA = (
    0, 512, 1024, 1536, 2048, 2560, 3072, 3584, 3840, 3908, 4932)

LEVELS = 7


class Count:

    def __init__(self, sem):
        self.sem, self.n = sem, 0

    def by(self, ins):
        self.n += 1
        ins.then_inc(self.sem, 1)
        return self.n


def plan():
    groups, fills = [], []

    def group(kind, col, width, units):
        g = len(groups)
        groups.append((kind, col, width))
        for what in units:
            fills.append((g, what))

    group("in", C_IQ, 256, [("iq", 0), ("iq", 1)])
    group("in", C_IK, 68, [("ik", 0)])
    for j in range(2):
        group("in", C_HF + GW * j, GW, [("hf", 2 * j), ("hf", 2 * j + 1)])
    for j in range(2):
        group("in", C_HI + GW * j, GW, [("hi", 3 * j + p) for p in range(3)])
    for j in range(2):
        group("in", C_HQ + GW * j, GW, [("hq", 2 * j), ("hq", 2 * j + 1)])
    for j in range(2):
        group("in", C_HG + GW * j, GW, [("hg", 2 * j), ("hg", 2 * j + 1)])
    for j in range(8):
        group("in", C_GH + GW * j, GW, [("gate", 2 * j), ("gate", 2 * j + 1)])
    for j in range(2):
        group("in", C_AK + GW * j, GW, [("ak", 2 * j), ("ak", 2 * j + 1)])
    fills += [(None, ("kt", i)) for i in range(NT)]
    for j in range(2):
        group("in", C_AQ + GW * j, GW, [("aq", 2 * j), ("aq", 2 * j + 1)])
    for j in range(2):
        group("in", C_AV + GW * j, GW, [("av", 3 * j + p) for p in range(3)])
    fills += [(None, ("attention", 0))]
    for j in range(4):
        group("branch", GW * j, GW, [("br", 4 * j + n) for n in range(4)])
    for j in range(4):
        group("out", GW * j, GW, [])
    fills += [(None, ("out", i)) for i in range(NT)]
    return groups, fills


STORED = 16 * (2 * HH + 2)
BATCHES = [(0, 2), (2, 5)]
UNITS = HH * NT


def hgrn_steps(what):
    kind, c = what
    if what == ("gate", 15):
        return [20, 21]
    return {"hq": [0] if c == 3 else [], "hg": [1 + c], "gate": [5 + c]}.get(kind, [])


def normed_head(k):
    return k // NT - 1 if k >= NT + 1 and k % NT == 1 else None


def prepared_head(k):
    return {6: 2, 11: 3}.get(k)


def encoder_layer(nc, x_prompt, x_sample, cache_k, cache_v, cache_idx_k, state_hgrn, w_in, hg_norm_w,
                  w_br_hg, w_br_att, w_out, ln1_g, ln1_b, ln2_g, ln2_b, w_rg, b_rg, w_re, b_re,
                  w_gate, w_up, w_down, c_ident, c_pairs, c_reset, c_lower, c_small, c_eoff, c_tid, c_order,
                  y_prompt, y_sample, nk_p, nv_p, nik_p, ns_p, nk_s, nv_s, nik_s, ns_s):
    groups, fills = plan()
    NG = len(groups)
    fill_of, n = {}, NT
    for _, what in fills:
        if what[0] != "attention":
            fill_of[what] = n
            n += 1
    last_of = {g: what for g, what in fills if g is not None}
    ends_group = lambda g, what: g is not None and last_of[g] == what
    OUT0 = NG - 4

    gates_d = nc.dram_tensor("gates_d", [16, P, T], F32).ap()
    x1_d = nc.dram_tensor("x1_d", [T, D], F32).ap()
    slot_d = nc.dram_tensor("slot_d", [NX * SLOT, 1], U32).ap()
    ys_d = nc.dram_tensor("ys_d", [NX * SLOT, D], F32).ap()

    with ExitStack() as ctx:
        base = nc.sbuf_base + (-nc.sbuf_base) % 64

        class Area:

            def __init__(self, start):
                self.at = start

            def __call__(self, name, shape, dt=F32):
                n = 4
                for s in shape[1:]:
                    n *= s
                t = nc.alloc_sbuf_tensor_at(name, shape, dt, offset=base + self.at)
                self.at += n + (-n) % 64
                return t

        def sem(name):
            return ctx.enter_context(nc.semaphore(name))

        xa = Area(0)
        xh = xa("x_hi", [P, KD, T], F32R)
        xl = xa("x_lo", [P, KD, T], F32R)
        raw = xa("w_raw", [P, RAW, KD, GW])
        wh = xa("w_hi", [P, 2, KD, GW], F32R)
        wl = xa("w_lo", [P, 2, KD, GW], F32R)
        ident = xa("ident", [P, P])
        ones = xa("ones", [P, P])
        small = xa("small", [P, 8])
        normw = xa("normw", [P, 1])
        route_start = xa.at
        pairs = xa("pairs", [P, LEVELS + 1, P])
        reset = xa("reset", [P, T])
        maskb = xa("maskb", [P, 1472])
        tok4 = xa("tok4", [P, NT, 68])
        wk = xa("wk", [P, 512])
        eq = xa("eq", [P, 512])
        top = xa("top", [P, 8])
        cnt = xa("cnt", [P, 2])
        route_end = xa.at
        gring = xa("gring", [P, 2, T])
        o_all = xa("o_all", [P, HH, T])
        S = xa("S", [P, 2, HH, P])
        mixer_end = xa.at
        sbuf_end = nc.sbuf_usable_end - base

        ya = Area(0)
        yh = ya("y_hi", [P, 8, T], F32R)
        yl = ya("y_lo", [P, 8, T], F32R)

        oa = Area(0)
        woh = oa("wo_hi", [P, 2, KD, GW], F32R)
        wol = oa("wo_lo", [P, 2, KD, GW], F32R)

        ha = Area(mixer_end)
        q = ha("q", [P, HH, T])
        kk = ha("kk", [P, HH, T])
        B = ha("B", [P, HH, T])
        L = ha("L", [P, HH, T])
        v = ha("v", [P, NT, 512])
        sg = ha("sg", [P, HH, T])
        kd = [ha("kd", [P, T]), reset]
        Gm = ha("Gm", [P, LEVELS + 1, P])
        AT = ha("AT", [P, 2, P])
        kdT = ha("kdT", [P, 2, P])
        eBT = ha("eBT", [P, 2, NT])
        xoff = ha.at
        X0 = ha("X0", [P, LEVELS, T])
        X1 = ha("X1", [P, LEVELS - HH, T])
        X = [[X0[:, l, :] for l in range(LEVELS)],
             [L[:, l, :] for l in range(HH)] + [X1[:, l, :] for l in range(LEVELS - HH)]]
        assert ha.at <= sbuf_end
        ia = Area(xoff)
        qi = ia("qi", [P, 2, T])
        kiw = ia("kiw", [68, T])
        ki2 = ia("ki2", [P, T])
        kic = ia("kic", [P, 2, 2, ID])
        kicT = ia("kicT", [P, PAST])
        relu = ia("relu", [P, 2, 512])
        xtok_area = Area(mixer_end)
        xtok = xtok_area("xtok", [P, NT, D])

        aa = Area(mixer_end)
        qa = aa("qa", [P, 4, T])
        ka = aa("ka", [P, 4, T])
        va = aa("va", [P, NT, 512])
        kc = aa("kc", [P, 2, 512])
        kcT = aa("kcT", [P, 4, PAST])
        vc = aa("vc", [P, 2, 512])
        Lm = aa("Lm", [P, RING, 512])
        Pr = aa("Pr", [P, RING, 512])
        PT = aa("PT", [P, 2, 4, P])
        ktok = aa("ktok", [P, NT, 512])
        mask0 = aa("mask0", [P, P])
        mx = aa("mx", [P, RING, 4])

        assert aa.at <= sbuf_end - 2 * 2 * T * 4

        ma = Area(mixer_end)
        mh = ma("m_hi", [P, KD, T], F32R)
        ml = ma("m_lo", [P, KD, T], F32R)
        xr = ma("xr", [P, NT, D])
        lnr = ma("lnr", [P, 4, D])
        gsum = ma("gsum", [P, 2, T])
        assert ma.at <= sbuf_end - 2 * 2 * T * 4
        gld = Area(sbuf_end - 2 * 2 * T * 4 - sbuf_end % 64)("gld", [P, 2, 2, T])

        ra = Area(route_start)
        x1T = ra("x1T", [P, 2, KD, P])
        wr = ra("wr", [P, KD, 20])
        br_ = ra("br_", [P, 20])
        lower = ra("lower", [P, P])
        eoff = ra("eoff", [P, NX])
        tid = ra("tid", [P, NT], U32)
        order = ra("order", [P, 4])
        zero = ra("zero", [P, NX * SLOT // P], U32)
        stats = ra("stats", [P, NT, 2, 6])
        mv = ra("mv", [P, NT, 2])
        rstd = ra("rstd", [P, NT])
        halfv = ra("halfv", [P, NT])
        newton = ra("newton", [P, NT])
        lg = ra("lg", [P, NT, 20])
        ge = ra("ge", [P, NT, 4])
        gx = ra("gx", [P, NT, 4])
        ohg = ra("ohg", [P, NT, 4])
        taken = ra("taken", [P, NT])
        prod = ra("prod", [P, NT, 4, 4])
        es = ra("es", [P, NT, 4])
        ee = ra("ee", [P, NT, 4])
        oh1 = ra("oh1", [P, NT, 4])
        oh2 = ra("oh2", [P, NT, 4])
        cols = ra("cols", [P, 10, NT])
        M1 = ra("M1", [P, NT, 4, 4])
        M2 = ra("M2", [P, NT, 4, 4])
        M = ra("M", [P, NT, NX])
        rank = ra("rank", [P, NT, NX])
        destf = ra("destf", [P, 2, NT])
        dest = ra("dest", [P, 2, NT], U32)
        flag = ra("flag", [P, 1], I32)
        stok = ra("stok", [P, NX], U32)
        stx = ra("stx", [P, 2], U32)
        zcol = ra("zcol", [P, 1], U32)
        zcol2 = ra("zcol2", [P, 1], U32)
        assert ra.at <= route_end, (ra.at, route_end)
        ea = Area(0)
        xg = ea("xg", [P, 2, D])
        xgT = ea("xgT", [P, 2, KD, P])
        hs = ea("hs", [P, 2, 2, CAP])
        hT = ea("hT", [P, 2, 2, CAP])
        ysb = ea("ysb", [P, 2, D])
        yg = Area(0)("yg", [P, 2, 2, D])
        wgu, wd = [], []
        for n, at in enumerate((ea.at, ea.at + 24576, route_end, route_end + 24576)):
            wa = Area(at)
            wgu.append(wa(f"wgu{n}", [P, 2, KD, F]))
            wd.append(wa(f"wd{n}", [P, 2, D]))
        assert wa.at <= mixer_end + 2 * KD * T * 4

        pp = ctx.enter_context(nc.psum_tensor("pp", [P, 2, 2, 512], F32))
        pw = ctx.enter_context(nc.psum_tensor("pw", [P, 4, 512], F32))
        ppf = [pp[:, b].rearrange("p a b -> p (a b)") for b in range(2)]

        w_hi = lambda g: wh[:, g % 2] if g < OUT0 + 2 else woh[:, g - OUT0 - 2]
        w_lo = lambda g: wl[:, g % 2] if g < OUT0 + 2 else wol[:, g - OUT0 - 2]
        logit_bank = lambda a: pp[:, a % 2, a // 2 % 2]

        s_x = [sem(f"s_xin{i}") for i in range(NT)]
        s_const = sem("s_const")
        s_raw = [sem(f"s_raw{i}") for i in range(RAW)]
        s_wh = sem("s_wh")
        s_wl = sem("s_wl")
        s_wlo = sem("s_wlo")
        s_lgd = sem("s_lgd")
        s_full = [sem(f"s_full{b}") for b in range(2)]
        s_free = [sem(f"s_free{b}") for b in range(2)]
        s_xh = sem("s_xh")
        s_xl = sem("s_xl")
        s_ones = sem("s_ones")
        d_chain, a_chain, p_chain = sem("d_chain"), sem("a_chain"), sem("p_chain")
        s_ev = {k: sem("s_ev_" + k) for k in ("iq", "ik", "hf", "hq", "hi", "hg", "gate", "ak", "aq", "av", "br", "out")}
        s_kic = sem("s_kic")
        s_ki2 = sem("s_ki2")
        s_it = sem("s_it")
        s_itc = sem("s_itc")
        s_sc = sem("s_sc")
        s_rl = sem("s_rl")
        s_acc = sem("s_acc")
        s_mask = sem("s_mask")
        s_L = sem("s_L")
        s_g = sem("s_g")
        s_k = sem("s_k")
        s_D = sem("s_D")
        s_X = sem("s_X")
        s_XM = sem("s_XM")
        s_kd = sem("s_kd")
        s_eB = sem("s_eB")
        s_qe = sem("s_qe")
        s_qem = sem("s_qem")
        s_G = sem("s_G")
        s_Gf = sem("s_Gf")
        s_AT = sem("s_AT")
        s_kdt = sem("s_kdt")
        s_ktc = sem("s_ktc")
        s_o = sem("s_o")
        s_of = sem("s_of")
        s_osq = sem("s_osq")
        s_ms = sem("s_ms")
        s_msc = sem("s_msc")
        s_rms = sem("s_rms")
        s_y = sem("s_y")
        s_st = sem("s_st")
        s_gst = [sem(f"s_gst{i}") for i in range(2)]
        s_store = sem("s_store")
        s_kt = sem("s_kt_done")
        s_kc = sem("s_kc")
        s_vc = sem("s_vc")
        s_sk = sem("s_sk")
        s_ct = sem("s_ct")
        s_ctc = sem("s_ctc")
        s_lg = sem("s_lg")
        s_Lm = sem("s_Lm")
        s_P = sem("s_P")
        s_PT = sem("s_PT")
        s_PTc = sem("s_PTc")
        s_O = sem("s_O")
        s_rd = sem("s_rd")
        s_Pn = sem("s_Pn")
        s_ygh, s_ygl = sem("s_ygh"), sem("s_ygl")
        s_yh = sem("s_yh")
        s_yl = sem("s_yl")
        s_gl = [sem("s_gl0"), sem("s_gl1")]
        s_sig = sem("s_sig")
        s_br = sem("s_br")
        s_m = sem("s_m")
        s_mh = sem("s_mh")
        s_ml = sem("s_ml")
        s_xr = sem("s_xr")
        s_ln = sem("s_ln")
        s_pad = sem("s_pad")
        s_res = sem("s_res")
        s_var = sem("s_var")
        s_sd = sem("s_sd")
        s_x1 = sem("s_x1")
        s_x1d = sem("s_x1d")
        s_rc = sem("s_rc")
        s_zero = sem("s_zero")
        s_zd = sem("s_zd")
        s_tx = sem("s_tx")
        s_txc = sem("s_txc")
        s_rl_ = sem("s_rl_")
        s_ge = sem("s_ge")
        s_gx = sem("s_gx")
        s_M = sem("s_M")
        s_rk = sem("s_rk")
        s_dest = sem("s_dest")
        s_sct = sem("s_sct")
        s_stok = sem("s_stok")
        m_w = [sem(f"m_w{i}") for i in range(4)]
        m_wd = [sem(f"m_wd{i}") for i in range(4)]
        m_g = [sem(f"m_g{i}") for i in range(2)]
        m_t, m_tc, m_gu, m_si, m_h, m_y, m_yc = (sem(n) for n in ("m_t", "m_tc", "m_gu", "m_si", "m_h", "m_y", "m_yc"))
        m_ys = [sem(f"m_ys{i}") for i in range(2)]
        e_g2 = sem("e_g2")
        e_next = sem("e_next")
        e_i, e_w, e_ix, e_g = sem("e_i"), sem("e_w"), sem("e_ix"), sem("e_g")
        e_t, e_tc, e_gu, e_si, e_h, e_y, e_yc, e_ys = (sem(n) for n in ("e_t", "e_tc", "e_gu", "e_si", "e_h", "e_y", "e_yc", "e_ys"))
        s_yg = [sem(f"s_yg{i}") for i in range(2)]
        s_ygf = sem("s_ygf")
        s_xa = sem("s_xa")
        s_v2 = sem("s_v2")
        s_sd2 = sem("s_sd2")
        s_out = sem("s_out")

        ys_v = ys_d.rearrange("(b s e) d -> e b s d", e=NX, b=BLOCKS)
        slot_v = slot_d.rearrange("(b s e) a -> e b s a", e=NX, b=BLOCKS)
        w_gate_e = w_gate[0].rearrange("g e (k p) f -> (g e) p k f", p=P)
        w_up_e = w_up[0].rearrange("g e (k p) f -> (g e) p k f", p=P)
        w_down_e = w_down[0].rearrange("g e (k p) d -> (g e) p k d", p=P)

        def dram_w(kind, col, width, slot):
            if kind == "in":
                return [(raw[:, slot, :, 0:width], w_in[0].rearrange("(k p) c -> p k c", p=P)[:, :, col:col + width])]
            if kind == "branch":
                return [(raw[:, slot, 0:4, 0:width], w_br_hg[0].rearrange("(k p) c -> p k c", p=P)[:, :, col:col + width]),
                        (raw[:, slot, 4:8, 0:width], w_br_att[0].rearrange("(k p) c -> p k c", p=P)[:, :, col:col + width])]
            return [(raw[:, slot, :, 0:width], w_out[0].rearrange("(k p) c -> p k c", p=P)[:, :, col:col + width])]

        raw_need = []
        sums = [0] * RAW
        for g, (kind, _, _) in enumerate(groups):
            sums[g % RAW] += 32 if kind == "branch" else 16
            raw_need.append(sums[g % RAW])

        def filled(engine, what):
            n = fill_of[what]
            engine.wait_ge(s_full[n % 2], n // 2 + 1)

        def group_used(engine, g):
            filled(engine, last_of[g])

        block = ctx.enter_context(nc.Block())

        @block.sync
        def _(sp):
            xp = x_prompt[0].rearrange("(i p) d -> i p d", p=P)
            sp.dma_start(ident[:], c_ident).then_inc(s_const, 16)
            for i in range(4):
                sp.dma_start(xtok[:, i, :], xp[i]).then_inc(s_x[i], 16)
            sp.dma_start(xtok[0:64, 4, :], x_sample[0]).then_inc(s_x[4], 16)

            def load_group(g):
                if g >= RAW:
                    sp.wait_ge(s_wh, g - RAW + 1)
                    sp.wait_ge(s_wl, g - RAW + 1)
                for dst, src in dram_w(*groups[g], g % RAW):
                    sp.dma_start(dst, src).then_inc(s_raw[g % RAW], 16)

            def load_gates(m):
                sp.dma_start(gld[:, m % 2], gates_d[m:m + 9:8].rearrange("a p t -> p a t")).then_inc(s_gl[m % 2], 16)

            for g in range(2):
                load_group(g)
            sp.wait_ge(s_xl, NT)
            for dup in range(2):
                sp.dma_start(kic[:, :, dup, :], cache_idx_k[0, 0].rearrange("(j p) d -> p j d", p=P)).then_inc(s_kic, 16)
            sp.dma_start(pairs[:], c_pairs).then_inc(s_const, 16)
            sp.dma_start(reset[:], c_reset).then_inc(s_const, 16)
            sp.dma_start(small[:], c_small).then_inc(s_const, 16)
            sp.dma_start(normw[:], hg_norm_w.rearrange("a d -> d a")).then_inc(s_const, 16)
            load_group(2)
            for g in range(3, NG):
                load_group(g)
                if g == 3:
                    sp.wait_ge(s_ev["ik"], 1)
                    sp.dma_start(ki2[64:128, :], kiw[0:64, :]).then_inc(s_ki2, 16)
                    for h in range(HH):
                        sp.dma_start(S[:, 1, h, :], state_hgrn[0, 0, h]).then_inc(s_st, 16)
                if g == 21:
                    sp.wait_ge(s_y, 1)
                    sp.dma_start(kc[:], cache_k[0, 0].rearrange("(j p) h d -> p j (h d)", p=P)).then_inc(s_kc, 16)
                    sp.dma_start(vc[:], cache_v[0, 0].rearrange("(j p) h d -> p j (h d)", p=P)).then_inc(s_vc, 16)
                    for c in range(2):
                        sp.wait_ge(s_gst[c], 16 * 8)
                    load_gates(0)
                    load_gates(1)
                if g == 22:
                    sp.wait_ge(s_of, UNITS)
                    for h in range(HH):
                        sp.dma_start(ns_p[0, 0, h], S[:, 0, h, :]).then_inc(s_store, 16)
                        sp.dma_start(ns_s[0, 0, h], S[:, 1, h, :]).then_inc(s_store, 16)
                    sp.dma_start(nik_p[0, 0].rearrange("(i p) c -> p i c", p=P), tok4[:, 0:4, 0:64]).then_inc(s_store, 16)
                    sp.dma_start(nik_s[0, 0], tok4[0:64, 4, 0:64]).then_inc(s_store, 16)
                if g == 24:
                    sp.wait_ge(s_kt, NT)
                    sp.dma_start(nk_p[0, 0].rearrange("(i p) h d -> p i (h d)", p=P), ktok[:, 0:4, :]).then_inc(s_sk, 16)
                    sp.dma_start(nk_s[0, 0].rearrange("s h d -> s (h d)"), ktok[0:64, 4, :]).then_inc(s_sk, 16)
                    sp.wait_ge(s_ev["av"], 6)
                    sp.dma_start(nv_p[0, 0].rearrange("(i p) h d -> p i (h d)", p=P), va[:, 0:4, :]).then_inc(s_sk, 16)
                    sp.dma_start(nv_s[0, 0].rearrange("s h d -> s (h d)"), va[0:64, 4, :]).then_inc(s_sk, 16)
                if g == 27:
                    sp.wait_ge(s_yl, NT)
                    sp.wait_ge(s_sk, 64)
                    sp.dma_start(xr[:, 0:4, :], x_prompt[0].rearrange("(i p) d -> p i d", p=P)).then_inc(s_xr, 16)
                    sp.dma_start(xr[0:64, 4, :], x_sample[0]).then_inc(s_xr, 16)
                    for n, row in enumerate((ln1_g, ln1_b, ln2_g, ln2_b)):
                        sp.dma_start(lnr[:, n, :], row.broadcast_to([P, D])).then_inc(s_ln, 16)

            sp.wait_ge(s_store, STORED)
            for dst, src in ((wr[:, :, 0:4], w_rg[0].rearrange("(k p) c -> p k c", p=P)),
                             (wr[:, :, 4:20], w_re[0].rearrange("(k p) c -> p k c", p=P)),
                             (br_[:, 0:4], b_rg.broadcast_to([P, 4])), (br_[:, 4:20], b_re.broadcast_to([P, 16])),
                             (lower[:], c_lower), (eoff[:], c_eoff), (tid[:], c_tid), (order[:], c_order)):
                sp.dma_start(dst, src).then_inc(s_rc, 16)
            sp.wait_ge(s_zero, 1)
            sp.dma_start(slot_d.rearrange("(p n) a -> p (n a)", p=P), zero[:]).then_inc(s_zd, 16)

            def expert_gate_up(e, j):
                sp.dma_start(wgu[j][:, 0], w_gate_e[e]).then_inc(m_w[j], 16)
                sp.dma_start(wgu[j][:, 1], w_up_e[e]).then_inc(m_w[j], 16)

            def expert_down(e, j):
                sp.dma_start(wd[j][:], w_down_e[e]).then_inc(m_wd[j], 16)

            def store_x1(i):
                sp.wait_ge(s_x1, i + 1)
                sp.dma_start(x1_d[i * P:i * P + ROWS[i]], xr[0:ROWS[i], i, :]).then_inc(s_x1d, 16)

            for i in range(NT - 1):
                store_x1(i)
            filled(sp, ("out", NT - 1))
            expert_gate_up(0, 0)
            expert_down(0, 0)
            store_x1(NT - 1)
            for j in (1, 2, 3):
                expert_gate_up(j, j)
                expert_down(j, j)
            sp.wait_ge(s_sct, 16 * 2 * NT)
            sp.dma_start(stok[:], slot_d[0:CAP * NX].rearrange("(s e) a -> s (e a)", e=NX)).then_inc(s_stok, 16)

            def store_y(e, j):
                sp.dma_start(ys_v[e, 0], ysb[:, j, :]).then_inc(m_ys[j], 16)

            with sp.Fori(1, NX // 4) as i:
                for j in range(4):
                    sp.wait_ge(m_gu, 4 * i + (j - 3))
                    expert_gate_up(4 * i + j, j)
                    sp.wait_ge(m_y, 4 * i + (j - 3))
                    expert_down(4 * i + j, j)
                    sp.wait_ge(m_yc, 4 * i + (j - 3))
                    store_y(4 * i + (j - 4), j % 2)
            for e in range(NX - 4, NX):
                sp.wait_ge(m_yc, e + 1)
                store_y(e, e % 2)
            sp.wait_ge(s_dest, len(BATCHES))
            over = sp.value_load(flag[0:1, 0:1], min_val=0, max_val=1)
            with sp.If(over > 0):
                sp.wait_ge(m_y, NX)
                sp.wait_ge(m_ys[0], 16 * NX // 2)
                sp.wait_ge(m_ys[1], 16 * NX // 2)
                with sp.Fori(0, NX) as e:
                    for k in range(1, BLOCKS):
                        n = (BLOCKS - 1) * e + k
                        sp.wait_ge(e_i, n)
                        sp.dma_start(wgu[0][:, 0], w_gate_e[e]).then_inc(e_w, 16)
                        sp.dma_start(wgu[0][:, 1], w_up_e[e]).then_inc(e_w, 16)
                        sp.dma_start(wd[0][:], w_down_e[e]).then_inc(e_w, 16)
                        sp.dma_start(stx[:, 0:1], slot_v[e, k], allow_slow_non_contiguous=True).then_inc(e_w, 16)
                        sp.wait_ge(e_yc, n)
                        sp.dma_start(ys_v[e, k], ysb[:, 0, :]).then_inc(e_ys, 16)
                        sp.wait_ge(e_ys, 16 * n)
                        sp.sem_inc(e_next, 1)
            for i in range(NT):
                sp.wait_ge(s_out, i + 1)
                dst = y_prompt[0, i * P:(i + 1) * P] if i < 4 else y_sample[0]
                sp.dma_start(dst, xr[0:ROWS[i], i, :]).then_inc(s_store, 16)
            sp.wait_ge(s_store, STORED + 16 * NT)
            sp.wait_ge(s_sk, 16 * 4)

        @block.tensor
        def _(pe):
            pe.wait_ge(s_const, 16)

            def open_fill(n):
                b = n % 2
                if n >= 2:
                    pe.wait_ge(s_free[b], n // 2)
                return b

            def transpose_x(i):
                b = open_fill(i)
                pe.wait_ge(s_x[i], 16)
                r = ROWS[i]
                for k in range(KD):
                    mm = pe.transpose(ppf[b][:, k * P:k * P + r], xtok[0:r, i, k * P:(k + 1) * P], ident[0:r, 0:r])
                mm.then_inc(s_full[b], 1)

            def columns(lhs_h, lhs_l, rhs_h, rhs_l, ks, b):
                for x, k in enumerate(ks):
                    for y, (lw, rx) in enumerate(((lhs_h, rhs_h), (lhs_h, rhs_l), (lhs_l, rhs_h))):
                        for half in range(2):
                            mm = pe.matmul(pp[0:lw(k).shape[1], b, half, 0:HT], lw(k), rx(k, half),
                                           start=(x == 0 and y == 0), stop=(x == len(ks) - 1 and y == 2))
                return mm

            def fill(n, g, what):
                kind, c = what
                slot = g % 2
                b = open_fill(n)
                if kind in ("iq", "ik", "hf", "hq", "hg", "gate", "ak", "aq"):
                    lo = 0 if kind == "ik" else P * (c % 2)
                    hi = lo + (68 if kind == "ik" else P)
                    mm = columns(lambda k: wh[:, slot, k, lo:hi], lambda k: wl[:, slot, k, lo:hi],
                                 lambda k, h: xh[:, k, h * HT:(h + 1) * HT],
                                 lambda k, h: xl[:, k, h * HT:(h + 1) * HT], range(KD), b)
                elif kind == "br":
                    lo = P * (c // 2 % 2)
                    k0 = 4 * (c % 2)
                    if c == 0:
                        pe.wait_ge(s_Lm, NT * AH)
                        pe.wait_ge(s_ygh, 1)
                        pe.wait_ge(s_ygl, 1)
                        pe.wait_ge(s_yh, NT)
                        pe.wait_ge(s_yl, NT)
                    mm = columns(lambda k: wh[:, slot, k, lo:lo + P], lambda k: wl[:, slot, k, lo:lo + P],
                                 lambda k, h: yh[:, k, h * HT:(h + 1) * HT],
                                 lambda k, h: yl[:, k, h * HT:(h + 1) * HT], range(k0, k0 + 4), b)
                elif kind in ("hi", "av"):
                    for i in range(2 * (c % 3), min(2 * (c % 3) + 2, NT)):
                        r = ROWS[i]
                        for k in range(KD):
                            for y, (lx, rw) in enumerate(((xh, wh), (xl, wh), (xh, wl))):
                                mm = pe.matmul(pp[0:r, b, i % 2, 0:GW], lx[:, k, i * P:i * P + r], rw[:, slot, k, :],
                                               start=(k == 0 and y == 0), stop=(k == KD - 1 and y == 2))
                mm.then_inc(s_full[b], 1)
                return mm

            def index_transposes():
                pe.wait_ge(s_kic, 32)
                for j in range(2):
                    mm = pe.transpose(pw[:, 2, j * P:(j + 1) * P], kic[:, j].rearrange("p a b -> p (a b)"), ident[:])
                mm.then_inc(s_it, 1)
                pe.wait_ge(s_ev["ik"], 1)
                for i in range(NT):
                    r = ROWS[i]
                    mm = pe.transpose(pw[0:r, 3, i * 68:(i + 1) * 68], kiw[:, i * P:i * P + r], ident[0:68, 0:68])
                mm.then_inc(s_it, 1)

            def index_scores(n, i):
                for ih in range(IH):
                    s = 4 * n + ih
                    if s >= 2:
                        pe.wait_ge(s_rl, s - 1)
                    lo = 64 * (ih % 2)
                    r = ROWS[i]
                    ql = qi[lo:lo + 64, ih // 2, i * P:i * P + r]
                    kt = ki2 if ih % 2 else kiw
                    if ih % 2:
                        pe.wait_ge(s_ki2, 16)
                    out = pw[0:r, s % 2, :]
                    if i < 4:
                        mm = pe.matmul(out[:, 0:KEYS[i]], ql, kt[lo:lo + 64, 0:KEYS[i]], start=True, stop=True)
                    else:
                        pe.matmul(out[:, 0:PAST], ql, kicT[lo:lo + 64, :], start=True, stop=True)
                        mm = pe.matmul(out[:, PAST:PAST + TS], ql, kt[lo:lo + 64, TP:T], start=True, stop=True)
                    mm.then_inc(s_sc, 1)

            def hgrn_pairs(u):
                h, c = u // NT, u % NT
                cs, cw = c * P, ROWS[c]
                nl = LEVELS if c < 4 else LEVELS - 1
                if u == 0:
                    pe.wait_ge(s_rl, 16)
                    pe.wait_ge(s_itc, 2)
                else:
                    pe.wait_ge(s_Gf, u)
                if c == 0:
                    pe.wait_ge(s_XM, 14 * h + 14)
                    pe.wait_ge(s_qem, 2 * h + 2)
                if c == 1 and h >= 1:
                    pe.wait_ge(s_msc, h)
                G = pw[:, 0:2, :].rearrange("p a (b c) -> p (a b) c", c=P)
                pe.matmul(G[0:cw, 0, 0:cw], kk[:, h, cs:cs + cw], q[:, h, cs:cs + cw], start=True, stop=True)
                for l in range(nl):
                    xx = X[h % 2][l][:, cs:cs + cw]
                    mm = pe.matmul(G[0:cw, l + 1, 0:cw], xx, xx, start=True, stop=True)
                mm.then_inc(s_G, 1)
                if u >= 1:
                    pe.wait_ge(s_ktc, u)
                pe.transpose(pw[0:cw, 2, 0:P], kd[h % 2][:, cs:cs + cw], ident[:]).then_inc(s_kdt, 1)

            def hgrn_out(u):
                h, c = u // NT, u % NT
                cs, cw = c * P, ROWS[c]
                pe.wait_ge(s_AT, u + 1)
                if u >= 1:
                    pe.wait_ge(s_of, u)
                if c == 4:
                    pe.wait_ge(s_st, 64)
                vv = v[0:cw, c, h * P:(h + 1) * P]
                group = 0 if c < 4 else 1
                pe.matmul(pw[:, 3, 0:cw], vv, AT[0:cw, u % 2, 0:cw], start=True, stop=(c == 0))
                if c > 0:
                    pe.matmul(pw[:, 3, 0:cw], S[:, group, h, :], B[:, h, cs:cs + cw], start=False, stop=True)
                pe.wait_ge(s_ktc, u + 1)
                pe.matmul(pw[:, 3, 256:384], kdT[0:cw, u % 2, :], vv, start=True, stop=True).then_inc(s_o, 1)

            def hgrn_square(h):
                pe.wait_ge(s_osq, h + 1)
                pe.wait_ge(s_Gf, min(NT * (h + 1) + 1, UNITS))
                for half in range(2):
                    mm = pe.matmul(pw[:, half, 0:HT], ones[:], X[h % 2][1][:, half * HT:(half + 1) * HT], start=True, stop=True)
                mm.then_inc(s_ms, 1)

            def hgrn_step(k):
                if normed_head(k) is not None:
                    hgrn_square(normed_head(k))
                if 1 <= k <= UNITS:
                    hgrn_out(k - 1)
                if k < UNITS:
                    hgrn_pairs(k)

            for i in range(NT):
                transpose_x(i)
            def key_rows(i):
                n = fill_of[("kt", i)]
                b = open_fill(n)
                pe.wait_ge(s_ev["ak"], 4)
                r = ROWS[i]
                for c in range(4):
                    mm = pe.transpose(ppf[b][0:r, c * P:(c + 1) * P], ka[:, c, i * P:i * P + r], ident[:])
                mm.then_inc(s_full[b], 1)

            def cache_keys():
                for j in range(2):
                    pe.wait_ge(s_kc, 16)
                    pe.wait_ge(s_msc, HH)
                    for c in range(4):
                        mm = pe.transpose(pw[:, j, c * P:(c + 1) * P], kc[:, j, c * P:(c + 1) * P], ident[:])
                    mm.then_inc(s_ct, 1)

            def logits(a):
                i, h = a // AH, a % AH
                r, lo, w = ROWS[i], 64 * (h % 2), KEYS[i]
                if a == 0:
                    pe.wait_ge(s_ctc, 2)
                    pe.wait_ge(s_ev["aq"], 4)
                if a < RING:
                    n = fill_of[("br", 0)]
                    n += (a - n) % 2
                    pe.wait_ge(s_free[n % 2], n // 2)
                else:
                    pe.wait_ge(s_Lm, a - RING + 1)
                ql = qa[lo:lo + 64, h // 2, i * P:i * P + r]
                out = logit_bank(a)[0:r]
                if i < 4:
                    mm = pe.matmul(out[:, 0:w], ql, ka[lo:lo + 64, h // 2, 0:w], start=True, stop=True)
                else:
                    pe.matmul(out[:, 0:PAST], ql, kcT[lo:lo + 64, h // 2, :], start=True, stop=True)
                    mm = pe.matmul(out[:, PAST:w], ql, ka[lo:lo + 64, h // 2, TP:T], start=True, stop=True)
                mm.then_inc(s_lg, 1)

            def key_parts(i):
                return [(j * P, min(P, KEYS[i] - j * P)) for j in range((KEYS[i] + P - 1) // P)]

            def turn(a):
                i = a // AH
                r = ROWS[i]
                pe.wait_ge(s_Pn, a + 1)
                if a >= 2:
                    pe.wait_ge(s_PTc, a - 1)
                for j, (at, w) in enumerate(key_parts(i)):
                    mm = pe.transpose(pw[0:w, a % 2, j * P:j * P + r], Pr[0:r, a % RING, at:at + w], ident[0:r, 0:r])
                mm.then_inc(s_PT, 1)

            def values(a):
                i, h = a // AH, a % AH
                r, lo = ROWS[i], AD * (h % 2)
                pe.wait_ge(s_PTc, a + 1)
                if a == 0:
                    pe.wait_ge(s_vc, 16)
                    pe.wait_ge(s_ev["av"], 6)
                if h == 0 and i >= 2:
                    pe.wait_ge(s_yl, i - 1)
                parts = key_parts(i)
                for j, (at, w) in enumerate(parts):
                    vv = va[0:w, j if i < 4 else 4, h * AD:(h + 1) * AD] if i < 4 or j == 2 else vc[:, j, h * AD:(h + 1) * AD]
                    mm = pe.matmul(pw[lo:lo + AD, 2 + i % 2, h // 2 * P:h // 2 * P + r], vv, PT[0:w, a % 2, j, 0:r],
                                   start=(j == 0), stop=(j == len(parts) - 1))
                mm.then_inc(s_O, 1)

            def attention():
                NA = NT * AH
                for a in range(NA + AHEAD + 1):
                    if a < NA:
                        logits(a)
                    if 0 <= a - AHEAD < NA:
                        turn(a - AHEAD)
                    if a - AHEAD - 1 >= 0:
                        values(a - AHEAD - 1)

            def out_tile(i):
                b = open_fill(fill_of[("out", i)])
                r = ROWS[i]
                if i == 0:
                    pe.wait_ge(s_mh, KD)
                    pe.wait_ge(s_ml, KD)
                for j in range(4):
                    if i == 0:
                        weights_ready(OUT0 + j)
                    for k in range(KD):
                        for y, (lx, rw) in enumerate(((mh, w_hi), (ml, w_hi), (mh, w_lo))):
                            mm = pe.matmul(pp[0:r, b, j // 2, GW * (j % 2):GW * (j % 2 + 1)], lx[:, k, i * P:i * P + r],
                                           rw(OUT0 + j)[:, k, :], start=(k == 0 and y == 0), stop=(k == KD - 1 and y == 2))
                mm.then_inc(s_full[b], 1)

            def router(i):
                pe.wait_ge(s_x1, i + 1)
                if i == 0:
                    pe.wait_ge(s_rc, 128)
                    pe.wait_ge(s_yl, NT)
                else:
                    pe.wait_ge(s_txc, i)
                for k in range(KD):
                    mm = pe.transpose(pw[:, k // 4, k % 4 * P:(k % 4 + 1) * P], xr[:, i, k * P:(k + 1) * P], ident[:])
                mm.then_inc(s_tx, 1)
                pe.wait_ge(s_txc, i + 1)
                for b, (first, _) in enumerate(BATCHES):
                    if b and i == first:
                        pe.wait_ge(s_lgd, b)
                for k in range(KD):
                    mm = pe.matmul(pw[:, 2, 20 * i:20 * i + 20], x1T[:, i % 2, k, :], wr[:, k, :], start=(k == 0), stop=(k == KD - 1))
                mm.then_inc(s_rl_, 1)

            def ranks(b):
                first, end = BATCHES[b]
                pe.wait_ge(s_M, b + 1)
                if b:
                    pe.wait_ge(s_dest, b)
                for i in range(first, end):
                    for j in range(i + 1):
                        mm = pe.matmul(pw[:, 3, NX * i:NX * (i + 1)], lower[:] if j == i else ones[:], M[:, j, :],
                                       start=(j == 0), stop=(j == i))
                if end == NT:
                    for j in range(NT):
                        mm = pe.matmul(pw[:, 3, NX * NT:NX * (NT + 1)], ones[:], M[:, j, :], start=(j == 0), stop=(j == NT - 1))
                mm.then_inc(s_rk, 1)

            def weights_ready(g):
                pe.wait_ge(s_wh, g + 1)
                if g < OUT0 + 2:
                    pe.wait_ge(s_wl, g + 1)
                else:
                    pe.wait_ge(s_wlo, g - OUT0 - 1)

            for n, (g, what) in enumerate(fills):
                if what[0] == "out":
                    break
                if what[0] == "kt":
                    key_rows(what[1])
                    if what[1] == NT - 1:
                        cache_keys()
                    continue
                if what[0] == "attention":
                    attention()
                    continue
                if n == 0 or fills[n - 1][0] != g:
                    weights_ready(g)
                    if g == 0:
                        pe.wait_ge(s_xh, NT)
                        pe.wait_ge(s_xl, NT)
                fill(fill_of[what], g, what)
                if what == ("hf", 0):
                    index_transposes()
                if what == ("hf", 1):
                    pe.wait_ge(s_itc, 2)
                    pe.wait_ge(s_ev["iq"], 2)
                    index_scores(0, 3)
                    index_scores(1, 4)
                if what == ("hf", 3):
                    index_scores(2, 2)
                    index_scores(3, 1)
                for k in hgrn_steps(what):
                    hgrn_step(k)

            for i in range(NT):
                out_tile(i)
                if i >= 1:
                    router(i - 1)
                if i == BATCHES[0][1] + 1:
                    ranks(0)
            router(NT - 1)
            ranks(1)

            def gate_up(out, w, xT):
                for half in range(2):
                    for f in range(2):
                        for k in range(KD):
                            mm = pe.matmul(out[:, (2 * half + f) * P:(2 * half + f + 1) * P], w[:, half, k, f * P:(f + 1) * P],
                                           xT[:, k, :], start=(k == 0), stop=(k == KD - 1))
                return mm

            def down(h_, w):
                for half in range(2):
                    for f in range(2):
                        mm = pe.matmul(ppf[1][:, half * 512:(half + 1) * 512], h_[:, f, :], w[:, f, half * 512:(half + 1) * 512],
                                       start=(f == 0), stop=(f == 1))
                return mm

            def expert(i, j, e):
                later = not isinstance(i, int)
                pe.wait_ge(m_g[j % 2], 32 * i + 16 * (j // 2 + 1))
                if later or j >= 1:
                    pe.wait_ge(m_tc, e)
                for k in range(KD):
                    mm = pe.transpose(ppf[0][:, k * P:(k + 1) * P], xg[:, j % 2, k * P:(k + 1) * P], ident[:])
                mm.then_inc(m_t, 1)
                if later or j >= 1:
                    pe.wait_ge(m_h, e)
                    pe.wait_ge(m_wd[(j - 1) % 4], 16 * i + (16 if j else 0))
                    if later or j >= 2:
                        pe.wait_ge(m_yc, 4 * i + (j - 1))
                    down(hT[:, (j - 1) % 2], wd[(j - 1) % 4]).then_inc(m_y, 1)
                pe.wait_ge(m_w[j], 32 * i + 32)
                pe.wait_ge(m_tc, 4 * i + (j + 1))
                gate_up(pw[:, j % 2], wgu[j], xgT[:, j % 2]).then_inc(m_gu, 1)

            for j in range(4):
                expert(0, j, j)
            with pe.Fori(1, NX // 4) as i:
                for j in range(4):
                    expert(i, j, 4 * i + j)
            pe.wait_ge(m_h, NX)
            pe.wait_ge(m_wd[3], 16 * NX // 4)
            pe.wait_ge(m_yc, NX - 1)
            down(hT[:, 1], wd[3]).then_inc(m_y, 1)
            over = pe.value_load(flag[0:1, 0:1], min_val=0, max_val=1)
            with pe.If(over > 0):
                pe.wait_ge(m_yc, NX)
                with pe.Fori(0, NX * (BLOCKS - 1)) as n:
                    pe.wait_ge(e_g, 16 * n + 16)
                    for k in range(KD):
                        mm = pe.transpose(ppf[0][:, k * P:(k + 1) * P], xg[:, 0, k * P:(k + 1) * P], ident[:])
                    mm.then_inc(e_t, 1)
                    pe.wait_ge(e_w, 64 * n + 64)
                    pe.wait_ge(e_tc, n + 1)
                    gate_up(pw[:, 0], wgu[0], xgT[:, 0]).then_inc(e_gu, 1)
                    pe.wait_ge(e_h, n + 1)
                    down(hT[:, 0], wd[0]).then_inc(e_y, 1)

        @block.scalar
        def _(act):
            chain = Count(a_chain)

            def link(ins):
                act.wait_ge(a_chain, chain.by(ins))

            def cut(g):
                act.wait_ge(s_raw[g % RAW], raw_need[g])
                if g >= 2:
                    group_used(act, min(g - 2, OUT0 - 1))
                width = groups[g][2]
                act.activation(w_hi(g)[:, :, 0:width], raw[:, g % RAW, :, 0:width], ACT.Copy).then_inc(s_wh, 1)

            def evacuate(what):
                kind, c = what
                n = fill_of[what]
                b = n % 2
                act.wait_ge(s_full[b], n // 2 + 1)
                src = pp[:, b, :, 0:HT]
                two = lambda t: t.rearrange("p (a b) -> p a b", a=2)
                func = ACT.Copy
                if kind in ("ak", "aq"):
                    if c == 0 and kind == "ak":
                        act.wait_ge(s_o, UNITS)
                    dst = two((ka if kind == "ak" else qa)[:, c, :])
                elif kind == "iq":
                    dst = two(qi[:, c, :])
                elif kind == "ik":
                    src, dst = pp[0:68, b, :, 0:HT], two(kiw[:, :])
                elif kind == "hf":
                    dst = two(B[:, c, :])
                elif kind == "hq":
                    dst, func = two(q[:, c, :]), ACT.Silu
                elif kind == "hg":
                    dst, func = two(sg[:, c, :]), ACT.Silu
                elif kind == "gate":
                    if c >= 2:
                        act.wait_ge(s_gst[c % 2], 16 * (c // 2))
                    dst = two(gring[:, c % 2, :])
                elif kind in ("hi", "av"):
                    t = v if kind == "hi" else va
                    i, cc = 2 * (c % 3), GW * (c // 3)
                    if i < 4:
                        src, dst = pp[:, b, :, 0:GW], t[:, i:i + 2, cc:cc + GW]
                    else:
                        src, dst = pp[0:64, b, 0, 0:GW], t[0:64, 4, cc:cc + GW]
                ev = act.activation(dst, src, func)
                ev.then_inc(s_ev[kind], 1)
                act.wait_ge(s_ev[kind], c + 1)
                act.nop().then_inc(s_free[b], 1)
                if kind == "gate":
                    act.dma_start(gates_d[c], gring[:, c % 2, :]).then_inc(s_gst[c % 2], 16)

            def x_high(i):
                b = i % 2
                act.wait_ge(s_full[b], i // 2 + 1)
                act.activation(xh[:, :, i * P:i * P + ROWS[i]], ppf[b].rearrange("p (k t) -> p k t", k=KD)[:, :, 0:ROWS[i]],
                               ACT.Copy).then_inc(s_xh, 1)

            def index_copies():
                act.wait_ge(s_it, 1)
                act.activation(kicT[:], pw[:, 2, 0:PAST], ACT.Copy).then_inc(s_itc, 1)
                act.wait_ge(s_it, 2)
                act.activation(tok4[:, 0:4, :], pw[:, 3, 0:272].rearrange("p (i c) -> p i c", c=68), ACT.Copy).then_inc(a_chain, 1)
                chain.n += 1
                act.activation(tok4[0:64, 4, :], pw[0:64, 3, 272:340], ACT.Copy).then_inc(s_itc, 1)

            def index_relu(n, i):
                r = ROWS[i]
                for ih in range(IH):
                    s = 4 * n + ih
                    act.wait_ge(s_sc, s + 1)
                    if s >= 2:
                        act.wait_ge(s_acc, s - 1)
                    act.activation(relu[0:r, s % 2, 0:KEYS[i]], pw[0:r, s % 2, 0:KEYS[i]], ACT.Relu, scale=ID ** -0.5).then_inc(s_rl, 1)

            def softplus(h):
                act.wait_ge(s_ev["hf"], h + 2)
                z, l = B[:, h:h + 2, :], L[:, h:h + 2, :]
                link(act.activation(l, z, ACT.Abs))
                link(act.activation(l, l, ACT.Exp, scale=-1.0))
                act.activation(l, l, ACT.Ln, bias=1.0).then_inc(s_L, 1)

            def key(h):
                act.wait_ge(s_g, 2 * h + 1)
                act.activation(kk[:, h, :], kk[:, h, :], ACT.Exp, scale=-1.0).then_inc(s_k, 1)

            def levels(h):
                for l in range(LEVELS):
                    act.wait_ge(s_D, 14 * h + 2 * l + 2)
                    w = TP if l == LEVELS - 1 else T
                    act.activation(X[h % 2][l][:, 0:w], X[h % 2][l][:, 0:w], ACT.Exp).then_inc(s_X, 1)
                if h == 1:
                    act.wait_ge(s_g, 2 * HH)
                if h >= 2:
                    act.wait_ge(s_kdt, NT * (h - 1))
                    act.wait_ge(s_of, NT * (h - 1))
                for c in range(NT):
                    cs, cw = c * P, ROWS[c]
                    e = act.activation(kd[h % 2][:, cs:cs + cw], B[:, h, cs:cs + cw], ACT.Exp, scale=-1.0,
                                       bias=B[:, h, cs + cw - 1:cs + cw])
                e.then_inc(s_kd, 1)
                act.activation(eBT[:, h % 2, 0:4], B[:, h, P - 1:TP:P], ACT.Exp)
                act.activation(eBT[:, h % 2, 4:5], B[:, h, T - 1:T], ACT.Exp).then_inc(s_eB, 1)
                act.wait_ge(s_kd, h + 1)
                act.wait_ge(s_eB, h + 1)
                act.activation(B[:, h, :], B[:, h, :], ACT.Exp).then_inc(s_qe, 1)

            def kd_copy(u):
                cw = ROWS[u % NT]
                act.wait_ge(s_kdt, u + 1)
                if u >= 2:
                    act.wait_ge(s_o, u - 1)
                act.activation(kdT[0:cw, u % 2, :], pw[0:cw, 2, 0:P], ACT.Copy).then_inc(s_ktc, 1)

            def square_copy(h):
                act.wait_ge(s_ms, h + 1)
                act.activation(q[:, h, :].rearrange("p (a b) -> p a b", a=2), pw[:, 0:2, 0:HT], ACT.Copy).then_inc(s_msc, 1)

            def head_norms():
                act.wait_ge(s_msc, HH)
                link(act.activation(q[:, :, :], q[:, :, :], ACT.Ln, scale=1.0 / P, bias=small[:, 0:1]))
                act.activation(q[:, :, :], q[:, :, :], ACT.Exp, scale=-0.5).then_inc(s_rms, 1)

            def hgrn_step(k):
                if normed_head(k) is not None:
                    square_copy(normed_head(k))
                if prepared_head(k - 1) is not None:
                    levels(prepared_head(k - 1))
                if k < UNITS:
                    kd_copy(k)
                if k == UNITS + 1:
                    head_norms()

            for i in range(NT):
                x_high(i)
                if i == 3:
                    cut(0)
            cut(1)
            act.wait_ge(s_const, 80)
            def cached_keys():
                for j in range(2):
                    act.wait_ge(s_ct, j + 1)
                    act.activation(kcT[:, :, j * P:(j + 1) * P], pw[:, j, :].rearrange("p (c t) -> p c t", c=4), ACT.Copy).then_inc(s_ctc, 1)

            def probs(a):
                i = a // AH
                r, w = ROWS[i], KEYS[i]
                act.wait_ge(s_Lm, a + 1)
                if a >= RING:
                    act.wait_ge(s_PT, a - RING + 1)
                act.activation(Pr[0:r, a % RING, 0:w], Lm[0:r, a % RING, 0:w], ACT.Exp, scale=-1.0,
                               bias=mx[0:r, a % RING, 1:2], accum_out=mx[0:r, a % RING, 2:3]).then_inc(s_P, 1)

            def probs_copy(a):
                i = a // AH
                r, nj = ROWS[i], (KEYS[i] + P - 1) // P
                act.wait_ge(s_PT, a + 1)
                if a >= 2:
                    act.wait_ge(s_O, a - 1)
                src = pw[:, a % 2, :].rearrange("p (j t) -> p j t", j=4)
                if i < 4:
                    ins = act.activation(PT[:, a % 2, 0:nj, :], src[:, 0:nj, :], ACT.Copy)
                else:
                    link(act.activation(PT[:, a % 2, 0:2, 0:64], src[:, 0:2, 0:64], ACT.Copy))
                    ins = act.activation(PT[0:64, a % 2, 2, 0:64], src[0:64, 2, 0:64], ACT.Copy)
                ins.then_inc(s_PTc, 1)

            def tile_high(i):
                r = ROWS[i]
                act.wait_ge(s_O, AH * (i + 1))
                act.activation(yh[:, 4:8, i * P:i * P + r], pw[:, 2 + i % 2, :].rearrange("p (c t) -> p c t", c=4)[:, :, 0:r],
                               ACT.Copy).then_inc(s_yh, 1)

            def attention():
                NA = NT * AH
                group_used(act, 23)
                for a in range(NA + AHEAD + 1):
                    if a < NA:
                        probs(a)
                    if 0 <= a - AHEAD < NA:
                        probs_copy(a - AHEAD)
                    if a - AHEAD - 2 >= 0 and (a - AHEAD - 2) % AH == AH - 1:
                        tile_high((a - AHEAD - 2) // AH)
                    if a == AH:
                        act.activation(yh[:, 0:4, :], o_all[:], ACT.Copy).then_inc(s_ygh, 1)
                    if a in (2 * AH, 3 * AH):
                        cut(22 + a // AH)
                tile_high(NT - 1)

            def gates(m):
                act.wait_ge(s_gl[m % 2], 16 * (m // 2 + 1))
                g_ = gld[:, m % 2].rearrange("p a t -> p (a t)")
                act.activation(g_, g_, ACT.Sigmoid).then_inc(s_sig, 1)

            def merged_high(m):
                act.wait_ge(s_m, m + 1)
                if m + 2 < KD:
                    act.dma_start(gld[:, m % 2], gates_d[m + 2:m + 11:8].rearrange("a p t -> p a t")).then_inc(s_gl[m % 2], 16)
                act.activation(mh[:, m, :], gsum[:, m % 2, :], ACT.Copy).then_inc(s_mh, 1)

            for n, (gg, what) in enumerate(fills):
                if what[0] == "kt":
                    if what[1] == NT - 1:
                        cached_keys()
                    continue
                if what[0] == "attention":
                    attention()
                    continue
                if what == ("hf", 0):
                    act.wait_ge(s_xl, NT)
                if what[0] == "br":
                    if what[1] % 2 == 0:
                        gates(what[1] // 2)
                    else:
                        merged_high(what[1] // 2)
                    if what[1] == 15:
                        for g in range(OUT0 + 1, NG):
                            cut(g)
                elif what[0] == "out":
                    break
                else:
                    evacuate(what)
                if what == ("hf", 0):
                    index_copies()
                if what == ("hf", 1):
                    index_relu(0, 3)
                    index_relu(1, 4)
                if what == ("hf", 3):
                    index_relu(2, 2)
                    index_relu(3, 1)
                if ends_group(gg, what) and gg + 2 <= OUT0 and gg + 2 not in (24, 25):
                    cut(gg + 2)
                if what == ("hf", 2):
                    softplus(0)
                if what == ("hi", 0):
                    softplus(2)
                if what in (("hi", 1), ("hi", 2)):
                    for h in range(2 * what[1] - 2, 2 * what[1]):
                        key(h)
                if what == ("hi", 3):
                    levels(0)
                if what == ("hi", 4):
                    levels(1)
                for k in hgrn_steps(what):
                    hgrn_step(k)

            def deviation(i, ready, done):
                act.wait_ge(ready, i + 1)
                act.activation(rstd[:, i:i + 1], mv[:, i, 1:2], ACT.Sqrt, bias=small[:, 1:2]).then_inc(done, 1)

            def x1_copy(i):
                act.wait_ge(s_tx, i + 1)
                if i >= 2:
                    act.wait_ge(s_rl_, i - 1)
                act.activation(x1T[:, i % 2].rearrange("p k t -> p (k t)"), pw[:, 0:2].rearrange("p a b -> p (a b)"), ACT.Copy).then_inc(s_txc, 1)

            def route_exponentials(b):
                first, end = BATCHES[b]
                act.wait_ge(s_gx, 2 * b + 1)
                act.activation(ge[:, first:end], gx[:, first:end], ACT.Exp).then_inc(s_ge, 1)
                act.wait_ge(s_gx, 2 * b + 2)
                act.activation(ee[:, first:end], es[:, first:end], ACT.Exp).then_inc(s_ge, 1)

            for i in range(NT):
                deviation(i, s_var, s_sd)
                if i >= 1:
                    x1_copy(i - 1)
                if i == BATCHES[0][1]:
                    route_exponentials(0)
            x1_copy(NT - 1)
            route_exponentials(1)

            def expert(e, j, first, x, t, tc, gu, si, h_):
                act.wait_ge(t, e + 1)
                if not first:
                    act.wait_ge(gu, x)
                act.activation(xgT[:, j].rearrange("p k t -> p (k t)"), ppf[0], ACT.Copy).then_inc(tc, 1)
                act.wait_ge(gu, e + 1)
                if not first:
                    act.wait_ge(h_, x)
                act.activation(hs[:, j].rearrange("p f t -> p (f t)"), pw[:, j, 0:256], ACT.Silu).then_inc(si, 1)

            for e in range(4):
                expert(e, e % 2, e < 2, e - 1, m_t, m_tc, m_gu, m_si, m_h)
            with act.Fori(1, NX // 4) as i:
                for j in range(4):
                    expert(4 * i + j, j % 2, False, 4 * i + (j - 1), m_t, m_tc, m_gu, m_si, m_h)
            over = act.value_load(flag[0:1, 0:1], min_val=0, max_val=1)
            with act.If(over > 0):
                act.wait_ge(m_h, NX)
                with act.Fori(0, NX * (BLOCKS - 1)) as n:
                    expert(n, 0, True, 0, e_t, e_tc, e_gu, e_si, e_h)
            for i in range(NT):
                deviation(i, s_v2, s_sd2)

        @block.gpsimd
        def _(pool):
            def cut(g):
                width = groups[g][2]
                pool.wait_ge(s_wh, g + 1)
                pool.tensor_tensor(w_lo(g)[:, :, 0:width], raw[:, g % RAW, :, 0:width],
                                   w_hi(g)[:, :, 0:width].bitcast(F32), ALU.subtract).then_inc(s_wl, 1)

            pool.memset(ones[:], 1.0).then_inc(s_ones, 1)

            def times(h):
                pool.wait_ge(s_k, h + 1)
                pool.wait_ge(s_ev["hq"], h + 1)
                for l in range(LEVELS):
                    hs = 1 << l
                    w = TP if l == LEVELS - 1 else T
                    pool.wait_ge(s_X, LEVELS * h + l + 1)
                    xv = X[h % 2][l][:, 0:w].rearrange("p (n a s) -> p n a s", a=2, s=hs)
                    qv = q[:, h, 0:w].rearrange("p (n a s) -> p n a s", a=2, s=hs)
                    kv = kk[:, h, 0:w].rearrange("p (n a s) -> p n a s", a=2, s=hs)
                    pool.tensor_tensor(xv[:, :, 1, :], xv[:, :, 1, :], qv[:, :, 1, :], ALU.mult).then_inc(s_XM, 1)
                    pool.tensor_tensor(xv[:, :, 0, :], xv[:, :, 0, :], kv[:, :, 0, :], ALU.mult).then_inc(s_XM, 1)
                pool.wait_ge(s_kd, h + 1)
                pool.tensor_tensor(kd[h % 2][:], kd[h % 2][:], kk[:, h, :], ALU.mult).then_inc(s_qem, 1)
                pool.wait_ge(s_qe, h + 1)
                pool.tensor_tensor(B[:, h, :], B[:, h, :], q[:, h, :], ALU.mult).then_inc(s_qem, 1)

            for g in range(2):
                cut(g)
            for gg, what in fills:
                if what[0] == "br":
                    break
                if gg is not None and last_of[gg] == what and gg + 2 < 24:
                    cut(gg + 2)
                if what == ("hq", 1):
                    times(0)
                if what == ("hg", 0):
                    times(1)
                for k in hgrn_steps(what):
                    if prepared_head(k - 1) is not None:
                        times(prepared_head(k - 1))
            for g in range(24, OUT0 + 2):
                cut(g)
            pool.wait_ge(s_Lm, NT * AH)
            pool.wait_ge(s_store, STORED)
            pool.memset(zero[:], 0).then_inc(s_zero, 1)
            pool.memset(zcol[:], 0).then_inc(s_zero, 1)
            pool.wait_ge(s_rc, 128)
            pool.wait_ge(s_zd, 16)
            for b, (first, end) in enumerate(BATCHES):
                pool.wait_ge(s_dest, b + 1)
                for i in range(first, end):
                    for c in range(2):
                        r = ROWS[i]
                        pool.indirect_dma_start(slot_d, bass.IndirectOffsetOnAxis(ap=dest[0:r, c, i:i + 1], axis=0),
                                                tid[0:r, i:i + 1], None).then_inc(s_sct, 16)
            pool.wait_ge(s_x1d, 16 * NT)
            pool.wait_ge(s_stok, 16)
            filled(pool, ("out", NT - 1))
            for e in range(NX):
                j = e % 2
                if e >= 2:
                    pool.wait_ge(m_t, e - 1)
                pool.indirect_dma_start(xg[:, j, :], None, x1_d, bass.IndirectOffsetOnAxis(ap=stok[:, e:e + 1], axis=0)).then_inc(m_g[j], 16)
            over = pool.value_load(flag[0:1, 0:1], min_val=0, max_val=1)
            with pool.If(over > 0):
                pool.wait_ge(m_t, NX)
                pool.wait_ge(s_zero, 2)
                pool.memset(stx[:, 1:2], 0).then_inc(e_i, 1)
                with pool.Fori(0, NX * (BLOCKS - 1)) as n:
                    pool.wait_ge(e_w, 64 * n + 64)
                    pool.tensor_tensor(stx[:, 1:2], stx[:, 0:1], zcol[:], ALU.add).then_inc(e_ix, 1)
                    pool.wait_ge(e_ix, n + 1)
                    pool.sem_inc(e_g2, 1)
                    pool.indirect_dma_start(xg[:, 0, :], None, x1_d, bass.IndirectOffsetOnAxis(ap=stx[:, 1:2], axis=0)).then_inc(e_g, 16)
                    pool.wait_ge(e_yc, n + 1)
                    pool.tensor_tensor(zcol2[:], zcol[:], zcol[:], ALU.add).then_inc(e_i, 1)
            for j in range(2):
                pool.wait_ge(m_ys[j], 16 * NX // 2)

            def gather_results(rows):
                pool.wait_ge(m_gu, NX)
                for i in range(NT):
                    r = ROWS[i]
                    if i >= 2:
                        pool.wait_ge(s_ygf, i - 1)
                    for c in range(2):
                        pool.indirect_dma_start(yg[0:r, i % 2, c, :], None, rows,
                                                bass.IndirectOffsetOnAxis(ap=dest[0:r, c, i:i + 1], axis=0)).then_inc(s_yg[i % 2], 16)

            with pool.If(over > 0):
                pool.wait_ge(e_ys, 16 * NX * (BLOCKS - 1))
                gather_results(ys_d)
            with pool.If(over < 1):
                gather_results(ys_d[0:CAP * NX])

        @block.vector
        def _(dve):
            chain = Count(d_chain)

            def link(ins):
                dve.wait_ge(d_chain, chain.by(ins))

            for i in range(NT):
                b, at, end = i % 2, i * P, i * P + ROWS[i]
                dve.wait_ge(s_xh, i + 1)
                dve.tensor_tensor(xl[:, :, at:end], ppf[b].rearrange("p (k t) -> p k t", k=KD)[:, :, 0:ROWS[i]],
                                  xh[:, :, at:end].bitcast(F32), ALU.subtract).then_inc(s_xl, 1)
                dve.wait_ge(s_xl, i + 1)
                dve.engine_nop().then_inc(s_free[b], 1)

            def index_sum(n, i):
                r = ROWS[i]
                acc = maskb[0:r, MOFF[i]:MOFF[i] + KEYS[i]]
                for ih in range(IH):
                    s = 4 * n + ih
                    dve.wait_ge(s_rl, s + 1)
                    rl = relu[0:r, s % 2, 0:KEYS[i]]
                    if s >= 1:
                        dve.wait_ge(s_acc, s)
                    if ih == 0:
                        dve.tensor_scalar(acc, rl, tok4[0:r, i, 64:65], None, ALU.mult).then_inc(s_acc, 1)
                    else:
                        dve.scalar_tensor_tensor(acc, rl, tok4[0:r, i, 64 + ih:65 + ih], acc, ALU.mult, ALU.add).then_inc(s_acc, 1)

            def select(n, i, first, last):
                r, w, rounds = ROWS[i], KEYS[i], TOPK[i] // 8
                acc = maskb[0:r, MOFF[i]:MOFF[i] + w]
                if first == 0:
                    dve.wait_ge(s_acc, 4 * n + 4)
                    if i < 4:
                        link(dve.memset(acc[0:64, w - 64:w], NEG))
                for it in range(first, min(last, rounds)):
                    src = acc if it == 0 else wk[0:r, 0:w]
                    link(dve.max(top[0:r, :], src))
                    if it < rounds - 1:
                        link(dve.match_replace(wk[0:r, 0:w], top[0:r, :], src, NEG))
                if last < rounds:
                    return
                thr = top[0:r, 7:8]
                above, equal = wk[0:r, 0:w], eq[0:r, 0:w]
                link(dve.tensor_scalar(above, acc, thr, None, ALU.is_gt))
                link(dve.tensor_scalar(equal, acc, thr, None, ALU.is_equal))
                link(dve.tensor_reduce(cnt[0:r, 0:1], above, AX.X, ALU.add))
                link(dve.tensor_scalar(cnt[0:r, 1:2], cnt[0:r, 0:1], -1.0, float(TOPK[i]), ALU.mult, ALU.add))
                link(dve.tensor_tensor_scan(acc, equal, equal, 0.0, ALU.add, ALU.max))
                link(dve.scalar_tensor_tensor(equal, acc, cnt[0:r, 1:2], equal, ALU.is_le, ALU.mult))
                link(dve.tensor_tensor(above, above, equal, ALU.add))
                dve.tensor_scalar(acc, above, BIG, -BIG, ALU.mult, ALU.add).then_inc(s_mask, 1)
                dve.wait_ge(s_mask, n + 1)

            def decay(h):
                z, l = B[:, h, :], L[:, h, :]
                dve.wait_ge(s_L, h // 2 + 1)
                dve.scalar_tensor_tensor(kk[:, h, :], z, 0.0, l, ALU.max, ALU.add).then_inc(s_g, 1)
                dve.wait_ge(s_g, 2 * h + 1)
                link(dve.scalar_tensor_tensor(l, z, 0.0, l, ALU.min, ALU.subtract))
                dve.tensor_tensor_scan(z, reset[:], l, 0.0, ALU.mult, ALU.add).then_inc(s_g, 1)

            def exponents(h):
                if h == 0:
                    dve.wait_ge(s_acc, 16)
                if h == 1:
                    dve.wait_ge(s_g, 2 * HH)
                if h >= 2:
                    dve.wait_ge(s_G, NT * (h - 1))
                    dve.wait_ge(s_ms, h - 1)
                for l in range(LEVELS):
                    hs = 1 << l
                    w = TP if l == LEVELS - 1 else T
                    nb = w // (2 * hs)
                    xv = X[h % 2][l][:, 0:w].rearrange("p (n a s) -> p n a s", a=2, s=hs)
                    bv = B[:, h, 0:w].rearrange("p (n a s) -> p n a s", a=2, s=hs)
                    mid = bv[:, :, 0, hs - 1:hs].broadcast_to([P, nb, hs])
                    dve.tensor_tensor(xv[:, :, 1, :], bv[:, :, 1, :], mid, ALU.subtract).then_inc(s_D, 1)
                    dve.tensor_tensor(xv[:, :, 0, :], mid, bv[:, :, 0, :], ALU.subtract).then_inc(s_D, 1)

            def chunk_weights(u):
                cw = ROWS[u % NT]
                nl = LEVELS + (1 if u % NT < 4 else 0)
                G = pw[:, 0:2, :].rearrange("p a (b c) -> p (a b) c", c=P)
                dve.wait_ge(s_G, u + 1)
                if u >= 1:
                    dve.wait_ge(s_AT, u)
                dve.tensor_tensor(Gm[0:cw, 0:nl, 0:cw], G[0:cw, 0:nl, 0:cw], pairs[0:cw, 0:nl, 0:cw], ALU.mult).then_inc(s_Gf, 1)
                dve.wait_ge(s_Gf, u + 1)
                if u >= 2:
                    dve.wait_ge(s_o, u - 1)
                dve.tensor_reduce(AT[0:cw, u % 2, 0:cw], Gm[0:cw, 0:nl, 0:cw].rearrange("p l t -> p t l"), AX.X, ALU.add).then_inc(s_AT, 1)

            def chunk_out(u):
                h, c = u // NT, u % NT
                cs, cw = c * P, ROWS[c]
                group = 0 if c < 4 else 1
                dve.wait_ge(s_o, u + 1)
                link(dve.tensor_copy(o_all[:, h, cs:cs + cw], pw[:, 3, 0:cw]))
                if c == 0:
                    ins = dve.tensor_copy(S[:, 0, h, :], pw[:, 3, 256:384])
                else:
                    dve.wait_ge(s_eB, h + 1)
                    ins = dve.scalar_tensor_tensor(S[:, group, h, :], S[:, group, h, :], eBT[:, h % 2, c:c + 1], pw[:, 3, 256:384], ALU.mult, ALU.add)
                ins.then_inc(s_of, 1)
                dve.wait_ge(s_of, u + 1)

            def head_out(h):
                o = o_all[:, h, :]
                dve.wait_ge(s_G, NT * (h + 1))
                dve.tensor_tensor(X[h % 2][1], o, o, ALU.mult).then_inc(s_osq, 1)
                dve.wait_ge(s_ev["hg"], h + 1)
                link(dve.scalar_tensor_tensor(o, o, normw[:, 0:1], sg[:, h, :], ALU.mult, ALU.mult))

            def head_scales():
                dve.wait_ge(s_rms, 1)
                dve.tensor_tensor(o_all[:], o_all[:], q[:], ALU.mult).then_inc(s_y, 1)
                dve.wait_ge(s_y, 1)

            def hgrn_step(k):
                if 1 <= k <= UNITS:
                    chunk_out(k - 1)
                    if k % NT == 0:
                        head_out(k // NT - 1)
                if k < UNITS:
                    chunk_weights(k)
                if prepared_head(k) is not None:
                    exponents(prepared_head(k))
                if k == UNITS + 1:
                    head_scales()

            dve.wait_ge(s_itc, 2)
            for i in range(NT):
                r = ROWS[i]
                link(dve.tensor_scalar(tok4[0:r, i, 64:68], tok4[0:r, i, 64:68], IH ** -0.5, None, ALU.mult))
            index_sum(0, 3)
            index_sum(1, 4)
            dve.wait_ge(s_const, 80)
            for h in (0, 1):
                decay(h)
            index_sum(2, 2)
            index_sum(3, 1)
            for h in (2, 3):
                decay(h)
            for h in (0, 1):
                exponents(h)
            select(0, 3, 0, 16)
            for k in range(UNITS + 2):
                if k < 3:
                    select(1, 4, 4 * k, 4 * k + 4)
                elif k < 7:
                    select(2, 2, 4 * (k - 3), 4 * (k - 2))
                elif 8 <= k < 12:
                    select(3, 1, 4 * (k - 8), 4 * (k - 7))
                hgrn_step(k)

            for i in range(NT):
                n = fill_of[("kt", i)]
                b, r = n % 2, ROWS[i]
                dve.wait_ge(s_full[b], n // 2 + 1)
                dve.tensor_copy(ktok[0:r, i, :], ppf[b][0:r, 0:512]).then_inc(s_kt, 1)
                dve.wait_ge(s_kt, i + 1)
                dve.engine_nop().then_inc(s_free[b], 1)

            link(dve.memset(mask0[:], 0.0))
            link(dve.memset(mask0[0:64, 64:128], -BIG))

            def masked(a):
                i = a // AH
                r, w, x = ROWS[i], KEYS[i], a % RING
                m_ = mask0[0:r, :] if i == 0 else maskb[0:r, MOFF[i]:MOFF[i] + w]
                dve.wait_ge(s_lg, a + 1)
                if a >= RING:
                    dve.wait_ge(s_P, a - RING + 1)
                    dve.wait_ge(s_rd, a - RING + 1)
                dve.tensor_tensor_reduce(Lm[0:r, x, 0:w], logit_bank(a)[0:r, 0:w], m_, -(AD ** -0.5), -NEG, ALU.add, ALU.min,
                                         mx[0:r, x, 1:2]).then_inc(s_Lm, 1)

            def normed(a):
                i = a // AH
                r, w, x = ROWS[i], KEYS[i], a % RING
                dve.wait_ge(s_P, a + 1)
                if a >= RING:
                    dve.wait_ge(s_Pn, a - RING + 1)
                dve.reciprocal(mx[0:r, x, 3:4], mx[0:r, x, 2:3]).then_inc(s_rd, 1)
                dve.wait_ge(s_rd, a + 1)
                dve.tensor_scalar(Pr[0:r, x, 0:w], Pr[0:r, x, 0:w], mx[0:r, x, 3:4], None, ALU.mult).then_inc(s_Pn, 1)

            def tile_low(i):
                r = ROWS[i]
                dve.wait_ge(s_yh, i + 1)
                dve.tensor_tensor(yl[:, 4:8, i * P:i * P + r], pw[:, 2 + i % 2, :].rearrange("p (c t) -> p c t", c=4)[:, :, 0:r],
                                  yh[:, 4:8, i * P:i * P + r].bitcast(F32), ALU.subtract).then_inc(s_yl, 1)

            NA = NT * AH
            for a in range(NA + AHEAD + 1):
                if a < NA:
                    masked(a)
                if 0 <= a - 1 < NA:
                    normed(a - 1)
                if a - AHEAD - 3 >= 0 and (a - AHEAD - 3) % AH == AH - 1:
                    tile_low((a - AHEAD - 3) // AH)
                if a == AH + 4:
                    dve.wait_ge(s_ygh, 1)
                    dve.tensor_tensor(yl[:, 0:4, :], o_all[:], yh[:, 0:4, :].bitcast(F32), ALU.subtract).then_inc(s_ygl, 1)
            tile_low(NT - 1)

            dve.wait_ge(s_sk, 64)
            for c in range(2):
                dve.wait_ge(s_gst[c], 16 * 8)

            def merged_low(m):
                dve.wait_ge(s_mh, m + 1)
                dve.tensor_tensor(ml[:, m, :], gsum[:, m % 2, :], mh[:, m, :].bitcast(F32), ALU.subtract).then_inc(s_ml, 1)

            def low_part(g):
                dve.wait_ge(s_wh, g + 1)
                dve.tensor_tensor(w_lo(g), raw[:, g % RAW], w_hi(g).bitcast(F32), ALU.subtract).then_inc(s_wlo, 1)

            for m in range(KD):
                dve.wait_ge(s_sig, m + 1)
                if m >= 1:
                    dve.wait_ge(s_m, m)
                for w in range(2):
                    n = fill_of[("br", 2 * m + w)]
                    b = n % 2
                    dve.wait_ge(s_full[b], n // 2 + 1)
                    two = lambda t: t.rearrange("p (a b) -> p a b", a=2)
                    dve.tensor_tensor(two(gring[:, w, :]), pp[:, b, :, 0:HT], two(gld[:, m % 2, w, :]), ALU.mult).then_inc(s_br, 1)
                    dve.wait_ge(s_br, 2 * m + w + 1)
                    dve.engine_nop().then_inc(s_free[b], 1)
                if m >= 2:
                    dve.wait_ge(s_ml, m - 1)
                dve.tensor_tensor(gsum[:, m % 2, :], gring[:, 0, :], gring[:, 1, :], ALU.add).then_inc(s_m, 1)
                if m >= 1:
                    merged_low(m - 1)
            merged_low(KD - 1)
            for g in range(OUT0 + 2, NG):
                low_part(g)

            dve.wait_ge(s_xr, 32)
            dve.wait_ge(s_store, STORED)
            link(dve.memset(xr[64:128, 4, :], 0.0))

            def residual(i):
                n = fill_of[("out", i)]
                b, r = n % 2, ROWS[i]
                dve.wait_ge(s_full[b], n // 2 + 1)
                dve.scalar_tensor_tensor(xr[0:r, i, :], xr[0:r, i, :], ALPHA, ppf[b][0:r], ALU.mult, ALU.add).then_inc(s_res, 1)
                dve.wait_ge(s_res, i + 1)
                dve.engine_nop().then_inc(s_free[b], 1)

            def moments(i, done):
                for half in range(2):
                    link(dve.bn_stats(stats[:, i, half, :], xr[:, i, half * 512:(half + 1) * 512]))
                dve.bn_aggr(mv[:, i, :], stats[:, i]).then_inc(done, 1)
                dve.wait_ge(done, i + 1)
                link(dve.tensor_scalar(halfv[:, i:i + 1], mv[:, i, 1:2], 1e-5, -0.5, ALU.add, ALU.mult))

            def inverse_root(i, ready):
                y, t = rstd[:, i:i + 1], newton[:, i:i + 1]
                dve.wait_ge(ready, i + 1)
                link(dve.reciprocal(y, y))
                link(dve.tensor_scalar(t, y, y, halfv[:, i:i + 1], ALU.mult, ALU.mult))
                link(dve.tensor_scalar(y, t, 1.5, y, ALU.add, ALU.mult))

            def normalize(i, row, done, ready):
                inverse_root(i, ready)
                link(dve.tensor_scalar(xr[:, i, :], xr[:, i, :], mv[:, i, 0:1], rstd[:, i:i + 1], ALU.subtract, ALU.mult))
                link(dve.tensor_tensor(xr[:, i, :], xr[:, i, :], lnr[:, row, :], ALU.mult))
                dve.tensor_tensor(xr[:, i, :], xr[:, i, :], lnr[:, row + 1, :], ALU.add).then_inc(done, 1)

            def route(b):
                first, end = BATCHES[b]
                n = end - first
                tl = slice(first, end)
                col = lambda c: cols[:, c, tl]
                wide = lambda t: t.unsqueeze(2).broadcast_to([P, n, 4])
                four = lambda t: t.unsqueeze(1).broadcast_to([P, n, 4])
                top1, es_, ge_, ee_, gx_ = ohg[:, tl], es[:, tl], ge[:, tl], ee[:, tl], gx[:, tl]

                def first_of(oh):
                    link(dve.tensor_tensor(oh, oh, four(order[:]), ALU.mult))
                    link(dve.tensor_reduce(taken[:, tl], oh, AX.X, ALU.max))
                    link(dve.tensor_tensor(oh, oh, wide(taken[:, tl]), ALU.is_equal))

                dve.wait_ge(s_rl_, end)
                dve.tensor_tensor(lg[:, tl], pw[:, 2, 20 * first:20 * end].rearrange("p (i c) -> p i c", c=20),
                                  br_[:].unsqueeze(1).broadcast_to([P, n, 20]), ALU.add).then_inc(s_lgd, 1)
                dve.wait_ge(s_lgd, b + 1)
                link(dve.tensor_reduce(col(0), lg[:, tl, 0:4], AX.X, ALU.max))
                dve.tensor_tensor(gx_, lg[:, tl, 0:4], wide(col(0)), ALU.subtract).then_inc(s_gx, 1)
                dve.wait_ge(s_gx, 2 * b + 1)
                link(dve.tensor_scalar(top1, gx_, 0.0, None, ALU.is_equal))
                first_of(top1)
                link(dve.tensor_tensor(prod[:, tl], lg[:, tl, 4:20].rearrange("p i (g e) -> p i g e", g=4),
                                       top1.unsqueeze(3).broadcast_to([P, n, 4, 4]), ALU.mult))
                link(dve.tensor_reduce(es_, prod[:, tl].rearrange("p i g e -> p i e g"), AX.X, ALU.add))
                link(dve.tensor_reduce(col(3), es_, AX.X, ALU.max))
                dve.tensor_tensor(es_, es_, wide(col(3)), ALU.subtract).then_inc(s_gx, 1)
                dve.wait_ge(s_ge, 2 * b + 1)
                link(dve.tensor_reduce(col(1), ge_, AX.X, ALU.add))
                link(dve.reciprocal(col(2), col(1)))
                dve.wait_ge(s_ge, 2 * b + 2)
                link(dve.tensor_reduce(col(4), ee_, AX.X, ALU.add))
                link(dve.reciprocal(col(4), col(4)))
                link(dve.tensor_tensor(es_, ee_, wide(col(4)), ALU.mult))
                for c, oh in ((5, oh1[:, tl]), (6, oh2[:, tl])):
                    link(dve.tensor_reduce(col(c), es_, AX.X, ALU.max))
                    link(dve.tensor_tensor(oh, es_, wide(col(c)), ALU.is_equal))
                    first_of(oh)
                    if c == 5:
                        link(dve.scalar_tensor_tensor(es_, oh, -2.0, es_, ALU.mult, ALU.add))
                for m_, oh in ((M1, oh1), (M2, oh2)):
                    link(dve.tensor_tensor(m_[:, tl], top1.unsqueeze(3).broadcast_to([P, n, 4, 4]),
                                           oh[:, tl].unsqueeze(2).broadcast_to([P, n, 4, 4]), ALU.mult))
                    if end == NT:
                        link(dve.memset(m_[64:128, 4], 0.0))
                flat = lambda t: t[:, tl].rearrange("p i g e -> p i (g e)")
                dve.tensor_tensor(M[:, tl], flat(M1), flat(M2), ALU.add).then_inc(s_M, 1)
                link(dve.tensor_tensor(col(7), col(5), col(6), ALU.add))
                link(dve.reciprocal(col(7), col(7)))
                link(dve.tensor_tensor(col(7), col(7), col(2), ALU.mult))
                link(dve.tensor_tensor(col(8), col(5), col(7), ALU.mult))
                link(dve.tensor_tensor(col(9), col(6), col(7), ALU.mult))

            def slots(b):
                first, end = BATCHES[b]
                n = end - first
                tl = slice(first, end)
                dve.wait_ge(s_rk, b + 1)
                link(dve.scalar_tensor_tensor(rank[:, tl], pw[:, 3, NX * first:NX * end].rearrange("p (i e) -> p i e", e=NX), float(NX),
                                              eoff[:].unsqueeze(1).broadcast_to([P, n, NX]), ALU.mult, ALU.add))
                if end == NT:
                    link(dve.tensor_reduce(cols[:, 0, 0:1], pw[:, 3, NX * NT:NX * (NT + 1)], AX.X, ALU.max))
                    link(dve.tensor_scalar(flag[:], cols[:, 0, 0:1], float(CAP), None, ALU.is_gt))
                for c, m_ in enumerate((M1, M2)):
                    pr = prod[:, tl].rearrange("p i g e -> p i (g e)")
                    link(dve.tensor_tensor(pr, m_[:, tl].rearrange("p i g e -> p i (g e)"), rank[:, tl], ALU.mult))
                    link(dve.tensor_reduce(destf[:, c, tl], pr, AX.X, ALU.add))
                dve.tensor_copy(dest[:, :, tl], destf[:, :, tl]).then_inc(s_dest, 1)
                dve.wait_ge(s_dest, b + 1)

            dve.wait_ge(s_rc, 128)
            dve.wait_ge(s_ln, 64)
            for i in range(NT):
                residual(i)
                moments(i, s_var)
                normalize(i, 0, s_x1, s_sd)
                if i == BATCHES[0][1]:
                    route(0)
                if i == BATCHES[0][1] + 1:
                    slots(0)
            route(1)
            slots(1)

            dve.wait_ge(s_x1d, 16 * NT)
            for i in range(NT):
                link(dve.tensor_scalar(xr[:, i, :], xr[:, i, :], ALPHA, None, ALU.mult))

            def expert(n, j, y_prev, ys_prev, si, h_, y_, yc):
                dve.wait_ge(si, n + 1)
                if y_prev is not None:
                    dve.wait_ge(y_, y_prev)
                dve.tensor_tensor(hT[:, j].rearrange("p f t -> p (f t)"), hs[:, j].rearrange("p f t -> p (f t)"),
                                  pw[:, j, 256:512], ALU.mult).then_inc(h_, 1)
                dve.wait_ge(y_, n + 1)
                if ys_prev is not None:
                    dve.wait_ge(m_ys[j], ys_prev)
                dve.tensor_copy(ysb[:, j, :], ppf[1]).then_inc(yc, 1)

            for e in range(4):
                expert(e, e % 2, e - 1 if e >= 2 else None, 16 * (e // 2) if e >= 2 else None, m_si, m_h, m_y, m_yc)
            with dve.Fori(1, NX // 4) as i:
                for j in range(4):
                    expert(4 * i + j, j % 2, 4 * i + (j - 1), 32 * i + 16 * (j // 2), m_si, m_h, m_y, m_yc)
            over = dve.value_load(flag[0:1, 0:1], min_val=0, max_val=1)
            with dve.If(over > 0):
                dve.wait_ge(m_ys[0], 16 * NX // 2)
                with dve.Fori(0, NX * (BLOCKS - 1)) as n:
                    expert(n, 0, None, None, e_si, e_h, e_y, e_yc)

            for i in range(NT):
                r = ROWS[i]
                dve.wait_ge(s_yg[i % 2], 32 * (i // 2 + 1))
                for c in range(2):
                    ins = dve.scalar_tensor_tensor(xr[0:r, i, :], yg[0:r, i % 2, c, :], cols[0:r, 8 + c, i:i + 1], xr[0:r, i, :],
                                                   ALU.mult, ALU.add)
                    if c == 0:
                        link(ins)
                    else:
                        ins.then_inc(s_ygf, 1)
                        dve.wait_ge(s_ygf, i + 1)
                moments(i, s_v2)
                normalize(i, 2, s_out, s_sd2)


def constants():
    import numpy as np
    t = np.arange(P)
    x = t[:, None] ^ t[None, :]
    pairs = np.zeros((P, LEVELS + 1, P), np.float32)
    pairs[:, 0, :] = x == 0
    for l in range(LEVELS):
        pairs[:, l + 1, :] = ((x >> l) == 1) & (t[:, None] < t[None, :])
    reset = np.ones((P, T), np.float32)
    reset[:, ::P] = 0
    small = np.zeros((P, 8), np.float32)
    small[:, 0] = 1e-6
    small[:, 1] = 1e-5
    small[:, 2] = -0.5
    lower = (t[:, None] < t[None, :]).astype(np.float32)
    return {"c_ident": np.eye(P, dtype=np.float32), "c_pairs": pairs, "c_reset": reset,
            "c_lower": lower, "c_small": small,
            "c_eoff": np.tile(np.arange(NX, dtype=np.float32), (P, 1)),
            "c_tid": (np.arange(P, dtype=np.uint32)[:, None] + P * np.arange(NT, dtype=np.uint32)[None, :]),
            "c_order": np.tile(np.arange(4, 0, -1, dtype=np.float32), (P, 1))}


_INS = ("x_prompt", "x_sample", "cache_k", "cache_v", "cache_idx_k", "state_hgrn", "w_in", "hg_norm_w",
        "w_br_hg", "w_br_att", "w_out", "ln1_g", "ln1_b", "ln2_g", "ln2_b", "w_rg", "b_rg", "w_re", "b_re",
        "w_gate", "w_up", "w_down")
_OUTS = ((1, TP, D), (1, TS, D),
         (1, 1, TP, AH, AD), (1, 1, TP, AH, AD), (1, 1, TP, ID), (1, 1, HH, P, P),
         (1, 1, TS, AH, AD), (1, 1, TS, AH, AD), (1, 1, TS, ID), (1, 1, HH, P, P))


def kernel(**inputs):
    import numpy as _np
    import concourse.bacc as _bacc
    from concourse import mybir as _mybir
    from concourse.bass_utils import run_bass_kernel_spmd as _run

    nc = _bacc.Bacc("TRN2", target_bir_lowering=False, num_devices=1)
    source = {name: _np.ascontiguousarray(inputs[name]) for name in _INS}
    source.update(constants())
    arrays, args = {}, []
    for name, a in source.items():
        arrays[f"in_{name}_dram"] = a
        args.append(nc.dram_tensor(f"in_{name}_dram", a.shape, _mybir.dt.from_np(a.dtype), kind="ExternalInput").ap())
    for i, shape in enumerate(_OUTS):
        args.append(nc.dram_tensor(f"out_{i}_dram", shape, F32, kind="ExternalOutput").ap())
    encoder_layer(nc, *args)
    r = _run(nc, [arrays], core_ids=[0])
    return tuple(r.results[0][f"out_{i}_dram"] for i in range(len(_OUTS)))
```

```python
from contextlib import ExitStack

import concourse.bass as bass
from concourse import mybir

F32 = mybir.dt.float32
F32R = mybir.dt.float32r
I32 = mybir.dt.int32
U32 = mybir.dt.uint32
ALU = mybir.AluOpType
ACT = mybir.ActivationFunctionType
AX = mybir.AxisListType

P = 128
D = 1024
KD = D // P
TP, TS = 512, 64
T = TP + TS
HT = T // 2
NT = 5
ROWS = [128, 128, 128, 128, 64]
HH = 4
AH, AD = 8, 64
IH, ID = 4, 64
PAST = 256
NX, F = 16, 256
CAP = 112
BLOCKS = 6
SLOT = BLOCKS * CAP
TOPK = [0, 128, 128, 128, 80]
KEYS = [128, 256, 384, 512, PAST + TS]
MOFF = [0, 0, 256, 640, 1152]
NEG = -3.0e38
BIG = 1.0e30
ALPHA = 2.0 ** 0.25
GW = 256
RAW = 2
RING = 4
AHEAD = RING - 1

C_HQ, C_HF, C_HI, C_HG, C_AQ, C_AK, C_AV, C_IQ, C_IK, C_GH, C_GA = (
    0, 512, 1024, 1536, 2048, 2560, 3072, 3584, 3840, 3908, 4932)

LEVELS = 7


class Count:

    def __init__(self, sem):
        self.sem, self.n = sem, 0

    def by(self, ins):
        self.n += 1
        ins.then_inc(self.sem, 1)
        return self.n


def plan():
    groups, fills = [], []

    def group(kind, col, width, units):
        g = len(groups)
        groups.append((kind, col, width))
        for what in units:
            fills.append((g, what))

    group("in", C_IQ, 256, [("iq", 0), ("iq", 1)])
    group("in", C_IK, 68, [("ik", 0)])
    for j in range(2):
        group("in", C_HF + GW * j, GW, [("hf", 2 * j), ("hf", 2 * j + 1)])
    for j in range(2):
        group("in", C_HI + GW * j, GW, [("hi", 3 * j + p) for p in range(3)])
    for j in range(2):
        group("in", C_HQ + GW * j, GW, [("hq", 2 * j), ("hq", 2 * j + 1)])
    for j in range(2):
        group("in", C_HG + GW * j, GW, [("hg", 2 * j), ("hg", 2 * j + 1)])
    for j in range(8):
        group("in", C_GH + GW * j, GW, [("gate", 2 * j), ("gate", 2 * j + 1)])
    for j in range(2):
        group("in", C_AK + GW * j, GW, [("ak", 2 * j), ("ak", 2 * j + 1)])
    fills += [(None, ("kt", i)) for i in range(NT)]
    for j in range(2):
        group("in", C_AQ + GW * j, GW, [("aq", 2 * j), ("aq", 2 * j + 1)])
    for j in range(2):
        group("in", C_AV + GW * j, GW, [("av", 3 * j + p) for p in range(3)])
    fills += [(None, ("attention", 0))]
    for j in range(4):
        group("branch", GW * j, GW, [("br", 4 * j + n) for n in range(4)])
    for j in range(4):
        group("out", GW * j, GW, [])
    fills += [(None, ("out", i)) for i in range(NT)]
    return groups, fills


STORED = 16 * (2 * HH + 2)
BATCHES = [(0, 2), (2, 5)]
POOL_GAINS = 2
DVE_NORMS = 1
TURNS = {(2, 1): 0, (2, 3): 1, (3, 3): 2, (4, 3): 3}
UNITS = HH * NT


def hgrn_steps(what):
    kind, c = what
    if what == ("gate", 15):
        return [20]
    if what == ("ak", 0):
        return [21]
    return {"hq": [0] if c == 3 else [], "hg": [1 + c], "gate": [5 + c]}.get(kind, [])


def normed_head(k):
    return k // NT - 1 if k >= NT + 1 and k % NT == 1 else None


def prepared_head(k):
    return {6: 2, 11: 3}.get(k)


def encoder_layer(nc, x_prompt, x_sample, cache_k, cache_v, cache_idx_k, state_hgrn, w_in, hg_norm_w,
                  w_br_hg, w_br_att, w_out, ln1_g, ln1_b, ln2_g, ln2_b, w_rg, b_rg, w_re, b_re,
                  w_gate, w_up, w_down, c_ident, c_pairs, c_reset, c_lower, c_small, c_eoff, c_tid, c_order, c_iota, c_tidf,
                  y_prompt, y_sample, nk_p, nv_p, nik_p, ns_p, nk_s, nv_s, nik_s, ns_s):
    groups, fills = plan()
    NG = len(groups)
    fill_of, n = {}, 0
    for _, what in fills:
        if what[0] != "attention":
            fill_of[what] = n
            n += 1
    last_of = {g: what for g, what in fills if g is not None}
    ends_group = lambda g, what: g is not None and last_of[g] == what
    OUT0 = NG - 4
    DVE_LOW = (2, OUT0 + 1, OUT0 + 3)

    gates_d = nc.dram_tensor("gates_d", [16, P, T], F32).ap()
    x1_d = nc.dram_tensor("x1_d", [T, D], F32).ap()
    slot_d = nc.dram_tensor("slot_d", [NX * SLOT, 1], U32).ap()
    ys_d = nc.dram_tensor("ys_d", [NX * SLOT, D], F32).ap()

    with ExitStack() as ctx:
        base = nc.sbuf_base + (-nc.sbuf_base) % 64

        class Area:

            def __init__(self, start):
                self.at = start

            def __call__(self, name, shape, dt=F32):
                n = 4
                for s in shape[1:]:
                    n *= s
                t = nc.alloc_sbuf_tensor_at(name, shape, dt, offset=base + self.at)
                self.at += n + (-n) % 64
                return t

        def sem(name):
            return ctx.enter_context(nc.semaphore(name))

        xa = Area(0)
        xh = xa("x_hi", [P, KD, T], F32R)
        xl = xa("x_lo", [P, KD, T], F32R)
        raw = xa("w_raw", [P, RAW, KD, GW])
        wh = xa("w_hi", [P, 2, KD, GW], F32R)
        wl = xa("w_lo", [P, 2, KD, GW], F32R)
        ident = xa("ident", [P, P])
        ones = xa("ones", [P, P])
        small = xa("small", [P, 8])
        normw = xa("normw", [P, 1])
        route_start = xa.at
        pairs = xa("pairs", [P, LEVELS + 1, P])
        reset = xa("reset", [P, T])
        maskb = xa("maskb", [P, 1472])
        tok4 = xa("tok4", [P, NT, 68])
        wk = xa("wk", [P, 512])
        eq = xa("eq", [P, 512])
        top = xa("top", [P, 8])
        cnt = xa("cnt", [P, 2])
        route_end = xa.at
        gring = xa("gring", [P, 2, T])
        ring_end = xa.at
        o_all = xa("o_all", [P, HH, T])
        S = xa("S", [P, 2, HH, P])
        mixer_end = xa.at
        sbuf_end = nc.sbuf_usable_end - base

        ya = Area(0)
        yh = ya("y_hi", [P, 8, T], F32R)
        yl = ya("y_lo", [P, 8, T], F32R)

        oa = Area(0)
        woh = oa("wo_hi", [P, 2, KD, GW], F32R)
        wol = oa("wo_lo", [P, 2, KD, GW], F32R)

        ha = Area(mixer_end)
        q = ha("q", [P, HH, T])
        kk = ha("kk", [P, HH, T])
        B = ha("B", [P, HH, T])
        L = ha("L", [P, HH, T])
        v = ha("v", [P, NT, 512])
        sg = ha("sg", [P, HH, T])
        kd = [ha("kd", [P, T]), reset]
        Gm = ha("Gm", [P, LEVELS + 1, P])
        AT = ha("AT", [P, 2, P])
        kdT = ha("kdT", [P, 2, P])
        eBT = ha("eBT", [P, 2, NT])
        xoff = ha.at
        X0 = ha("X0", [P, LEVELS, T])
        X1 = ha("X1", [P, LEVELS - HH, T])
        X = [[X0[:, l, :] for l in range(LEVELS)],
             [L[:, l, :] for l in range(HH)] + [X1[:, l, :] for l in range(LEVELS - HH)]]
        assert ha.at <= sbuf_end
        ia = Area(xoff)
        qi = ia("qi", [P, 2, T])
        kiw = ia("kiw", [68, T])
        ki2 = ia("ki2", [P, T])
        kic = ia("kic", [P, 2, 2, ID])
        kicT = ia("kicT", [P, PAST])
        relu = ia("relu", [P, 2, 512])
        xtok_area = Area(mixer_end)
        xtok = xtok_area("xtok", [P, NT, D])

        aa = Area(mixer_end)
        qa = aa("qa", [P, 4, T])
        ka = aa("ka", [P, 4, T])
        va = aa("va", [P, NT, 512])
        kc = aa("kc", [P, 2, 512])
        kcT = aa("kcT", [P, 4, PAST])
        vc = aa("vc", [P, 2, 512])
        Lm = aa("Lm", [P, RING, 512])
        Pr = aa("Pr", [P, RING, 512])
        PT = aa("PT", [P, 2, 4, P])
        ktok = aa("ktok", [P, NT, 512])
        mask0 = aa("mask0", [P, P])
        mx = aa("mx", [P, RING, 4])

        assert aa.at <= sbuf_end - 2 * 2 * T * 4

        ma = Area(mixer_end)
        mh = ma("m_hi", [P, KD, T], F32R)
        ml = ma("m_lo", [P, KD, T], F32R)
        xr = ma("xr", [P, NT, D])
        lnr = ma("lnr", [P, 4, D])
        gsum = ma("gsum", [P, 2, T])
        assert ma.at <= sbuf_end - 2 * 2 * T * 4
        gld = Area(sbuf_end - 2 * 2 * T * 4 - sbuf_end % 64)("gld", [P, 2, 2, T])

        ra = Area(route_start)
        x1T = ra("x1T", [P, 2, KD, P])
        wr = ra("wr", [P, KD, 20])
        br_ = ra("br_", [P, 20])
        lower = ra("lower", [P, P])
        eoff = ra("eoff", [P, NX])
        tid = ra("tid", [P, NT], U32)
        order = ra("order", [P, 4])
        iota = ra("iota", [P, P])
        tidf = ra("tidf", [P, NT, NX])
        Mt = ra("Mt", [P, 2, NT, NX])
        rk = ra("rk", [P, 2, NT])
        es2 = ra("es2", [P, NT, 4])
        ex = ra("ex", [P, NT, 4])
        nmr = ra("nmr", [P, NT])
        zero = ra("zero", [P, NX * SLOT // P], U32)
        stats = ra("stats", [P, NT, 2, 6])
        mv = ra("mv", [P, NT, 2])
        rstd = ra("rstd", [P, NT])
        halfv = ra("halfv", [P, NT])
        newton = ra("newton", [P, NT])
        lg = ra("lg", [P, NT, 20])
        ge = ra("ge", [P, NT, 4])
        gx = ra("gx", [P, NT, 4])
        ohg = ra("ohg", [P, NT, 4])
        taken = ra("taken", [P, NT])
        prod = ra("prod", [P, NT, 4, 4])
        es = ra("es", [P, NT, 4])
        ee = ra("ee", [P, NT, 4])
        oh1 = ra("oh1", [P, NT, 4])
        oh2 = ra("oh2", [P, NT, 4])
        cols = ra("cols", [P, 10, NT])
        M1 = ra("M1", [P, NT, 4, 4])
        M2 = ra("M2", [P, NT, 4, 4])
        M = ra("M", [P, NT, NX])
        before = ra("before", [P, NT + 1, NX])
        destf = ra("destf", [P, 2, NT])
        dest = ra("dest", [P, 2, NT], U32)
        flag = ra("flag", [P, 1], I32)
        stok = ra("stok", [P, NX], U32)
        stokf = ra("stokf", [P, NX])
        stx = ra("stx", [P, 2], U32)
        zcol = ra("zcol", [P, 1], U32)
        zcol2 = ra("zcol2", [P, 1], U32)
        hot = ra("hot", [P, 2, NT, P])
        assert ra.at - 5120 <= route_end and ra.at <= ring_end
        dg = hot
        ea = Area(0)
        xg = ea("xg", [P, 2, D])
        xgT = ea("xgT", [P, 2, KD, CAP])
        hs = ea("hs", [P, 2, 2, CAP])
        hT = ea("hT", [P, 2, 2, CAP])
        ysb = ea("ysb", [P, 2, D])
        yg = Area(0)("yg", [P, NT, 2, D])
        wgu, wd = [], []
        raw_start = 2 * KD * T * 4
        assert ea.at <= raw_start - 2 * D * 4
        for n, (at, down_at) in enumerate(((raw_start, raw_start - 2 * D * 4),
                                           (raw_start + 16384, raw_start + 2 * 16384),
                                           (ring_end, ring_end + 16384),
                                           (ring_end + 24576, ring_end + 24576 + 16384))):
            wgu.append(Area(at)(f"wgu{n}", [P, 2, KD, F]))
            wd.append(Area(down_at)(f"wd{n}", [P, 2, D]))
        assert ring_end + 2 * 24576 <= mixer_end + 2 * KD * T * 4

        pp = ctx.enter_context(nc.psum_tensor("pp", [P, 2, 2, 512], F32))
        pw = ctx.enter_context(nc.psum_tensor("pw", [P, 4, 512], F32))
        ppf = [pp[:, b].rearrange("p a b -> p (a b)") for b in range(2)]

        w_hi = lambda g: wh[:, g % 2] if g < OUT0 + 2 else woh[:, g - OUT0 - 2]
        w_lo = lambda g: wl[:, g % 2] if g < OUT0 + 2 else wol[:, g - OUT0 - 2]
        pwf = [pw[:, 2 * b:2 * b + 2].rearrange("p a b -> p (a b)") for b in range(2)]
        turned_x = [ppf[0], ppf[1], pwf[0], pwf[1], ppf[1]]
        total = lambda i: (xr[:, 0, :], pwf[0], pwf[1], ppf[0], ppf[1])[i]
        logit_bank = lambda a: pp[:, a % 2, a // 2 % 2]

        s_x = [sem(f"s_xin{i}") for i in range(NT)]
        s_const = sem("s_const")
        s_raw = [sem(f"s_raw{i}") for i in range(RAW)]
        s_wh = sem("s_wh")
        s_wl = sem("s_wl")
        s_wlo = sem("s_wlo")
        s_flag = sem("s_flag")
        s_hot = sem("s_hot")
        s_id = sem("s_id")
        s_nmr, s_z, s_zg = sem("s_nmr"), sem("s_z"), sem("s_zg")
        s_lgd = sem("s_lgd")
        s_full = [sem(f"s_full{b}") for b in range(2)]
        s_free = [sem(f"s_free{b}") for b in range(2)]
        s_xh = sem("s_xh")
        s_xl = sem("s_xl")
        s_ones = sem("s_ones")
        d_chain, a_chain = sem("d_chain"), sem("a_chain")
        s_ev = {k: sem("s_ev_" + k) for k in ("iq", "ik", "hf", "hq", "hi", "hg", "gate", "ak", "aq", "av")}
        s_kic = sem("s_kic")
        s_it = sem("s_it")
        s_itc = sem("s_itc")
        s_sc = sem("s_sc")
        s_rl = sem("s_rl")
        s_acc = sem("s_acc")
        s_mask = sem("s_mask")
        s_L = sem("s_L")
        s_g = sem("s_g")
        s_k = sem("s_k")
        s_D = sem("s_D")
        s_X = sem("s_X")
        s_XM = sem("s_XM")
        s_kd = sem("s_kd")
        s_eB = sem("s_eB")
        s_qe = sem("s_qe")
        s_qem = sem("s_qem")
        s_G = sem("s_G")
        s_Gf = sem("s_Gf")
        s_AT = sem("s_AT")
        s_kdt = sem("s_kdt")
        s_ktc = sem("s_ktc")
        s_o = sem("s_o")
        s_of = sem("s_of")
        s_osq = sem("s_osq")
        s_ms = sem("s_ms")
        s_msc = sem("s_msc")
        s_rms = sem("s_rms")
        s_y = sem("s_y")
        s_st = sem("s_st")
        s_gst = [sem(f"s_gst{i}") for i in range(2)]
        s_store = sem("s_store")
        s_kt = sem("s_kt")
        s_kc = sem("s_kc")
        s_sk = sem("s_sk")
        s_ct = sem("s_ct")
        s_ctc = sem("s_ctc")
        s_lg = sem("s_lg")
        s_Lm = sem("s_Lm")
        s_P = sem("s_P")
        s_PT = sem("s_PT")
        s_PTc = sem("s_PTc")
        s_O = sem("s_O")
        s_rd = sem("s_rd")
        s_Pn = sem("s_Pn")
        s_ygh, s_ygl = sem("s_ygh"), sem("s_ygl")
        s_yh = sem("s_yh")
        s_yl = sem("s_yl")
        s_gl = [sem("s_gl0"), sem("s_gl1")]
        s_sig = sem("s_sig")
        s_br = sem("s_br")
        s_m = sem("s_m")
        s_mh = sem("s_mh")
        s_ml = sem("s_ml")
        s_xr = sem("s_xr")
        s_res = sem("s_res")
        s_var = sem("s_var")
        s_sd = sem("s_sd")
        s_x1 = sem("s_x1")
        s_x1d = sem("s_x1d")
        s_rc = sem("s_rc")
        s_zero = sem("s_zero")
        s_zd = sem("s_zd")
        s_tx = sem("s_tx")
        s_txc = sem("s_txc")
        s_logit = sem("s_logit")
        s_ge = sem("s_ge")
        s_gx = sem("s_gx")
        s_M = sem("s_M")
        s_rk = sem("s_rk")
        s_dest = sem("s_dest")
        s_sct = sem("s_sct")
        s_stok = sem("s_stok")
        m_w = [sem(f"m_w{i}") for i in range(4)]
        m_wd = [sem(f"m_wd{i}") for i in range(4)]
        m_g = [sem(f"m_g{i}") for i in range(2)]
        m_t, m_tc, m_gu, m_si, m_h, m_y, m_yc = (sem(n) for n in ("m_t", "m_tc", "m_gu", "m_si", "m_h", "m_y", "m_yc"))
        m_ys = [sem(f"m_ys{i}") for i in range(2)]
        e_pad = sem("e_pad")
        e_i, e_w, e_ix, e_g = sem("e_i"), sem("e_w"), sem("e_ix"), sem("e_g")
        e_t, e_tc, e_gu, e_si, e_h, e_y, e_yc, e_ys = (sem(n) for n in ("e_t", "e_tc", "e_gu", "e_si", "e_h", "e_y", "e_yc", "e_ys"))
        s_yg = [sem(f"s_yg{i}") for i in range(NT)]
        s_dg = sem("s_dg")
        s_v2 = sem("s_v2")
        s_sd2 = sem("s_sd2")
        s_out = sem("s_out")
        s_last = sem("s_last")

        ys_v = ys_d.rearrange("(b s e) d -> e b s d", e=NX, b=BLOCKS)
        slot_v = slot_d.rearrange("(b s e) a -> e b s a", e=NX, b=BLOCKS)
        w_gate_e = w_gate[0].rearrange("g e (k p) f -> (g e) p k f", p=P)
        w_up_e = w_up[0].rearrange("g e (k p) f -> (g e) p k f", p=P)
        w_down_e = w_down[0].rearrange("g e (k p) d -> (g e) p k d", p=P)

        def dram_w(kind, col, width, slot):
            if kind == "in":
                return [(raw[:, slot, :, 0:width], w_in[0].rearrange("(k p) c -> p k c", p=P)[:, :, col:col + width])]
            if kind == "branch":
                return [(raw[:, slot, 0:4, 0:width], w_br_hg[0].rearrange("(k p) c -> p k c", p=P)[:, :, col:col + width]),
                        (raw[:, slot, 4:8, 0:width], w_br_att[0].rearrange("(k p) c -> p k c", p=P)[:, :, col:col + width])]
            return [(raw[:, slot, :, 0:width], w_out[0].rearrange("(k p) c -> p k c", p=P)[:, :, col:col + width])]

        raw_need = []
        sums = [0] * RAW
        for g, (kind, _, _) in enumerate(groups):
            sums[g % RAW] += 32 if kind == "branch" else 16
            raw_need.append(sums[g % RAW])

        def filled(engine, what):
            n = fill_of[what]
            engine.wait_ge(s_full[n % 2], n // 2 + 1)

        def low_ready(engine, g):
            if g in DVE_LOW:
                engine.wait_ge(s_wlo, DVE_LOW.index(g) + 1)
            else:
                engine.wait_ge(s_wl, g + 1 - sum(h < g for h in DVE_LOW))

        def group_used(engine, g):
            filled(engine, last_of[g])

        block = ctx.enter_context(nc.Block())

        @block.sync
        def _(sp):
            xp = x_prompt[0].rearrange("(i p) d -> i p d", p=P)
            sp.dma_start(ident[:], c_ident).then_inc(s_const, 16)
            for i in range(3):
                sp.dma_start(xtok[:, i, :], xp[i]).then_inc(s_x[i], 16)

            def load_group(g):
                if g >= RAW:
                    sp.wait_ge(s_wh, g - RAW + 1)
                    low_ready(sp, g - RAW)
                for dst, src in dram_w(*groups[g], g % RAW):
                    sp.dma_start(dst, src).then_inc(s_raw[g % RAW], 16)

            def load_gates(m):
                sp.dma_start(gld[:, m % 2], gates_d[m:m + 9:8].rearrange("a p t -> p a t")).then_inc(s_gl[m % 2], 16)

            load_group(0)
            sp.dma_start(xtok[:, 3, :], xp[3]).then_inc(s_x[3], 16)
            sp.dma_start(xtok[0:64, 4, :], x_sample[0]).then_inc(s_x[4], 16)
            load_group(1)
            sp.wait_ge(s_xl, NT)
            for dup in range(2):
                sp.dma_start(kic[:, :, dup, :], cache_idx_k[0, 0].rearrange("(j p) d -> p j d", p=P)).then_inc(s_kic, 16)
            sp.dma_start(pairs[:], c_pairs).then_inc(s_const, 16)
            sp.dma_start(reset[:], c_reset).then_inc(s_const, 16)
            sp.dma_start(small[:], c_small).then_inc(s_const, 16)
            sp.dma_start(normw[:], hg_norm_w.rearrange("a d -> d a")).then_inc(s_const, 16)
            load_group(2)
            for g in range(3, NG):
                load_group(g)
                if g == 3:
                    sp.wait_ge(s_ev["ik"], 1)
                    sp.dma_start(ki2[64:128, :], kiw[0:64, :]).then_inc(s_kic, 16)
                    for h in range(HH):
                        sp.dma_start(S[:, 1, h, :], state_hgrn[0, 0, h]).then_inc(s_st, 16)
                if g == 21:
                    sp.wait_ge(s_y, 1)
                    sp.dma_start(kc[:], cache_k[0, 0].rearrange("(j p) h d -> p j (h d)", p=P)).then_inc(s_kc, 16)
                    sp.dma_start(vc[:], cache_v[0, 0].rearrange("(j p) h d -> p j (h d)", p=P)).then_inc(s_kc, 16)
                    for c in range(2):
                        sp.wait_ge(s_gst[c], 16 * 8)
                    load_gates(0)
                    load_gates(1)
                if g == 22:
                    sp.wait_ge(s_of, UNITS)
                    for h in range(HH):
                        sp.dma_start(ns_p[0, 0, h], S[:, 0, h, :]).then_inc(s_store, 16)
                        sp.dma_start(ns_s[0, 0, h], S[:, 1, h, :]).then_inc(s_store, 16)
                    sp.dma_start(nik_p[0, 0].rearrange("(i p) c -> p i c", p=P), tok4[:, 0:4, 0:64]).then_inc(s_store, 16)
                    sp.dma_start(nik_s[0, 0], tok4[0:64, 4, 0:64]).then_inc(s_store, 16)
                if g == 24:
                    sp.wait_ge(s_kt, NT)
                    sp.dma_start(nk_p[0, 0].rearrange("(i p) h d -> p i (h d)", p=P), ktok[:, 0:4, :]).then_inc(s_sk, 16)
                    sp.dma_start(nk_s[0, 0].rearrange("s h d -> s (h d)"), ktok[0:64, 4, :]).then_inc(s_sk, 16)
                    sp.wait_ge(s_ev["av"], 6)
                    sp.dma_start(nv_p[0, 0].rearrange("(i p) h d -> p i (h d)", p=P), va[:, 0:4, :]).then_inc(s_sk, 16)
                    sp.dma_start(nv_s[0, 0].rearrange("s h d -> s (h d)"), va[0:64, 4, :]).then_inc(s_sk, 16)
                if g == 27:
                    sp.wait_ge(s_yl, NT)
                    sp.wait_ge(s_sk, 64)
                    sp.dma_start(xr[:, 0:4, :], x_prompt[0].rearrange("(i p) d -> p i d", p=P)).then_inc(s_xr, 16)
                    sp.dma_start(xr[0:64, 4, :], x_sample[0]).then_inc(s_xr, 16)
                    for n, row in enumerate((ln1_g, ln1_b, ln2_g, ln2_b)):
                        sp.dma_start(lnr[:, n, :], row.broadcast_to([P, D])).then_inc(s_xr, 16)

            sp.wait_ge(s_store, STORED)
            for dst, src in ((wr[:, :, 0:4], w_rg[0].rearrange("(k p) c -> p k c", p=P)),
                             (wr[:, :, 4:20], w_re[0].rearrange("(k p) c -> p k c", p=P)),
                             (br_[:, 0:4], b_rg.broadcast_to([P, 4])), (br_[:, 4:20], b_re.broadcast_to([P, 16])),
                             (lower[:], c_lower), (eoff[:], c_eoff), (tid[:], c_tid), (order[:], c_order),
                             (iota[:], c_iota), (tidf[:], c_tidf)):
                sp.dma_start(dst, src).then_inc(s_rc, 16)

            def expert_gate_up(e, j):
                sp.dma_start(wgu[j][:, 0], w_gate_e[e]).then_inc(m_w[j], 16)
                sp.dma_start(wgu[j][:, 1], w_up_e[e]).then_inc(m_w[j], 16)

            def expert_down(e, j):
                sp.dma_start(wd[j][:], w_down_e[e]).then_inc(m_wd[j], 16)

            def store_x1(i):
                sp.wait_ge(s_x1, i + 1)
                sp.dma_start(x1_d[i * P:i * P + ROWS[i]], xr[0:ROWS[i], i, :]).then_inc(s_x1d, 16)

            sp.wait_ge(s_wh, NG)
            for g in (NG - 2, NG - 1):
                low_ready(sp, g)
            expert_gate_up(0, 0)
            for i in range(NT - 1):
                store_x1(i)
            filled(sp, ("out", NT - 1))
            expert_down(0, 0)
            expert_gate_up(1, 1)
            store_x1(NT - 1)
            expert_down(1, 1)
            expert_gate_up(2, 2)
            expert_down(2, 2)
            for j in range(2):
                sp.wait_ge(m_g[j], 16)
            expert_gate_up(3, 3)
            expert_down(3, 3)
            def store_y(e, j):
                sp.dma_start(ys_v[e, 0], ysb[0:CAP, j, :]).then_inc(m_ys[j], 16)

            with sp.Fori(1, NX // 4) as i:
                for j in range(4):
                    sp.wait_ge(m_gu, 4 * i + (j - 3))
                    expert_gate_up(4 * i + j, j)
                    sp.wait_ge(m_y, 4 * i + (j - 3))
                    expert_down(4 * i + j, j)
                    sp.wait_ge(m_yc, 4 * i + (j - 3))
                    store_y(4 * i + (j - 4), j % 2)
            for e in range(NX - 4, NX):
                sp.wait_ge(m_yc, e + 1)
                store_y(e, e % 2)
            sp.wait_ge(s_flag, 1)
            over = sp.value_load(flag[0:1, 0:1], min_val=0, max_val=1)
            with sp.If(over > 0):
                sp.wait_ge(s_zero, 2)
                sp.dma_start(slot_d.rearrange("(p n) a -> p (n a)", p=P), zero[:]).then_inc(s_zd, 16)
                sp.wait_ge(s_sct, 16 * 2 * NT)
                sp.wait_ge(m_y, NX)
                sp.wait_ge(m_ys[0], 16 * NX // 2)
                sp.wait_ge(m_ys[1], 16 * NX // 2)
                with sp.Fori(0, NX) as e:
                    for k in range(1, BLOCKS):
                        n = (BLOCKS - 1) * e + k
                        sp.wait_ge(e_i, n)
                        sp.dma_start(wgu[0][:, 0], w_gate_e[e]).then_inc(e_w, 16)
                        sp.dma_start(wgu[0][:, 1], w_up_e[e]).then_inc(e_w, 16)
                        sp.dma_start(wd[0][:], w_down_e[e]).then_inc(e_w, 16)
                        sp.dma_start(stx[0:CAP, 0:1], slot_v[e, k], allow_slow_non_contiguous=True).then_inc(e_w, 16)
                        sp.wait_ge(e_yc, n)
                        sp.dma_start(ys_v[e, k], ysb[0:CAP, 0, :]).then_inc(e_ys, 16)
                        sp.wait_ge(e_ys, 16 * n)
                        sp.sem_inc(e_pad, 1)
            for i in range(NT):
                if i < NT - DVE_NORMS:
                    sp.wait_ge(s_out, i + 1)
                else:
                    sp.wait_ge(s_last, i + 1 - (NT - DVE_NORMS))
                dst = y_prompt[0, i * P:(i + 1) * P] if i < 4 else y_sample[0]
                sp.dma_start(dst, xr[0:ROWS[i], i, :]).then_inc(s_store, 16)
            sp.wait_ge(s_store, STORED + 16 * NT)
            sp.wait_ge(s_sk, 16 * 4)

        @block.tensor
        def _(pe):
            pe.wait_ge(s_const, 16)

            def open_fill(n):
                b = n % 2
                if n >= 2:
                    pe.wait_ge(s_free[b], n // 2)
                return b

            def transpose_x(i):
                pe.wait_ge(s_x[i], 16)
                if i == NT - 1:
                    pe.wait_ge(s_xl, 2)
                r = ROWS[i]
                for k in range(KD):
                    mm = pe.transpose(turned_x[i][:, k * P:k * P + r], xtok[0:r, i, k * P:(k + 1) * P], ident[0:r, 0:r])
                mm.then_inc(s_tx, 1)

            def columns(lhs_h, lhs_l, rhs_h, rhs_l, ks, b):
                for x, k in enumerate(ks):
                    for y, (lw, rx) in enumerate(((lhs_h, rhs_h), (lhs_h, rhs_l), (lhs_l, rhs_h))):
                        for half in range(2):
                            mm = pe.matmul(pp[0:lw(k).shape[1], b, half, 0:HT], lw(k), rx(k, half),
                                           start=(x == 0 and y == 0), stop=(x == len(ks) - 1 and y == 2))
                return mm

            def first_columns(width):
                pe.wait_ge(s_wh, 1)
                pe.wait_ge(s_xh, NT)
                for y, (lw, rx) in enumerate(((wh, xh), (wh, xl), (wl, xh))):
                    if y == 1:
                        pe.wait_ge(s_xl, NT)
                    if y == 2:
                        low_ready(pe, 0)
                    for k in range(KD):
                        for half in range(2):
                            mm = pe.matmul(pp[0:width, 0, half, 0:HT], lw[:, 0, k, 0:width], rx[:, k, half * HT:(half + 1) * HT],
                                           start=(y == 0 and k == 0), stop=(y == 2 and k == KD - 1))
                mm.then_inc(s_full[0], 1)

            def fill(n, g, what):
                kind, c = what
                slot = g % 2
                b = open_fill(n)
                if kind in ("iq", "ik", "hf", "hq", "hg", "gate", "ak", "aq"):
                    lo = 0 if kind == "ik" else P * (c % 2)
                    hi = lo + (68 if kind == "ik" else P)
                    mm = columns(lambda k: wh[:, slot, k, lo:hi], lambda k: wl[:, slot, k, lo:hi],
                                 lambda k, h: xh[:, k, h * HT:(h + 1) * HT],
                                 lambda k, h: xl[:, k, h * HT:(h + 1) * HT], range(KD), b)
                elif kind == "br":
                    lo = P * (c // 2 % 2)
                    k0 = 4 * (c % 2)
                    if c == 0:
                        pe.wait_ge(s_Lm, NT * AH)
                        pe.wait_ge(s_ygh, HH)
                        pe.wait_ge(s_ygl, HH)
                    if c == 1:
                        pe.wait_ge(s_yh, NT)
                        pe.wait_ge(s_yl, NT)
                    mm = columns(lambda k: wh[:, slot, k, lo:lo + P], lambda k: wl[:, slot, k, lo:lo + P],
                                 lambda k, h: yh[:, k, h * HT:(h + 1) * HT],
                                 lambda k, h: yl[:, k, h * HT:(h + 1) * HT], range(k0, k0 + 4), b)
                elif kind in ("hi", "av"):
                    for i in range(2 * (c % 3), min(2 * (c % 3) + 2, NT)):
                        r = ROWS[i]
                        for k in range(KD):
                            for y, (lx, rw) in enumerate(((xh, wh), (xl, wh), (xh, wl))):
                                mm = pe.matmul(pp[0:r, b, i % 2, 0:GW], lx[:, k, i * P:i * P + r], rw[:, slot, k, :],
                                               start=(k == 0 and y == 0), stop=(k == KD - 1 and y == 2))
                mm.then_inc(s_full[b], 1)
                return mm

            def index_transposes():
                pe.wait_ge(s_kic, 32)
                for j in range(2):
                    mm = pe.transpose(pw[:, 2, j * P:(j + 1) * P], kic[:, j].rearrange("p a b -> p (a b)"), ident[:])
                mm.then_inc(s_it, 1)
                pe.wait_ge(s_ev["ik"], 1)
                for i in range(NT):
                    r = ROWS[i]
                    mm = pe.transpose(pw[0:r, 3, i * 68:(i + 1) * 68], kiw[:, i * P:i * P + r], ident[0:68, 0:68])
                mm.then_inc(s_it, 1)

            def index_scores(n, i):
                for ih in range(IH):
                    s = 4 * n + ih
                    if s >= 2:
                        pe.wait_ge(s_rl, s - 1)
                    lo = 64 * (ih % 2)
                    r = ROWS[i]
                    ql = qi[lo:lo + 64, ih // 2, i * P:i * P + r]
                    kt = ki2 if ih % 2 else kiw
                    if ih % 2:
                        pe.wait_ge(s_kic, 48)
                    out = pw[0:r, s % 2, :]
                    if i < 4:
                        mm = pe.matmul(out[:, 0:KEYS[i]], ql, kt[lo:lo + 64, 0:KEYS[i]], start=True, stop=True)
                    else:
                        pe.matmul(out[:, 0:PAST], ql, kicT[lo:lo + 64, :], start=True, stop=True)
                        mm = pe.matmul(out[:, PAST:PAST + TS], ql, kt[lo:lo + 64, TP:T], start=True, stop=True)
                    mm.then_inc(s_sc, 1)

            def hgrn_pairs(u):
                h, c = u // NT, u % NT
                cs, cw = c * P, ROWS[c]
                nl = LEVELS if c < 4 else LEVELS - 1
                if u == 0:
                    pe.wait_ge(s_rl, 16)
                    pe.wait_ge(s_itc, 2)
                else:
                    pe.wait_ge(s_Gf, u)
                if c == 0:
                    pe.wait_ge(s_XM, 14 * h + 14)
                    pe.wait_ge(s_qem, 2 * h + 2)
                if c == 1 and h >= 1:
                    pe.wait_ge(s_msc, h)
                G = pw[:, 0:2, :].rearrange("p a (b c) -> p (a b) c", c=P)
                pe.matmul(G[0:cw, 0, 0:cw], kk[:, h, cs:cs + cw], q[:, h, cs:cs + cw], start=True, stop=True)
                for l in range(nl):
                    xx = X[h % 2][l][:, cs:cs + cw]
                    mm = pe.matmul(G[0:cw, l + 1, 0:cw], xx, xx, start=True, stop=True)
                mm.then_inc(s_G, 1)
                if u >= 1:
                    pe.wait_ge(s_ktc, u)
                pe.transpose(pw[0:cw, 2, 0:P], kd[h % 2][:, cs:cs + cw], ident[:]).then_inc(s_kdt, 1)

            def hgrn_out(u):
                h, c = u // NT, u % NT
                cs, cw = c * P, ROWS[c]
                pe.wait_ge(s_AT, u + 1)
                if u >= 1:
                    pe.wait_ge(s_of, u)
                if c == 4:
                    pe.wait_ge(s_st, 64)
                vv = v[0:cw, c, h * P:(h + 1) * P]
                group = 0 if c < 4 else 1
                pe.matmul(pw[:, 3, 0:cw], vv, AT[0:cw, u % 2, 0:cw], start=True, stop=(c == 0))
                if c > 0:
                    pe.matmul(pw[:, 3, 0:cw], S[:, group, h, :], B[:, h, cs:cs + cw], start=False, stop=True)
                pe.wait_ge(s_ktc, u + 1)
                pe.matmul(pw[:, 3, 256:384], kdT[0:cw, u % 2, :], vv, start=True, stop=True).then_inc(s_o, 1)

            def hgrn_square(h):
                pe.wait_ge(s_osq, h + 1)
                pe.wait_ge(s_Gf, min(NT * (h + 1) + 1, UNITS))
                for half in range(2):
                    mm = pe.matmul(pw[:, half, 0:HT], ones[:], X[h % 2][1][:, half * HT:(half + 1) * HT], start=True, stop=True)
                mm.then_inc(s_ms, 1)

            def hgrn_step(k):
                if normed_head(k) is not None:
                    hgrn_square(normed_head(k))
                if 1 <= k <= UNITS:
                    hgrn_out(k - 1)
                if k < UNITS:
                    hgrn_pairs(k)

            for i in range(NT):
                transpose_x(i)
            def key_rows(i):
                n = fill_of[("kt", i)]
                b = open_fill(n)
                pe.wait_ge(s_ev["ak"], 4)
                r = ROWS[i]
                for c in range(4):
                    mm = pe.transpose(ppf[b][0:r, c * P:(c + 1) * P], ka[:, c, i * P:i * P + r], ident[:])
                mm.then_inc(s_full[b], 1)

            def cache_keys():
                for j in range(2):
                    pe.wait_ge(s_kc, 32)
                    pe.wait_ge(s_msc, HH)
                    for c in range(4):
                        mm = pe.transpose(pw[:, j, c * P:(c + 1) * P], kc[:, j, c * P:(c + 1) * P], ident[:])
                    mm.then_inc(s_ct, 1)

            def logits(a):
                i, h = a // AH, a % AH
                r, lo, w = ROWS[i], 64 * (h % 2), KEYS[i]
                if a == 0:
                    pe.wait_ge(s_ctc, 2)
                    pe.wait_ge(s_ev["aq"], 4)
                if a < RING:
                    n = fill_of[("br", 0)]
                    n += (a - n) % 2
                    pe.wait_ge(s_free[n % 2], n // 2)
                else:
                    pe.wait_ge(s_Lm, a - RING + 1)
                ql = qa[lo:lo + 64, h // 2, i * P:i * P + r]
                out = logit_bank(a)[0:r]
                if i < 4:
                    mm = pe.matmul(out[:, 0:w], ql, ka[lo:lo + 64, h // 2, 0:w], start=True, stop=True)
                else:
                    pe.matmul(out[:, 0:PAST], ql, kcT[lo:lo + 64, h // 2, :], start=True, stop=True)
                    mm = pe.matmul(out[:, PAST:w], ql, ka[lo:lo + 64, h // 2, TP:T], start=True, stop=True)
                mm.then_inc(s_lg, 1)

            def key_parts(i):
                return [(j * P, min(P, KEYS[i] - j * P)) for j in range((KEYS[i] + P - 1) // P)]

            def turn(a):
                i = a // AH
                r = ROWS[i]
                pe.wait_ge(s_Pn, a + 1)
                if a >= 2:
                    pe.wait_ge(s_PTc, a - 1)
                for j, (at, w) in enumerate(key_parts(i)):
                    mm = pe.transpose(pw[0:w, a % 2, j * P:j * P + r], Pr[0:r, a % RING, at:at + w], ident[0:r, 0:r])
                mm.then_inc(s_PT, 1)

            def values(a):
                i, h = a // AH, a % AH
                r, lo = ROWS[i], AD * (h % 2)
                pe.wait_ge(s_PTc, a + 1)
                if a == 0:
                    pe.wait_ge(s_kc, 32)
                    pe.wait_ge(s_ev["av"], 6)
                if h == 0 and i >= 2:
                    pe.wait_ge(s_yl, i - 1)
                parts = key_parts(i)
                for j, (at, w) in enumerate(parts):
                    vv = va[0:w, j if i < 4 else 4, h * AD:(h + 1) * AD] if i < 4 or j == 2 else vc[:, j, h * AD:(h + 1) * AD]
                    mm = pe.matmul(pw[lo:lo + AD, 2 + i % 2, h // 2 * P:h // 2 * P + r], vv, PT[0:w, a % 2, j, 0:r],
                                   start=(j == 0), stop=(j == len(parts) - 1))
                mm.then_inc(s_O, 1)

            def attention():
                NA = NT * AH
                for a in range(NA + AHEAD + 1):
                    if a < NA:
                        logits(a)
                    if 0 <= a - AHEAD < NA:
                        turn(a - AHEAD)
                    if a - AHEAD - 1 >= 0:
                        values(a - AHEAD - 1)

            def out_group(i, j):
                n = fill_of[("out", i)]
                b, r = n % 2, ROWS[i]
                if j == 0:
                    open_fill(n)
                if i == 0:
                    weights_ready(OUT0 + j)
                if (i, j) in TURNS:
                    turn_x1(TURNS[i, j])
                for k in range(KD):
                    if i == 0 and j == 0:
                        pe.wait_ge(s_mh, k + 1)
                        pe.wait_ge(s_ml, k + 1)
                    for y, (lx, rw) in enumerate(((mh, w_hi), (ml, w_hi), (mh, w_lo))):
                        mm = pe.matmul(pp[0:r, b, j // 2, GW * (j % 2):GW * (j % 2 + 1)], lx[:, k, i * P:i * P + r],
                                       rw(OUT0 + j)[:, k, :], start=(k == 0 and y == 0), stop=(k == KD - 1 and y == 2))
                if j == 3:
                    mm.then_inc(s_full[b], 1)

            def turn_x1(i):
                pe.wait_ge(s_x1, i + 1)
                if i == 0:
                    pe.wait_ge(s_rc, 160)
                    pe.wait_ge(s_yl, NT)
                else:
                    pe.wait_ge(s_txc, i)
                for k in range(KD):
                    mm = pe.transpose(pw[:, k // 4, k % 4 * P:(k % 4 + 1) * P], xr[:, i, k * P:(k + 1) * P], ident[:])
                mm.then_inc(s_tx, 1)

            def router(i):
                pe.wait_ge(s_txc, i + 1)
                for b, (first, _) in enumerate(BATCHES):
                    if b and i == first:
                        pe.wait_ge(s_lgd, b)
                for k in range(KD):
                    mm = pe.matmul(pw[:, 2, 20 * i:20 * i + 20], x1T[:, i % 2, k, :], wr[:, k, :], start=(k == 0), stop=(k == KD - 1))
                mm.then_inc(s_logit, 1)

            def slot_tokens(b):
                first, end = BATCHES[b]
                pe.wait_ge(s_hot, b + 1)
                for i in range(first, end):
                    for c in range(2):
                        mm = pe.matmul(pw[:, 3, 256 + NX * b:256 + NX * (b + 1)], hot[:, c, i, :], Mt[:, c, i, :],
                                       start=(i == first and c == 0), stop=(i == end - 1 and c == 1))
                mm.then_inc(s_id, 1)

            def ranks(b):
                first, end = BATCHES[b]
                pe.wait_ge(s_M, b + 1)
                if b:
                    pe.wait_ge(s_hot, b)
                at, upto = NX * first, NX * end
                flat = lambda t: t.rearrange("p i e -> p (i e)")
                if first == 0:
                    pe.matmul(pw[:, 3, at:NX], lower[:], M[:, 0, :], start=True, stop=True)
                    first, at = 1, NX
                pe.matmul(pw[:, 3, at:upto], lower[:], flat(M[:, first:end, :]), start=True, stop=False)
                mm = pe.matmul(pw[:, 3, at:upto], ones[:], flat(before[:, first:end, :]), start=False, stop=True)
                if end == NT:
                    mm = pe.matmul(pw[:, 3, upto:upto + NX], ones[:], before[:, NT, :], start=True, stop=True)
                mm.then_inc(s_rk, 1)

            def weights_ready(g):
                pe.wait_ge(s_wh, g + 1)
                low_ready(pe, g)

            for n, (g, what) in enumerate(fills):
                if what[0] == "out":
                    break
                if what[0] == "kt":
                    key_rows(what[1])
                    if what[1] == NT - 1:
                        cache_keys()
                    continue
                if what[0] == "attention":
                    attention()
                    continue
                if n == 0:
                    first_columns(P)
                    continue
                if fills[n - 1][0] != g:
                    weights_ready(g)
                fill(fill_of[what], g, what)
                if what == ("hf", 0):
                    index_transposes()
                if what == ("hf", 1):
                    pe.wait_ge(s_itc, 2)
                    pe.wait_ge(s_ev["iq"], 2)
                    index_scores(0, 3)
                    index_scores(1, 4)
                if what == ("hf", 3):
                    index_scores(2, 2)
                    index_scores(3, 1)
                for k in hgrn_steps(what):
                    hgrn_step(k)

            for i in range(NT):
                for t, j in {0: [(0, 0), (1, 0), (0, 1), (1, 1), (0, 2), (0, 3)], 1: [(1, 2), (1, 3)]}.get(i, [(i, j) for j in range(4)]):
                    out_group(t, j)
                if i == 2:
                    router(0)
                if i >= 2:
                    router(i - 1)
                if i == BATCHES[0][1] + 1:
                    ranks(0)
            slot_tokens(0)
            turn_x1(NT - 1)
            router(NT - 1)
            ranks(1)
            slot_tokens(1)

            def gate_up(out, w, xT):
                for half in range(2):
                    for f in range(2):
                        for k in range(KD):
                            mm = pe.matmul(out[:, (2 * half + f) * CAP:(2 * half + f + 1) * CAP], w[:, half, k, f * P:(f + 1) * P],
                                           xT[:, k, :], start=(k == 0), stop=(k == KD - 1))
                return mm

            def down(h_, w):
                for half in range(2):
                    for f in range(2):
                        mm = pe.matmul(ppf[1][0:CAP, half * 512:(half + 1) * 512], h_[:, f, :], w[:, f, half * 512:(half + 1) * 512],
                                       start=(f == 0), stop=(f == 1))
                return mm

            def expert(i, j, e):
                later = not isinstance(i, int)
                pe.wait_ge(m_g[j % 2], 32 * i + 16 * (j // 2 + 1))
                if later or j >= 1:
                    pe.wait_ge(m_tc, e)
                for k in range(KD):
                    mm = pe.transpose(ppf[0][:, k * P:k * P + CAP], xg[0:CAP, j % 2, k * P:(k + 1) * P], ident[0:CAP, 0:CAP])
                mm.then_inc(m_t, 1)
                if later or j >= 1:
                    pe.wait_ge(m_h, e)
                    pe.wait_ge(m_wd[(j - 1) % 4], 16 * i + (16 if j else 0))
                    if later or j >= 2:
                        pe.wait_ge(m_yc, 4 * i + (j - 1))
                    down(hT[:, (j - 1) % 2], wd[(j - 1) % 4]).then_inc(m_y, 1)
                pe.wait_ge(m_w[j], 32 * i + 32)
                pe.wait_ge(m_tc, 4 * i + (j + 1))
                gate_up(pw[:, j % 2], wgu[j], xgT[:, j % 2]).then_inc(m_gu, 1)

            for j in range(4):
                expert(0, j, j)
            with pe.Fori(1, NX // 4) as i:
                for j in range(4):
                    expert(i, j, 4 * i + j)
            pe.wait_ge(m_h, NX)
            pe.wait_ge(m_wd[3], 16 * NX // 4)
            pe.wait_ge(m_yc, NX - 1)
            down(hT[:, 1], wd[3]).then_inc(m_y, 1)
            over = pe.value_load(flag[0:1, 0:1], min_val=0, max_val=1)
            with pe.If(over > 0):
                pe.wait_ge(m_yc, NX)
                with pe.Fori(0, NX * (BLOCKS - 1)) as n:
                    pe.wait_ge(e_g, 16 * n + 16)
                    for k in range(KD):
                        mm = pe.transpose(ppf[0][:, k * P:k * P + CAP], xg[0:CAP, 0, k * P:(k + 1) * P], ident[0:CAP, 0:CAP])
                    mm.then_inc(e_t, 1)
                    pe.wait_ge(e_w, 64 * n + 64)
                    pe.wait_ge(e_tc, n + 1)
                    gate_up(pw[:, 0], wgu[0], xgT[:, 0]).then_inc(e_gu, 1)
                    pe.wait_ge(e_h, n + 1)
                    down(hT[:, 0], wd[0]).then_inc(e_y, 1)
                pe.wait_ge(e_yc, NX * (BLOCKS - 1))

            def residual(i):
                r = ROWS[i]
                for half in range(2):
                    pe.matmul(total(i)[0:r, half * 512:(half + 1) * 512], ident[0:r, 0:r], xr[0:r, i, half * 512:(half + 1) * 512],
                              start=True, stop=False)

            def results(i):
                r = ROWS[i]
                pe.wait_ge(s_dg, NT + 2 * i)
                pe.wait_ge(s_yg[i], 32)
                for c in range(2):
                    for half in range(2):
                        mm = pe.matmul(total(i)[0:r, half * 512:(half + 1) * 512], dg[0:r, c, i, 0:r],
                                       yg[0:r, i, c, half * 512:(half + 1) * 512], start=False, stop=(c == 1))
                mm.then_inc(s_tx, 1)

            pe.wait_ge(s_dg, NT)
            pe.wait_ge(m_yc, NX)
            pe.wait_ge(m_ys[1], 16 * NX // 2)
            for i in range(1, NT):
                residual(i)
            for i in range(1, NT):
                results(i)

        @block.scalar
        def _(act):
            chain = Count(a_chain)

            def link(ins):
                act.wait_ge(a_chain, chain.by(ins))

            def cut(g):
                act.wait_ge(s_raw[g % RAW], raw_need[g])
                if g >= 2:
                    group_used(act, min(g - 2, OUT0 - 1))
                width = groups[g][2]
                act.activation(w_hi(g)[:, :, 0:width], raw[:, g % RAW, :, 0:width], ACT.Copy).then_inc(s_wh, 1)

            def evacuate(what):
                kind, c = what
                n = fill_of[what]
                b = n % 2
                act.wait_ge(s_full[b], n // 2 + 1)
                src = pp[:, b, :, 0:HT]
                two = lambda t: t.rearrange("p (a b) -> p a b", a=2)
                func = ACT.Copy
                if kind in ("ak", "aq"):
                    if c == 0 and kind == "ak":
                        act.wait_ge(s_o, UNITS)
                    dst = two((ka if kind == "ak" else qa)[:, c, :])
                elif kind == "iq":
                    dst = two(qi[:, c, :])
                elif kind == "ik":
                    src, dst = pp[0:68, b, :, 0:HT], two(kiw[:, :])
                elif kind == "hf":
                    dst = two(B[:, c, :])
                elif kind == "hq":
                    dst, func = two(q[:, c, :]), ACT.Silu
                elif kind == "hg":
                    dst, func = two(sg[:, c, :]), ACT.Silu
                elif kind == "gate":
                    if c >= 2:
                        act.wait_ge(s_gst[c % 2], 16 * (c // 2))
                    dst = two(gring[:, c % 2, :])
                elif kind in ("hi", "av"):
                    t = v if kind == "hi" else va
                    i, cc = 2 * (c % 3), GW * (c // 3)
                    if i < 4:
                        src, dst = pp[:, b, :, 0:GW], t[:, i:i + 2, cc:cc + GW]
                    else:
                        src, dst = pp[0:64, b, 0, 0:GW], t[0:64, 4, cc:cc + GW]
                ev = act.activation(dst, src, func)
                ev.then_inc(s_ev[kind], 1)
                act.wait_ge(s_ev[kind], c + 1)
                act.nop().then_inc(s_free[b], 1)
                if kind == "gate":
                    act.dma_start(gates_d[c], gring[:, c % 2, :]).then_inc(s_gst[c % 2], 16)

            def x_high(i):
                act.wait_ge(s_tx, i + 1)
                act.activation(xh[:, :, i * P:i * P + ROWS[i]], turned_x[i].rearrange("p (k t) -> p k t", k=KD)[:, :, 0:ROWS[i]],
                               ACT.Copy).then_inc(s_xh, 1)

            def index_copies():
                act.wait_ge(s_it, 1)
                act.activation(kicT[:], pw[:, 2, 0:PAST], ACT.Copy).then_inc(s_itc, 1)
                act.wait_ge(s_it, 2)
                act.activation(tok4[:, 0:4, :], pw[:, 3, 0:272].rearrange("p (i c) -> p i c", c=68), ACT.Copy).then_inc(a_chain, 1)
                chain.n += 1
                act.activation(tok4[0:64, 4, :], pw[0:64, 3, 272:340], ACT.Copy).then_inc(s_itc, 1)

            def index_relu(n, i):
                r = ROWS[i]
                for ih in range(IH):
                    s = 4 * n + ih
                    act.wait_ge(s_sc, s + 1)
                    if s >= 2:
                        act.wait_ge(s_acc, s - 1)
                    act.activation(relu[0:r, s % 2, 0:KEYS[i]], pw[0:r, s % 2, 0:KEYS[i]], ACT.Relu, scale=ID ** -0.5).then_inc(s_rl, 1)

            def softplus(h):
                act.wait_ge(s_ev["hf"], h + 2)
                z, l = B[:, h:h + 2, :], L[:, h:h + 2, :]
                link(act.activation(l, z, ACT.Abs))
                link(act.activation(l, l, ACT.Exp, scale=-1.0))
                act.activation(l, l, ACT.Ln, bias=1.0).then_inc(s_L, 1)

            def key(h):
                act.wait_ge(s_g, 2 * h + 1)
                act.activation(kk[:, h, :], kk[:, h, :], ACT.Exp, scale=-1.0).then_inc(s_k, 1)

            def levels(h):
                for l in range(LEVELS):
                    act.wait_ge(s_D, 14 * h + 2 * l + 2)
                    w = TP if l == LEVELS - 1 else T
                    act.activation(X[h % 2][l][:, 0:w], X[h % 2][l][:, 0:w], ACT.Exp).then_inc(s_X, 1)
                if h == 1:
                    act.wait_ge(s_g, 2 * HH)
                if h >= 2:
                    act.wait_ge(s_kdt, NT * (h - 1))
                    act.wait_ge(s_of, NT * (h - 1))
                for c in range(NT):
                    cs, cw = c * P, ROWS[c]
                    e = act.activation(kd[h % 2][:, cs:cs + cw], B[:, h, cs:cs + cw], ACT.Exp, scale=-1.0,
                                       bias=B[:, h, cs + cw - 1:cs + cw])
                e.then_inc(s_kd, 1)
                act.activation(eBT[:, h % 2, 0:4], B[:, h, P - 1:TP:P], ACT.Exp)
                act.activation(eBT[:, h % 2, 4:5], B[:, h, T - 1:T], ACT.Exp).then_inc(s_eB, 1)
                act.wait_ge(s_kd, h + 1)
                act.wait_ge(s_eB, h + 1)
                act.activation(B[:, h, :], B[:, h, :], ACT.Exp).then_inc(s_qe, 1)

            def kd_copy(u):
                cw = ROWS[u % NT]
                act.wait_ge(s_kdt, u + 1)
                if u >= 2:
                    act.wait_ge(s_o, u - 1)
                act.activation(kdT[0:cw, u % 2, :], pw[0:cw, 2, 0:P], ACT.Copy).then_inc(s_ktc, 1)

            def square_copy(h):
                act.wait_ge(s_ms, h + 1)
                act.activation(q[:, h, :].rearrange("p (a b) -> p a b", a=2), pw[:, 0:2, 0:HT], ACT.Copy).then_inc(s_msc, 1)

            def head_norms():
                act.wait_ge(s_msc, HH)
                link(act.activation(q[:, :, :], q[:, :, :], ACT.Ln, scale=1.0 / P, bias=small[:, 0:1]))
                act.activation(q[:, :, :], q[:, :, :], ACT.Exp, scale=-0.5).then_inc(s_rms, 1)

            def hgrn_step(k):
                if prepared_head(k - 1) is not None:
                    levels(prepared_head(k - 1))
                if k < UNITS:
                    kd_copy(k)
                if k == UNITS + 1:
                    head_norms()

            for i in range(NT):
                x_high(i)
                if i == 1:
                    cut(0)
            cut(1)
            act.wait_ge(s_const, 80)
            def cached_keys():
                for j in range(2):
                    act.wait_ge(s_ct, j + 1)
                    act.activation(kcT[:, :, j * P:(j + 1) * P], pw[:, j, :].rearrange("p (c t) -> p c t", c=4), ACT.Copy).then_inc(s_ctc, 1)

            def probs(a):
                i = a // AH
                r, w = ROWS[i], KEYS[i]
                act.wait_ge(s_Lm, a + 1)
                if a >= RING:
                    act.wait_ge(s_PT, a - RING + 1)
                act.activation(Pr[0:r, a % RING, 0:w], Lm[0:r, a % RING, 0:w], ACT.Exp, scale=-1.0,
                               bias=mx[0:r, a % RING, 1:2], accum_out=mx[0:r, a % RING, 2:3]).then_inc(s_P, 1)

            def probs_copy(a):
                i = a // AH
                r, nj = ROWS[i], (KEYS[i] + P - 1) // P
                act.wait_ge(s_PT, a + 1)
                if a >= 2:
                    act.wait_ge(s_O, a - 1)
                src = pw[:, a % 2, :].rearrange("p (j t) -> p j t", j=4)
                if i < 4:
                    ins = act.activation(PT[:, a % 2, 0:nj, :], src[:, 0:nj, :], ACT.Copy)
                else:
                    link(act.activation(PT[:, a % 2, 0:2, 0:64], src[:, 0:2, 0:64], ACT.Copy))
                    ins = act.activation(PT[0:64, a % 2, 2, 0:64], src[0:64, 2, 0:64], ACT.Copy)
                ins.then_inc(s_PTc, 1)

            def tile_high(i):
                r = ROWS[i]
                act.wait_ge(s_O, AH * (i + 1))
                act.activation(yh[:, 4:8, i * P:i * P + r], pw[:, 2 + i % 2, :].rearrange("p (c t) -> p c t", c=4)[:, :, 0:r],
                               ACT.Copy).then_inc(s_yh, 1)

            def attention():
                NA = NT * AH
                group_used(act, 23)
                for a in range(NA + AHEAD + 1):
                    if a < NA:
                        probs(a)
                    if 0 <= a - AHEAD < NA:
                        probs_copy(a - AHEAD)
                    if a - AHEAD - 2 >= 0 and (a - AHEAD - 2) % AH == AH - 1:
                        tile_high((a - AHEAD - 2) // AH)
                    if AH <= a < AH + HH:
                        act.activation(yh[:, a - AH, :], o_all[:, a - AH, :], ACT.Copy).then_inc(s_ygh, 1)
                    if a in (2 * AH, 3 * AH):
                        cut(22 + a // AH)
                tile_high(NT - 1)

            def gates(m):
                act.wait_ge(s_gl[m % 2], 16 * (m // 2 + 1))
                g_ = gld[:, m % 2].rearrange("p a t -> p (a t)")
                act.activation(g_, g_, ACT.Sigmoid).then_inc(s_sig, 1)

            def merged_high(m):
                act.wait_ge(s_m, m + 1)
                if m + 2 < KD:
                    act.dma_start(gld[:, m % 2], gates_d[m + 2:m + 11:8].rearrange("a p t -> p a t")).then_inc(s_gl[m % 2], 16)
                act.activation(mh[:, m, :], gsum[:, m % 2, :], ACT.Copy).then_inc(s_mh, 1)

            for n, (gg, what) in enumerate(fills):
                if what[0] == "kt":
                    if what[1] == NT - 1:
                        cached_keys()
                    continue
                if what[0] == "attention":
                    attention()
                    continue
                if what == ("hf", 0):
                    act.wait_ge(s_xl, NT)
                if what[0] == "br":
                    if what[1] == 0:
                        gates(0)
                    elif what[1] % 2:
                        merged_high(what[1] // 2)
                        if what[1] < 15:
                            gates(what[1] // 2 + 1)
                    if what[1] == 15:
                        for g in range(OUT0 + 1, NG):
                            cut(g)
                elif what[0] == "out":
                    break
                else:
                    evacuate(what)
                if what == ("hf", 0):
                    index_copies()
                if what == ("hf", 1):
                    index_relu(0, 3)
                    index_relu(1, 4)
                if what == ("hf", 3):
                    index_relu(2, 2)
                    index_relu(3, 1)
                for k in hgrn_steps(what):
                    if normed_head(k) is not None:
                        square_copy(normed_head(k))
                if ends_group(gg, what) and gg + 2 <= OUT0 and gg + 2 not in (24, 25):
                    cut(gg + 2)
                if what == ("hf", 2):
                    softplus(0)
                if what == ("hi", 0):
                    softplus(2)
                if what in (("hi", 1), ("hi", 2)):
                    for h in range(2 * what[1] - 2, 2 * what[1]):
                        key(h)
                if what == ("hi", 3):
                    levels(0)
                if what == ("hi", 4):
                    levels(1)
                for k in hgrn_steps(what):
                    hgrn_step(k)

            def deviation(i, ready, done):
                act.wait_ge(ready, i + 1)
                r = ROWS[i] if done is s_sd2 else P
                act.activation(rstd[0:r, i:i + 1], mv[0:r, i, 1:2], ACT.Sqrt, bias=small[0:r, 1:2]).then_inc(done, 1)

            def x1_copy(i):
                act.wait_ge(s_tx, NT + i + 1)
                if i >= 2:
                    act.wait_ge(s_logit, i - 1)
                act.activation(x1T[:, i % 2].rearrange("p k t -> p (k t)"), pw[:, 0:2].rearrange("p a b -> p (a b)"), ACT.Copy).then_inc(s_txc, 1)

            for i in range(NT):
                if i >= 1:
                    x1_copy(i - 1)
                deviation(i, s_var, s_sd)
            x1_copy(NT - 1)
            for n, (to, at) in enumerate(((ge, gx), (ee, ex))):
                act.wait_ge(s_gx, n + 1)
                act.activation(to[:], at[:], ACT.Exp).then_inc(s_ge, 1)

            def expert(e, j, first, x, t, tc, gu, si, h_):
                act.wait_ge(t, e + 1)
                if not first:
                    act.wait_ge(gu, x)
                act.activation(xgT[:, j], ppf[0].rearrange("p (k t) -> p k t", k=KD)[:, :, 0:CAP], ACT.Copy).then_inc(tc, 1)
                act.wait_ge(gu, e + 1)
                if not first:
                    act.wait_ge(h_, x)
                act.activation(hs[:, j].rearrange("p f t -> p (f t)"), pw[:, j, 0:2 * CAP], ACT.Silu).then_inc(si, 1)

            for e in range(4):
                expert(e, e % 2, e < 2, e - 1, m_t, m_tc, m_gu, m_si, m_h)
            with act.Fori(1, NX // 4) as i:
                for j in range(4):
                    expert(4 * i + j, j % 2, False, 4 * i + (j - 1), m_t, m_tc, m_gu, m_si, m_h)
            over = act.value_load(flag[0:1, 0:1], min_val=0, max_val=1)
            with act.If(over > 0):
                act.wait_ge(m_h, NX)
                with act.Fori(0, NX * (BLOCKS - 1)) as n:
                    expert(n, 0, True, 0, e_t, e_tc, e_gu, e_si, e_h)
            for i in range(NT):
                deviation(i, s_v2, s_sd2)
                if i < NT - DVE_NORMS:
                    act.wait_ge(s_nmr, i + 1)
                    act.activation(xr[:, i, :], total(i), ACT.Identity, scale=rstd[:, i:i + 1], bias=nmr[:, i:i + 1]).then_inc(s_z, 1)

        @block.gpsimd
        def _(pool):
            def cut(g):
                if g in DVE_LOW:
                    return
                width = groups[g][2]
                pool.wait_ge(s_wh, g + 1)
                pool.tensor_tensor(w_lo(g)[:, :, 0:width], raw[:, g % RAW, :, 0:width],
                                   w_hi(g)[:, :, 0:width].bitcast(F32), ALU.subtract).then_inc(s_wl, 1)

            pool.memset(ones[:], 1.0).then_inc(s_ones, 1)

            def halves(h, l):
                w = TP if l == LEVELS - 1 else T
                return [t[:, 0:w].rearrange("p (n a s) -> p n a s", a=2, s=1 << l) for t in (X[h % 2][l], q[:, h, :], kk[:, h, :])]

            def times_keys(h):
                pool.wait_ge(s_k, h + 1)
                for l in range(LEVELS):
                    pool.wait_ge(s_X, LEVELS * h + l + 1)
                    xv, _, kv = halves(h, l)
                    pool.tensor_tensor(xv[:, :, 0, :], xv[:, :, 0, :], kv[:, :, 0, :], ALU.mult).then_inc(s_XM, 1)
                pool.wait_ge(s_kd, h + 1)
                pool.tensor_tensor(kd[h % 2][:], kd[h % 2][:], kk[:, h, :], ALU.mult).then_inc(s_qem, 1)

            def times_queries(h):
                pool.wait_ge(s_ev["hq"], h + 1)
                for l in range(LEVELS):
                    xv, qv, _ = halves(h, l)
                    pool.tensor_tensor(xv[:, :, 1, :], xv[:, :, 1, :], qv[:, :, 1, :], ALU.mult).then_inc(s_XM, 1)
                pool.wait_ge(s_qe, h + 1)
                pool.tensor_tensor(B[:, h, :], B[:, h, :], q[:, h, :], ALU.mult).then_inc(s_qem, 1)

            for g in range(2):
                cut(g)
            for gg, what in fills:
                if what[0] == "br":
                    break
                if gg is not None and last_of[gg] == what and gg + 2 < 24:
                    cut(gg + 2)
                if what == ("hi", 4):
                    times_keys(0)
                if what == ("hq", 0):
                    times_queries(0)
                if what == ("hq", 2):
                    times_keys(1)
                if what == ("hg", 0):
                    times_queries(1)
                for k in hgrn_steps(what):
                    if prepared_head(k - 1) is not None:
                        times_keys(prepared_head(k - 1))
                        times_queries(prepared_head(k - 1))
            for g in range(24, NG):
                cut(g)
            pool.wait_ge(s_x1d, 16 * NT)
            pool.wait_ge(s_stok, 1)
            filled(pool, ("out", NT - 1))
            for e in range(NX):
                j = e % 2
                if e >= 2:
                    pool.wait_ge(m_t, e - 1)
                pool.indirect_dma_start(xg[0:CAP, j, :], None, x1_d, bass.IndirectOffsetOnAxis(ap=stok[0:CAP, e:e + 1], axis=0)).then_inc(m_g[j], 16)
            pool.wait_ge(s_flag, 1)
            over = pool.value_load(flag[0:1, 0:1], min_val=0, max_val=1)
            with pool.If(over > 0):
                pool.memset(zero[:], 0).then_inc(s_zero, 1)
                pool.memset(zcol[:], 0).then_inc(s_zero, 1)
                pool.wait_ge(s_zd, 16)
                pool.wait_ge(s_dest, 1)
                for i in range(NT):
                    for c in range(2):
                        r = ROWS[i]
                        pool.indirect_dma_start(slot_d, bass.IndirectOffsetOnAxis(ap=dest[0:r, c, i:i + 1], axis=0),
                                                tid[0:r, i:i + 1], None).then_inc(s_sct, 16)
                pool.wait_ge(m_t, NX)
                pool.wait_ge(s_zero, 2)
                pool.memset(stx[:, 1:2], 0).then_inc(e_i, 1)
                with pool.Fori(0, NX * (BLOCKS - 1)) as n:
                    pool.wait_ge(e_w, 64 * n + 64)
                    pool.tensor_tensor(stx[0:CAP, 1:2], stx[0:CAP, 0:1], zcol[0:CAP], ALU.add).then_inc(e_ix, 1)
                    pool.wait_ge(e_ix, n + 1)
                    pool.sem_inc(e_pad, 1)
                    pool.indirect_dma_start(xg[0:CAP, 0, :], None, x1_d, bass.IndirectOffsetOnAxis(ap=stx[0:CAP, 1:2], axis=0)).then_inc(e_g, 16)
                    pool.wait_ge(e_yc, n + 1)
                    pool.tensor_tensor(zcol2[:], zcol[:], zcol[:], ALU.add).then_inc(e_i, 1)
            for j in range(2):
                pool.wait_ge(m_ys[j], 16 * NX // 2)
            pool.wait_ge(s_dest, 1)

            def gather_results(rows):
                for i in range(NT):
                    r = ROWS[i]
                    for c in range(2):
                        pool.indirect_dma_start(yg[0:r, i, c, :], None, rows,
                                                bass.IndirectOffsetOnAxis(ap=dest[0:r, c, i:i + 1], axis=0)).then_inc(s_yg[i], 16)

            with pool.If(over > 0):
                pool.wait_ge(e_ys, 16 * NX * (BLOCKS - 1))
                gather_results(ys_d)
            with pool.If(over < 1):
                gather_results(ys_d[0:CAP * NX])
            for i in range(NT - DVE_NORMS):
                if i < POOL_GAINS:
                    pool.wait_ge(s_z, i + 1)
                    pool.tensor_tensor(xr[:, i, :], xr[:, i, :], lnr[:, 2, :], ALU.mult).then_inc(s_ones, 1)
                    pool.wait_ge(s_ones, i + 2)
                else:
                    pool.wait_ge(s_zg, i + 1 - POOL_GAINS)
                pool.tensor_tensor(xr[:, i, :], xr[:, i, :], lnr[:, 3, :], ALU.add).then_inc(s_out, 1)

        @block.vector
        def _(dve):
            chain = Count(d_chain)

            def link(ins):
                dve.wait_ge(d_chain, chain.by(ins))

            def low_part(g):
                width = groups[g][2]
                dve.wait_ge(s_wh, g + 1)
                dve.tensor_tensor(w_lo(g)[:, :, 0:width], raw[:, g % RAW, :, 0:width],
                                  w_hi(g)[:, :, 0:width].bitcast(F32), ALU.subtract).then_inc(s_wlo, 1)

            for i in range(NT):
                at, end = i * P, i * P + ROWS[i]
                dve.wait_ge(s_xh, i + 1)
                dve.tensor_tensor(xl[:, :, at:end], turned_x[i].rearrange("p (k t) -> p k t", k=KD)[:, :, 0:ROWS[i]],
                                  xh[:, :, at:end].bitcast(F32), ALU.subtract).then_inc(s_xl, 1)
            low_part(2)

            def index_sum(n, i):
                r = ROWS[i]
                acc = maskb[0:r, MOFF[i]:MOFF[i] + KEYS[i]]
                for ih in range(IH):
                    s = 4 * n + ih
                    dve.wait_ge(s_rl, s + 1)
                    rl = relu[0:r, s % 2, 0:KEYS[i]]
                    if s >= 1:
                        dve.wait_ge(s_acc, s)
                    if ih == 0:
                        dve.tensor_scalar(acc, rl, tok4[0:r, i, 64:65], None, ALU.mult).then_inc(s_acc, 1)
                    else:
                        dve.scalar_tensor_tensor(acc, rl, tok4[0:r, i, 64 + ih:65 + ih], acc, ALU.mult, ALU.add).then_inc(s_acc, 1)

            def select(n, i, first, last):
                r, w, rounds = ROWS[i], KEYS[i], TOPK[i] // 8
                acc = maskb[0:r, MOFF[i]:MOFF[i] + w]
                if first == 0:
                    dve.wait_ge(s_acc, 4 * n + 4)
                    if i < 4:
                        link(dve.memset(acc[0:64, w - 64:w], NEG))
                for it in range(first, min(last, rounds)):
                    src = acc if it == 0 else wk[0:r, 0:w]
                    link(dve.max(top[0:r, :], src))
                    if it < rounds - 1:
                        link(dve.match_replace(wk[0:r, 0:w], top[0:r, :], src, NEG))
                if last < rounds:
                    return
                thr = top[0:r, 7:8]
                above, equal = wk[0:r, 0:w], eq[0:r, 0:w]
                link(dve.tensor_scalar(above, acc, thr, None, ALU.is_gt))
                link(dve.tensor_scalar(equal, acc, thr, None, ALU.is_equal))
                link(dve.tensor_reduce(cnt[0:r, 0:1], above, AX.X, ALU.add))
                link(dve.tensor_scalar(cnt[0:r, 1:2], cnt[0:r, 0:1], -1.0, float(TOPK[i]), ALU.mult, ALU.add))
                link(dve.tensor_tensor_scan(acc, equal, equal, 0.0, ALU.add, ALU.max))
                link(dve.scalar_tensor_tensor(equal, acc, cnt[0:r, 1:2], equal, ALU.is_le, ALU.mult))
                link(dve.tensor_tensor(above, above, equal, ALU.add))
                dve.tensor_scalar(acc, above, BIG, -BIG, ALU.mult, ALU.add).then_inc(s_mask, 1)
                dve.wait_ge(s_mask, n + 1)

            def decay(h):
                z, l = B[:, h, :], L[:, h, :]
                dve.wait_ge(s_L, h // 2 + 1)
                dve.scalar_tensor_tensor(kk[:, h, :], z, 0.0, l, ALU.max, ALU.add).then_inc(s_g, 1)
                dve.wait_ge(s_g, 2 * h + 1)
                link(dve.scalar_tensor_tensor(l, z, 0.0, l, ALU.min, ALU.subtract))
                dve.tensor_tensor_scan(z, reset[:], l, 0.0, ALU.mult, ALU.add).then_inc(s_g, 1)

            def exponents(h):
                if h == 0:
                    dve.wait_ge(s_acc, 16)
                if h == 1:
                    dve.wait_ge(s_g, 2 * HH)
                if h >= 2:
                    dve.wait_ge(s_G, NT * (h - 1))
                    dve.wait_ge(s_ms, h - 1)
                for l in range(LEVELS):
                    hs = 1 << l
                    w = TP if l == LEVELS - 1 else T
                    nb = w // (2 * hs)
                    xv = X[h % 2][l][:, 0:w].rearrange("p (n a s) -> p n a s", a=2, s=hs)
                    bv = B[:, h, 0:w].rearrange("p (n a s) -> p n a s", a=2, s=hs)
                    mid = bv[:, :, 0, hs - 1:hs].broadcast_to([P, nb, hs])
                    dve.tensor_tensor(xv[:, :, 1, :], bv[:, :, 1, :], mid, ALU.subtract).then_inc(s_D, 1)
                    dve.tensor_tensor(xv[:, :, 0, :], mid, bv[:, :, 0, :], ALU.subtract).then_inc(s_D, 1)

            def chunk_weights(u):
                cw = ROWS[u % NT]
                nl = LEVELS + (1 if u % NT < 4 else 0)
                G = pw[:, 0:2, :].rearrange("p a (b c) -> p (a b) c", c=P)
                dve.wait_ge(s_G, u + 1)
                if u >= 1:
                    dve.wait_ge(s_AT, u)
                dve.tensor_tensor(Gm[0:cw, 0:nl, 0:cw], G[0:cw, 0:nl, 0:cw], pairs[0:cw, 0:nl, 0:cw], ALU.mult).then_inc(s_Gf, 1)
                dve.wait_ge(s_Gf, u + 1)
                if u >= 2:
                    dve.wait_ge(s_o, u - 1)
                dve.tensor_reduce(AT[0:cw, u % 2, 0:cw], Gm[0:cw, 0:nl, 0:cw].rearrange("p l t -> p t l"), AX.X, ALU.add).then_inc(s_AT, 1)

            def chunk_out(u):
                h, c = u // NT, u % NT
                cs, cw = c * P, ROWS[c]
                group = 0 if c < 4 else 1
                dve.wait_ge(s_o, u + 1)
                link(dve.tensor_copy(o_all[:, h, cs:cs + cw], pw[:, 3, 0:cw]))
                if c == 0:
                    ins = dve.tensor_copy(S[:, 0, h, :], pw[:, 3, 256:384])
                else:
                    dve.wait_ge(s_eB, h + 1)
                    ins = dve.scalar_tensor_tensor(S[:, group, h, :], S[:, group, h, :], eBT[:, h % 2, c:c + 1], pw[:, 3, 256:384], ALU.mult, ALU.add)
                ins.then_inc(s_of, 1)
                dve.wait_ge(s_of, u + 1)

            def head_out(h):
                o = o_all[:, h, :]
                dve.wait_ge(s_G, NT * (h + 1))
                dve.tensor_tensor(X[h % 2][1], o, o, ALU.mult).then_inc(s_osq, 1)
                dve.wait_ge(s_ev["hg"], h + 1)
                link(dve.scalar_tensor_tensor(o, o, normw[:, 0:1], sg[:, h, :], ALU.mult, ALU.mult))

            def head_scales():
                dve.wait_ge(s_rms, 1)
                dve.tensor_tensor(o_all[:], o_all[:], q[:], ALU.mult).then_inc(s_y, 1)
                dve.wait_ge(s_y, 1)

            def hgrn_step(k):
                if 1 <= k <= UNITS:
                    chunk_out(k - 1)
                    if k % NT == 0:
                        head_out(k // NT - 1)
                if k < UNITS:
                    chunk_weights(k)
                if prepared_head(k) is not None:
                    exponents(prepared_head(k))
                if k == UNITS + 1:
                    head_scales()

            dve.wait_ge(s_itc, 2)
            for i in range(NT):
                r = ROWS[i]
                link(dve.tensor_scalar(tok4[0:r, i, 64:68], tok4[0:r, i, 64:68], IH ** -0.5, None, ALU.mult))
            index_sum(0, 3)
            index_sum(1, 4)
            dve.wait_ge(s_const, 80)
            decay(0)
            index_sum(2, 2)
            index_sum(3, 1)
            decay(1)
            for h in (2, 3):
                decay(h)
            for h in (0, 1):
                exponents(h)
            select(0, 3, 0, 16)
            for k in range(UNITS + 2):
                if k < 3:
                    select(1, 4, 4 * k, 4 * k + 4)
                elif k < 7:
                    select(2, 2, 4 * (k - 3), 4 * (k - 2))
                elif 8 <= k < 12:
                    select(3, 1, 4 * (k - 8), 4 * (k - 7))
                hgrn_step(k)

            for i in range(NT):
                n = fill_of[("kt", i)]
                b, r = n % 2, ROWS[i]
                dve.wait_ge(s_full[b], n // 2 + 1)
                dve.tensor_copy(ktok[0:r, i, :], ppf[b][0:r, 0:512]).then_inc(s_kt, 1)
                dve.wait_ge(s_kt, i + 1)
                dve.engine_nop().then_inc(s_free[b], 1)

            link(dve.memset(mask0[:], 0.0))
            link(dve.memset(mask0[0:64, 64:128], -BIG))

            def masked(a):
                i = a // AH
                r, w, x = ROWS[i], KEYS[i], a % RING
                m_ = mask0[0:r, :] if i == 0 else maskb[0:r, MOFF[i]:MOFF[i] + w]
                dve.wait_ge(s_lg, a + 1)
                if a >= RING:
                    dve.wait_ge(s_P, a - RING + 1)
                    dve.wait_ge(s_rd, a - RING + 1)
                dve.tensor_tensor_reduce(Lm[0:r, x, 0:w], logit_bank(a)[0:r, 0:w], m_, -(AD ** -0.5), -NEG, ALU.add, ALU.min,
                                         mx[0:r, x, 1:2]).then_inc(s_Lm, 1)

            def normed(a):
                i = a // AH
                r, w, x = ROWS[i], KEYS[i], a % RING
                dve.wait_ge(s_P, a + 1)
                if a >= RING:
                    dve.wait_ge(s_Pn, a - RING + 1)
                dve.reciprocal(mx[0:r, x, 3:4], mx[0:r, x, 2:3]).then_inc(s_rd, 1)
                dve.wait_ge(s_rd, a + 1)
                dve.tensor_scalar(Pr[0:r, x, 0:w], Pr[0:r, x, 0:w], mx[0:r, x, 3:4], None, ALU.mult).then_inc(s_Pn, 1)

            def tile_low(i):
                r = ROWS[i]
                dve.wait_ge(s_yh, i + 1)
                dve.tensor_tensor(yl[:, 4:8, i * P:i * P + r], pw[:, 2 + i % 2, :].rearrange("p (c t) -> p c t", c=4)[:, :, 0:r],
                                  yh[:, 4:8, i * P:i * P + r].bitcast(F32), ALU.subtract).then_inc(s_yl, 1)

            NA = NT * AH
            for a in range(NA + AHEAD + 1):
                if a < NA:
                    masked(a)
                if 0 <= a - 1 < NA:
                    normed(a - 1)
                if a - AHEAD - 3 >= 0 and (a - AHEAD - 3) % AH == AH - 1:
                    tile_low((a - AHEAD - 3) // AH)
                if 0 <= a - AH - 4 < HH:
                    h = a - AH - 4
                    dve.wait_ge(s_ygh, h + 1)
                    dve.tensor_tensor(yl[:, h, :], o_all[:, h, :], yh[:, h, :].bitcast(F32), ALU.subtract).then_inc(s_ygl, 1)
            tile_low(NT - 1)

            dve.wait_ge(s_sk, 64)
            for c in range(2):
                dve.wait_ge(s_gst[c], 16 * 8)

            def merged_low(m):
                dve.wait_ge(s_mh, m + 1)
                dve.tensor_tensor(ml[:, m, :], gsum[:, m % 2, :], mh[:, m, :].bitcast(F32), ALU.subtract).then_inc(s_ml, 1)

            for m in range(KD):
                dve.wait_ge(s_sig, m + 1)
                if m >= 1:
                    dve.wait_ge(s_m, m)
                for w in range(2):
                    n = fill_of[("br", 2 * m + w)]
                    b = n % 2
                    dve.wait_ge(s_full[b], n // 2 + 1)
                    two = lambda t: t.rearrange("p (a b) -> p a b", a=2)
                    dve.tensor_tensor(two(gring[:, w, :]), pp[:, b, :, 0:HT], two(gld[:, m % 2, w, :]), ALU.mult).then_inc(s_br, 1)
                    dve.wait_ge(s_br, 2 * m + w + 1)
                    dve.engine_nop().then_inc(s_free[b], 1)
                if m >= 2:
                    dve.wait_ge(s_ml, m - 1)
                dve.tensor_tensor(gsum[:, m % 2, :], gring[:, 0, :], gring[:, 1, :], ALU.add).then_inc(s_m, 1)
                if m >= 1:
                    merged_low(m - 1)
            merged_low(KD - 1)
            for g in (OUT0 + 1, OUT0 + 3):
                low_part(g)

            dve.wait_ge(s_xr, 96)
            dve.wait_ge(s_store, STORED)

            def residual(i):
                n = fill_of[("out", i)]
                b, r = n % 2, ROWS[i]
                if i == NT - 2:
                    link(dve.memset(xr[64:128, 4, :], 0.0))
                dve.wait_ge(s_full[b], n // 2 + 1)
                dve.scalar_tensor_tensor(xr[0:r, i, :], xr[0:r, i, :], ALPHA, ppf[b][0:r], ALU.mult, ALU.add).then_inc(s_res, 1)
                dve.wait_ge(s_res, i + 1)
                dve.engine_nop().then_inc(s_free[b], 1)

            def moments(i, x, r, done):
                for half in range(2):
                    link(dve.bn_stats(stats[0:r, i, half, :], x[0:r, half * 512:(half + 1) * 512]))
                dve.bn_aggr(mv[0:r, i, :], stats[0:r, i]).then_inc(done, 1)
                dve.wait_ge(done, i + 1)
                link(dve.tensor_scalar(halfv[0:r, i:i + 1], mv[0:r, i, 1:2], 1e-5, -0.5, ALU.add, ALU.mult))

            def inverse_root(i, r, ready):
                y, t = rstd[0:r, i:i + 1], newton[0:r, i:i + 1]
                dve.wait_ge(ready, i + 1)
                link(dve.reciprocal(y, y))
                link(dve.tensor_scalar(t, y, y, halfv[0:r, i:i + 1], ALU.mult, ALU.mult))
                link(dve.tensor_scalar(y, t, 1.5, y, ALU.add, ALU.mult))

            def normalize(i):
                link(dve.scalar_tensor_tensor(xr[:, i, :], xr[:, i, :], mv[:, i, 0:1], lnr[:, 0, :], ALU.subtract, ALU.mult))
                inverse_root(i, P, s_sd)
                dve.scalar_tensor_tensor(xr[:, i, :], xr[:, i, :], rstd[:, i:i + 1], lnr[:, 1, :], ALU.mult, ALU.add).then_inc(s_x1, 1)

            def first_of(oh, values, highest, tl):
                n = tl.stop - tl.start
                wide = lambda t: t.unsqueeze(2).broadcast_to([P, n, 4])
                link(dve.tensor_tensor(oh, values, wide(highest), ALU.is_equal))
                link(dve.tensor_tensor(oh, oh, order[:].unsqueeze(1).broadcast_to([P, n, 4]), ALU.mult))
                link(dve.tensor_reduce(taken[:, tl], oh, AX.X, ALU.max))
                link(dve.tensor_tensor(oh, oh, wide(taken[:, tl]), ALU.is_equal))

            def route(b):
                first, end = BATCHES[b]
                n = end - first
                tl = slice(first, end)
                col = lambda c: cols[:, c, tl]
                dve.wait_ge(s_logit, end)
                dve.tensor_tensor(lg[:, tl], pw[:, 2, 20 * first:20 * end].rearrange("p (i c) -> p i c", c=20),
                                  br_[:].unsqueeze(1).broadcast_to([P, n, 20]), ALU.add).then_inc(s_lgd, 1)
                dve.wait_ge(s_lgd, b + 1)
                link(dve.tensor_reduce(col(0), lg[:, tl, 0:4], AX.X, ALU.max))
                first_of(ohg[:, tl], lg[:, tl, 0:4], col(0), tl)
                group = ohg[:, tl].unsqueeze(3).broadcast_to([P, n, 4, 4])
                link(dve.tensor_tensor(prod[:, tl], lg[:, tl, 4:20].rearrange("p i (g e) -> p i g e", g=4), group, ALU.mult))
                link(dve.tensor_reduce(es[:, tl], prod[:, tl].rearrange("p i g e -> p i e g"), AX.X, ALU.add))
                link(dve.tensor_reduce(col(3), es[:, tl], AX.X, ALU.max))
                first_of(oh1[:, tl], es[:, tl], col(3), tl)
                link(dve.scalar_tensor_tensor(es2[:, tl], oh1[:, tl], -BIG, es[:, tl], ALU.mult, ALU.add))
                link(dve.tensor_reduce(col(4), es2[:, tl], AX.X, ALU.max))
                first_of(oh2[:, tl], es2[:, tl], col(4), tl)
                for m_, oh in ((M1, oh1), (M2, oh2)):
                    link(dve.tensor_tensor(m_[:, tl], group, oh[:, tl].unsqueeze(2).broadcast_to([P, n, 4, 4]), ALU.mult))
                    if end == NT:
                        link(dve.memset(m_[64:128, 4], 0.0))
                flat = lambda t: t[:, tl].rearrange("p i g e -> p i (g e)")
                link(dve.tensor_tensor(M[:, tl], flat(M1), flat(M2), ALU.add))
                for i in range(max(first, 1), end + 1):
                    ins = (dve.tensor_copy(before[:, 1, :], M[:, 0, :]) if i == 1 else
                           dve.tensor_tensor(before[:, i, :], before[:, i - 1, :], M[:, i - 1, :], ALU.add))
                    if i < end:
                        link(ins)
                    else:
                        ins.then_inc(s_M, 1)
                        dve.wait_ge(s_M, b + 1)
                for c, m_ in enumerate((M1, M2)):
                    link(dve.tensor_tensor(Mt[:, c, tl], flat(m_), tidf[:, tl], ALU.mult))

            def one_hot_ranks(b):
                first, end = BATCHES[b]
                tl = slice(first, end)
                ranks_ = pw[:, 3, NX * first:NX * end].rearrange("p (i e) -> p i e", e=NX)
                dve.wait_ge(s_rk, b + 1)
                for c, m_ in enumerate((M1, M2)):
                    pr = prod[:, tl].rearrange("p i g e -> p i (g e)")
                    link(dve.tensor_tensor(pr, m_[:, tl].rearrange("p i g e -> p i (g e)"), ranks_, ALU.mult))
                    link(dve.tensor_reduce(rk[:, c, tl], pr, AX.X, ALU.add))
                if end == NT:
                    link(dve.tensor_reduce(cols[:, 1, 0:1], pw[:, 3, NX * NT:NX * (NT + 1)], AX.X, ALU.max))
                for i in range(first, end):
                    for c in range(2):
                        ins = dve.tensor_scalar(hot[:, c, i, :], iota[:], rk[:, c, i:i + 1], None, ALU.is_equal)
                ins.then_inc(s_hot, 1)
                dve.wait_ge(s_hot, b + 1)

            def weights():
                wide = lambda t: t.unsqueeze(2).broadcast_to([P, NT, 4])
                col = lambda c: cols[:, c, :]
                dve.tensor_scalar(flag[:], cols[:, 1, 0:1], float(CAP), None, ALU.is_gt).then_inc(s_flag, 1)
                dve.wait_ge(s_flag, 1)
                dve.tensor_tensor(gx[:], lg[:, :, 0:4], wide(col(0)), ALU.subtract).then_inc(s_gx, 1)
                dve.tensor_tensor(ex[:], es[:], wide(col(3)), ALU.subtract).then_inc(s_gx, 1)
                for c, m_ in enumerate((M1, M2)):
                    pr = prod[:].rearrange("p i g e -> p i (g e)")
                    link(dve.tensor_tensor(pr, m_[:].rearrange("p i g e -> p i (g e)"), eoff[:].unsqueeze(1).broadcast_to([P, NT, NX]), ALU.mult))
                    link(dve.tensor_reduce(destf[:, c, :], pr, AX.X, ALU.add))
                link(dve.scalar_tensor_tensor(destf[:], rk[:], float(NX), destf[:], ALU.mult, ALU.add))
                dve.tensor_copy(dest[:], destf[:]).then_inc(s_dest, 1)
                dve.wait_ge(s_ge, 2)
                link(dve.tensor_reduce(col(1), ge[:], AX.X, ALU.add))
                link(dve.reciprocal(col(2), col(1)))
                link(dve.tensor_reduce(col(4), ee[:], AX.X, ALU.add))
                link(dve.reciprocal(col(4), col(4)))
                link(dve.tensor_tensor(ee[:], ee[:], wide(col(4)), ALU.mult))
                for c, oh in ((5, oh1), (6, oh2)):
                    link(dve.tensor_tensor(oh[:], oh[:], ee[:], ALU.mult))
                    link(dve.tensor_reduce(col(c), oh[:], AX.X, ALU.add))
                link(dve.tensor_tensor(col(7), col(5), col(6), ALU.add))
                link(dve.reciprocal(col(7), col(7)))
                link(dve.tensor_tensor(col(7), col(7), col(2), ALU.mult))
                link(dve.tensor_tensor(col(8), col(5), col(7), ALU.mult))
                link(dve.tensor_tensor(col(9), col(6), col(7), ALU.mult))

            dve.wait_ge(s_rc, 160)
            dve.wait_ge(s_xr, 96)
            for i in range(NT):
                residual(i)
                moments(i, xr[:, i, :], P, s_var)
                normalize(i)
                if i == BATCHES[0][1]:
                    route(0)
                if i == BATCHES[0][1] + 1:
                    one_hot_ranks(0)
            route(1)
            one_hot_ranks(1)
            dve.wait_ge(s_id, len(BATCHES))
            link(dve.tensor_copy(stokf[:], pw[:, 3, 256:256 + NX]))
            dve.tensor_tensor(stok[:], stokf[:], pw[:, 3, 256 + NX:256 + 2 * NX], ALU.add).then_inc(s_stok, 1)
            weights()

            dve.wait_ge(s_x1d, 16 * NT)
            for i in range(NT):
                dve.tensor_scalar(xr[:, i, :], xr[:, i, :], ALPHA, None, ALU.mult).then_inc(s_dg, 1)

            def expert(n, j, y_prev, ys_prev, si, h_, y_, yc):
                dve.wait_ge(si, n + 1)
                if y_prev is not None:
                    dve.wait_ge(y_, y_prev)
                dve.tensor_tensor(hT[:, j].rearrange("p f t -> p (f t)"), hs[:, j].rearrange("p f t -> p (f t)"),
                                  pw[:, j, 2 * CAP:4 * CAP], ALU.mult).then_inc(h_, 1)
                dve.wait_ge(y_, n + 1)
                if ys_prev is not None:
                    dve.wait_ge(m_ys[j], ys_prev)
                dve.tensor_copy(ysb[0:CAP, j, :], ppf[1][0:CAP]).then_inc(yc, 1)

            for e in range(4):
                expert(e, e % 2, e - 1 if e >= 2 else None, 16 * (e // 2) if e >= 2 else None, m_si, m_h, m_y, m_yc)
            with dve.Fori(1, NX // 4) as i:
                for j in range(4):
                    expert(4 * i + j, j % 2, 4 * i + (j - 1), 32 * i + 16 * (j // 2), m_si, m_h, m_y, m_yc)
            over = dve.value_load(flag[0:1, 0:1], min_val=0, max_val=1)
            with dve.If(over > 0):
                dve.wait_ge(m_ys[0], 16 * NX // 2)
                with dve.Fori(0, NX * (BLOCKS - 1)) as n:
                    expert(n, 0, None, None, e_si, e_h, e_y, e_yc)

            for i in range(1, NT):
                r = ROWS[i]
                for c in range(2):
                    dve.tensor_scalar(dg[0:r, c, i, :], ident[0:r, :], cols[0:r, 8 + c, i:i + 1], None, ALU.mult).then_inc(s_dg, 1)

            def scaled(i):
                inverse_root(i, P, s_sd2)
                dve.scalar_tensor_tensor(nmr[:, i:i + 1], mv[:, i, 0:1], -1.0, rstd[:, i:i + 1], ALU.mult, ALU.mult).then_inc(s_nmr, 1)

            def gains(i):
                dve.wait_ge(s_z, i + 1)
                dve.tensor_tensor(xr[:, i, :], xr[:, i, :], lnr[:, 2, :], ALU.mult).then_inc(s_zg, 1)

            for i in range(NT):
                r = ROWS[i]
                if i == 0:
                    dve.wait_ge(s_yg[0], 32)
                    for c in range(2):
                        link(dve.scalar_tensor_tensor(xr[:, 0, :], yg[:, 0, c, :], cols[:, 8 + c, 0:1], xr[:, 0, :], ALU.mult, ALU.add))
                else:
                    dve.wait_ge(s_tx, 2 * NT + i)
                moments(i, total(i), r, s_v2)
                if POOL_GAINS <= i - 1 < NT - DVE_NORMS:
                    gains(i - 1)
                if i < NT - DVE_NORMS:
                    scaled(i)
                else:
                    link(dve.scalar_tensor_tensor(xr[0:r, i, :], total(i)[0:r], mv[0:r, i, 0:1], lnr[0:r, 2, :], ALU.subtract, ALU.mult))
                    inverse_root(i, r, s_sd2)
                    dve.scalar_tensor_tensor(xr[0:r, i, :], xr[0:r, i, :], rstd[0:r, i:i + 1], lnr[0:r, 3, :],
                                             ALU.mult, ALU.add).then_inc(s_last, 1)


def constants():
    import numpy as np
    t = np.arange(P)
    x = t[:, None] ^ t[None, :]
    pairs = np.zeros((P, LEVELS + 1, P), np.float32)
    pairs[:, 0, :] = x == 0
    for l in range(LEVELS):
        pairs[:, l + 1, :] = ((x >> l) == 1) & (t[:, None] < t[None, :])
    reset = np.ones((P, T), np.float32)
    reset[:, ::P] = 0
    small = np.zeros((P, 8), np.float32)
    small[:, 0] = 1e-6
    small[:, 1] = 1e-5
    lower = (t[:, None] < t[None, :]).astype(np.float32)
    return {"c_ident": np.eye(P, dtype=np.float32), "c_pairs": pairs, "c_reset": reset,
            "c_lower": lower, "c_small": small,
            "c_eoff": np.tile(np.arange(NX, dtype=np.float32), (P, 1)),
            "c_tid": (np.arange(P, dtype=np.uint32)[:, None] + P * np.arange(NT, dtype=np.uint32)[None, :]),
            "c_order": np.tile(np.arange(4, 0, -1, dtype=np.float32), (P, 1)),
            "c_iota": np.tile(np.arange(P, dtype=np.float32), (P, 1)),
            "c_tidf": np.repeat((t[:, None] + P * np.arange(NT)[None, :]).astype(np.float32)[:, :, None], NX, axis=2)}


_INS = ("x_prompt", "x_sample", "cache_k", "cache_v", "cache_idx_k", "state_hgrn", "w_in", "hg_norm_w",
        "w_br_hg", "w_br_att", "w_out", "ln1_g", "ln1_b", "ln2_g", "ln2_b", "w_rg", "b_rg", "w_re", "b_re",
        "w_gate", "w_up", "w_down")
_OUTS = ((1, TP, D), (1, TS, D),
         (1, 1, TP, AH, AD), (1, 1, TP, AH, AD), (1, 1, TP, ID), (1, 1, HH, P, P),
         (1, 1, TS, AH, AD), (1, 1, TS, AH, AD), (1, 1, TS, ID), (1, 1, HH, P, P))


def kernel(**inputs):
    import numpy as _np
    import concourse.bacc as _bacc
    from concourse import mybir as _mybir
    from concourse.bass_utils import run_bass_kernel_spmd as _run

    nc = _bacc.Bacc("TRN2", target_bir_lowering=False, num_devices=1)
    source = {name: _np.ascontiguousarray(inputs[name]) for name in _INS}
    source.update(constants())
    arrays, args = {}, []
    for name, a in source.items():
        arrays[f"in_{name}_dram"] = a
        args.append(nc.dram_tensor(f"in_{name}_dram", a.shape, _mybir.dt.from_np(a.dtype), kind="ExternalInput").ap())
    for i, shape in enumerate(_OUTS):
        args.append(nc.dram_tensor(f"out_{i}_dram", shape, F32, kind="ExternalOutput").ap())
    encoder_layer(nc, *args)
    r = _run(nc, [arrays], core_ids=[0])
    return tuple(r.results[0][f"out_{i}_dram"] for i in range(len(_OUTS)))
```
